# Optimizing a Trainium2 kernel written in Bass

```python
import jax, jax.numpy as jnp
from jax import lax
import numpy as np
import math

D_MODEL = 1024
BATCH = 1
SEQ = 512
DEPTH = 1

CHUNK = 64
D_RNN = 1024
RNN_BLOCKS = 16
RNN_BLOCK_DIM = D_RNN // RNN_BLOCKS
CONV_WIDTH = 4
LRU_C = 8.0
N_HEADS = 16
N_KV_HEADS = 4
HEAD_DIM = 64
D_ATTN = N_HEADS * HEAD_DIM
D_KV = N_KV_HEADS * HEAD_DIM
IDX_HEADS = 8
IDX_DIM = 64
TOPK_MAX = 256
D_FF = 4 * D_MODEL
N_BRANCHES = 2
EPS = 1e-6
SPLITS = (D_RNN, D_RNN, D_ATTN, D_KV, D_KV, IDX_HEADS * IDX_DIM, IDX_DIM, IDX_HEADS, N_BRANCHES * D_MODEL)
D_IN = D_RNN + D_RNN + D_ATTN + D_KV + D_KV + IDX_HEADS * IDX_DIM + IDX_DIM + IDX_HEADS + N_BRANCHES * D_MODEL


def rms_norm(x, w):
    xf = x.astype(jnp.float32)
    y = xf * lax.rsqrt(jnp.mean(xf * xf, axis=-1, keepdims=True) + EPS)
    return (y * w.astype(jnp.float32)).astype(x.dtype)

def causal_depthwise_conv(x, w, b):
    T = x.shape[1]
    xp = jnp.pad(x, ((0, 0), (CONV_WIDTH - 1, 0), (0, 0)))
    out = b
    for j in range(CONV_WIDTH):
        out = out + xp[:, j:j + T] * w[j]
    return out

def block_diag_linear(x, w, b):
    xb = x.reshape(x.shape[:-1] + (RNN_BLOCKS, RNN_BLOCK_DIM))
    y = jnp.einsum('btnd,nde->btne', xb, w)
    return y.reshape(x.shape) + b

def rg_lru(x, wa, ba, wx, bx, lam):
    r = jax.nn.sigmoid(block_diag_linear(x, wa, ba).astype(jnp.float32))
    i = jax.nn.sigmoid(block_diag_linear(x, wx, bx).astype(jnp.float32))
    log_a = -LRU_C * r * jax.nn.softplus(-lam.astype(jnp.float32))
    a = jnp.exp(log_a)
    mult = jnp.sqrt(-jnp.expm1(2.0 * log_a))
    u = mult * (i * x.astype(jnp.float32))

    def combine(c1, c2):
        a1, b1 = c1
        a2, b2 = c2
        return a1 * a2, a2 * b1 + b2

    _, h = lax.associative_scan(combine, (a, u), axis=1)
    return h.astype(x.dtype)

def dsa_attention(q, k, v, iq, ik, iw):
    B, T = q.shape[0], q.shape[1]
    n_chunks = T // CHUNK
    top_k = min(TOPK_MAX, T // 4)
    group = N_HEADS // N_KV_HEADS
    scale = HEAD_DIM ** -0.5
    idx_scale = (IDX_DIM ** -0.5) * (IDX_HEADS ** -0.5)
    key_pos = jnp.arange(T)

    def one_chunk(c):
        start = c * CHUNK
        qc = lax.dynamic_slice_in_dim(q, start, CHUNK, axis=1)
        iqc = lax.dynamic_slice_in_dim(iq, start, CHUNK, axis=1)
        iwc = lax.dynamic_slice_in_dim(iw, start, CHUNK, axis=1)
        limit = start + CHUNK
        visible = key_pos < limit
        rel = jax.nn.relu(jnp.einsum('bqhd,bsd->bqhs', iqc, ik).astype(jnp.float32))
        score = jnp.einsum('bqhs,bqh->bqs', rel, iwc.astype(jnp.float32)) * idx_scale
        score = jnp.where(visible, score, -jnp.inf)
        _, idx = lax.top_k(score, top_k)
        valid = idx < limit
        k_sel = jax.vmap(lambda kb, ib: kb[ib])(k, idx)
        v_sel = jax.vmap(lambda vb, ib: vb[ib])(v, idx)
        qg = qc.reshape(B, CHUNK, N_KV_HEADS, group, HEAD_DIM)
        s = jnp.einsum('bqgrd,bqkgd->bqgrk', qg, k_sel).astype(jnp.float32) * scale
        s = jnp.where(valid[:, :, None, None, :], s, -jnp.inf)
        p = jax.nn.softmax(s, axis=-1).astype(v.dtype)
        o = jnp.einsum('bqgrk,bqkgd->bqgrd', p, v_sel)
        return o.reshape(B, CHUNK, D_ATTN)

    out = lax.map(one_chunk, jnp.arange(n_chunks))
    return out.transpose(1, 0, 2, 3).reshape(B, T, D_ATTN)

def hybrid_layer(x, norm1_w, w_in, conv_w, conv_b, rg_wa, rg_ba, rg_wx, rg_bx, rg_lambda,
                 q_norm_w, k_norm_w, idx_k_norm_w, w_o_rnn, w_o_attn, gate_b, w_out,
                 norm2_w, w_ff_in, w_ff_out):
    B, T, _ = x.shape
    h = rms_norm(x, norm1_w)
    u = h @ w_in
    offsets = np.cumsum(SPLITS)[:-1].tolist()
    rnn_x, rnn_gate, q, k, v, iq, ik, iw, g = jnp.split(u, offsets, axis=-1)

    xc = causal_depthwise_conv(rnn_x, conv_w, conv_b)
    y_rnn = rg_lru(xc, rg_wa, rg_ba, rg_wx, rg_bx, rg_lambda) * jax.nn.gelu(rnn_gate)

    q = rms_norm(q.reshape(B, T, N_HEADS, HEAD_DIM), q_norm_w)
    k = rms_norm(k.reshape(B, T, N_KV_HEADS, HEAD_DIM), k_norm_w)
    v = v.reshape(B, T, N_KV_HEADS, HEAD_DIM)
    iq = iq.reshape(B, T, IDX_HEADS, IDX_DIM)
    ik = rms_norm(ik, idx_k_norm_w)
    y_attn = dsa_attention(q, k, v, iq, ik, iw)

    gates = jax.nn.sigmoid((g + gate_b.reshape(-1)).astype(jnp.float32)).astype(x.dtype)
    gates = gates.reshape(B, T, N_BRANCHES, D_MODEL)
    merged = gates[:, :, 0] * (y_rnn @ w_o_rnn) + gates[:, :, 1] * (y_attn @ w_o_attn)
    x = x + merged @ w_out

    h2 = rms_norm(x, norm2_w)
    x = x + jnp.square(jax.nn.relu(h2 @ w_ff_in)) @ w_ff_out
    return x

def first_inputs(seed: int = 0) -> dict:
    key = jax.random.key(seed)
    ks = jax.random.split(key, 24)
    f32 = jnp.float32

    def nrm(k, shape, scale):
        return jax.random.normal(k, shape, f32) * scale

    a0 = jax.random.uniform(ks[9], (DEPTH, D_RNN), f32, 0.9, 0.999) ** (1.0 / LRU_C)
    rg_lambda = jnp.log(a0) - jnp.log1p(-a0)
    return {
        "x": nrm(ks[0], (BATCH, SEQ, D_MODEL), 1.0),
        "norm1_w": 1.0 + nrm(ks[1], (DEPTH, D_MODEL), 0.02),
        "w_in": nrm(ks[2], (DEPTH, D_MODEL, D_IN), D_MODEL ** -0.5),
        "conv_w": nrm(ks[3], (DEPTH, CONV_WIDTH, D_RNN), CONV_WIDTH ** -0.5),
        "conv_b": nrm(ks[4], (DEPTH, D_RNN), 0.02),
        "rg_wa": nrm(ks[5], (DEPTH, RNN_BLOCKS, RNN_BLOCK_DIM, RNN_BLOCK_DIM), RNN_BLOCK_DIM ** -0.5),
        "rg_ba": nrm(ks[6], (DEPTH, D_RNN), 0.02),
        "rg_wx": nrm(ks[7], (DEPTH, RNN_BLOCKS, RNN_BLOCK_DIM, RNN_BLOCK_DIM), RNN_BLOCK_DIM ** -0.5),
        "rg_bx": nrm(ks[8], (DEPTH, D_RNN), 0.02),
        "rg_lambda": rg_lambda,
        "q_norm_w": 1.0 + nrm(ks[10], (DEPTH, HEAD_DIM), 0.02),
        "k_norm_w": 1.0 + nrm(ks[11], (DEPTH, HEAD_DIM), 0.02),
        "idx_k_norm_w": 1.0 + nrm(ks[12], (DEPTH, IDX_DIM), 0.02),
        "w_o_rnn": nrm(ks[13], (DEPTH, D_RNN, D_MODEL), D_RNN ** -0.5),
        "w_o_attn": nrm(ks[14], (DEPTH, D_ATTN, D_MODEL), D_ATTN ** -0.5),
        "gate_b": nrm(ks[15], (DEPTH, N_BRANCHES, D_MODEL), 0.02),
        "w_out": nrm(ks[16], (DEPTH, D_MODEL, D_MODEL), D_MODEL ** -0.5),
        "norm2_w": 1.0 + nrm(ks[17], (DEPTH, D_MODEL), 0.02),
        "w_ff_in": nrm(ks[18], (DEPTH, D_MODEL, D_FF), D_MODEL ** -0.5),
        "w_ff_out": nrm(ks[19], (DEPTH, D_FF, D_MODEL), D_FF ** -0.5),
    }

def first_block(x, norm1_w, w_in, conv_w, conv_b, rg_wa, rg_ba, rg_wx, rg_bx, rg_lambda,
              q_norm_w, k_norm_w, idx_k_norm_w, w_o_rnn, w_o_attn, gate_b, w_out,
              norm2_w, w_ff_in, w_ff_out):
    for l in range(DEPTH):
        x = hybrid_layer(x, norm1_w[l], w_in[l], conv_w[l], conv_b[l], rg_wa[l], rg_ba[l],
                         rg_wx[l], rg_bx[l], rg_lambda[l], q_norm_w[l], k_norm_w[l],
                         idx_k_norm_w[l], w_o_rnn[l], w_o_attn[l], gate_b[l], w_out[l],
                         norm2_w[l], w_ff_in[l], w_ff_out[l])
    return x


MEM_LEN = 256
GLA_HEADS = 4
GLA_DK = 64
GLA_DV = 128
GLA_RANK = 16
GLA_TAU = 16.0
GLA_CHUNK = 64
SWA_HEADS = 8
SWA_KV_HEADS = 2
SWA_DH = 64
WINDOW = 128
REL_BUCKETS = 32
REL_MAX_DIST = 128
CROSS_HEADS = 4
CROSS_DH = D_MODEL // CROSS_HEADS
D_FF_2 = 2816
CONV_WIDTH_2 = 3

GLA_KW = GLA_HEADS * GLA_DK
GLA_VW = GLA_HEADS * GLA_DV
SWA_QW = SWA_HEADS * SWA_DH
SWA_KVW = SWA_KV_HEADS * SWA_DH
D_MIX = GLA_VW + SWA_QW
IN_SPLITS = (GLA_KW, GLA_KW, GLA_VW, GLA_VW, GLA_RANK, SWA_QW, SWA_KVW, SWA_KVW)
D_IN_2 = 2320


def rms_norm_2(x, g):
    xf = x.astype(jnp.float32)
    y = xf * lax.rsqrt(jnp.mean(xf * xf, axis=-1, keepdims=True) + EPS)
    return (y * g.astype(jnp.float32)).astype(x.dtype)

def t5_bucket(dist):
    n = jnp.maximum(dist, 0)
    max_exact = REL_BUCKETS // 2
    nf = jnp.maximum(n, 1).astype(jnp.float32)
    large = max_exact + (jnp.log(nf / max_exact) / math.log(REL_MAX_DIST / max_exact)
                         * (REL_BUCKETS - max_exact)).astype(jnp.int32)
    large = jnp.minimum(large, REL_BUCKETS - 1)
    return jnp.where(n < max_exact, n, large)

def gla_mixer(q, k, v, r, a_low, w_alpha, b_alpha, gla_gain):
    f32 = jnp.float32
    B, T, _ = q.shape
    C = GLA_CHUNK
    N = T // C
    log_a = jax.nn.log_sigmoid((a_low @ w_alpha + b_alpha).astype(f32)) / GLA_TAU

    def heads(t, d):
        return t.astype(f32).reshape(B, N, C, GLA_HEADS, d).transpose(0, 3, 1, 2, 4)

    qh = heads(q, GLA_DK) * (GLA_DK ** -0.5)
    kh = heads(k, GLA_DK)
    vh = heads(v, GLA_DV)
    bcum = jnp.cumsum(heads(log_a, GLA_DK), axis=3)
    b_last = bcum[:, :, :, -1:, :]
    q_dec = qh * jnp.exp(bcum)
    k_inv = kh * jnp.exp(-bcum)
    k_to_end = kh * jnp.exp(b_last - bcum)
    causal = jnp.tril(jnp.ones((C, C), dtype=bool))
    att = jnp.where(causal, jnp.einsum('bhnik,bhnjk->bhnij', q_dec, k_inv), 0.0)
    o_intra = jnp.einsum('bhnij,bhnjv->bhniv', att, vh)
    kv = jnp.einsum('bhnck,bhncv->nbhkv', k_to_end, vh)
    decay = jnp.exp(b_last[:, :, :, 0, :]).transpose(2, 0, 1, 3)

    def step(S, inp):
        d, kv_n = inp
        return d[..., None] * S + kv_n, S

    S0 = jnp.zeros((B, GLA_HEADS, GLA_DK, GLA_DV), f32)
    _, S_prev = lax.scan(step, S0, (decay, kv))
    o_inter = jnp.einsum('bhnck,nbhkv->bhncv', q_dec, S_prev)
    o = (o_intra + o_inter).transpose(0, 2, 3, 1, 4).reshape(B, T, GLA_HEADS, GLA_DV)
    o = o * lax.rsqrt(jnp.mean(o * o, axis=-1, keepdims=True) + EPS) * gla_gain.astype(f32)
    o = o.reshape(B, T, GLA_VW) * jax.nn.silu(r.astype(f32))
    return o.astype(q.dtype)

def swa_mixer(q, k, v, rel_bias, sinks):
    f32 = jnp.float32
    B, T, _ = q.shape
    L = WINDOW
    NB = T // L
    G = SWA_HEADS // SWA_KV_HEADS
    qb = q.astype(f32).reshape(B, NB, L, SWA_KV_HEADS, G, SWA_DH) * (SWA_DH ** -0.5)
    kb = k.astype(f32).reshape(B, NB, L, SWA_KV_HEADS, SWA_DH)
    vb = v.astype(f32).reshape(B, NB, L, SWA_KV_HEADS, SWA_DH)

    def with_prev(t):
        prev = jnp.pad(t, ((0, 0), (1, 0), (0, 0), (0, 0), (0, 0)))[:, :-1]
        return jnp.concatenate([prev, t], axis=2)

    kk = with_prev(kb)
    vv = with_prev(vb)
    s = jnp.einsum('bnqhgd,bnkhd->bnhgqk', qb, kk)
    qpos = jnp.arange(L)[:, None] + L
    kpos = jnp.arange(2 * L)[None, :]
    dist = qpos - kpos
    bias = rel_bias.astype(f32)[t5_bucket(dist)]
    bias = bias.transpose(2, 0, 1).reshape(SWA_KV_HEADS, G, L, 2 * L)
    in_window = (dist >= 0) & (dist < WINDOW)
    has_prev = (jnp.arange(NB)[:, None, None] > 0) | (kpos[None] >= L)
    mask = in_window[None] & has_prev
    s = jnp.where(mask[None, :, None, None], s + bias, -jnp.inf)
    sink = sinks.astype(f32).reshape(SWA_KV_HEADS, G)[None, None, :, :, None, None]
    m = jnp.maximum(jnp.max(s, axis=-1, keepdims=True), sink)
    p = jnp.exp(s - m)
    p = p / (jnp.sum(p, axis=-1, keepdims=True) + jnp.exp(sink - m))
    o = jnp.einsum('bnhgqk,bnkhd->bnqhgd', p, vv)
    return o.reshape(B, T, SWA_QW).astype(q.dtype)

def cross_attn(h, memn, w_q, w_k, w_v, w_o):
    B, T, _ = h.shape
    q = (h @ w_q).reshape(B, T, CROSS_HEADS, CROSS_DH)
    k = (memn @ w_k).reshape(B, MEM_LEN, CROSS_HEADS, CROSS_DH)
    v = (memn @ w_v).reshape(B, MEM_LEN, CROSS_HEADS, CROSS_DH)
    s = jnp.einsum('bqhd,bkhd->bhqk', q, k).astype(jnp.float32) * (CROSS_DH ** -0.5)
    p = jax.nn.softmax(s, axis=-1).astype(v.dtype)
    o = jnp.einsum('bhqk,bkhd->bqhd', p, v).reshape(B, T, D_MODEL)
    return o @ w_o

def conv_ffn(h, w_up, conv_w, conv_b, w_down):
    u = h @ w_up
    u = lax.conv_general_dilated(u, conv_w[:, None, :].astype(u.dtype), window_strides=(1,),
                                 padding=[(CONV_WIDTH_2 - 1, 0)],
                                 dimension_numbers=('NWC', 'WIO', 'NWC'),
                                 feature_group_count=2 * D_FF_2) + conv_b
    gate, val = jnp.split(u, 2, axis=-1)
    return (jax.nn.silu(gate) * val) @ w_down

def second_inputs(seed: int = 0) -> dict:
    key = jax.random.key(seed)
    ks = jax.random.split(key, 24)
    f32 = jnp.float32

    def nrm(k, shape, scale):
        return jax.random.normal(k, shape, f32) * scale

    def gain(k, shape):
        return 1.0 + 0.02 * jax.random.normal(k, shape, f32)

    return {
        "x": nrm(ks[0], (BATCH, SEQ, D_MODEL), 1.0),
        "mem": nrm(ks[1], (BATCH, MEM_LEN, D_MODEL), 1.0),
        "norm_mix": gain(ks[2], (DEPTH, D_MODEL)),
        "w_in": nrm(ks[3], (DEPTH, D_MODEL, D_IN_2), D_MODEL ** -0.5),
        "w_alpha": nrm(ks[4], (DEPTH, GLA_RANK, GLA_KW), GLA_RANK ** -0.5),
        "b_alpha": nrm(ks[5], (DEPTH, GLA_KW), 0.1),
        "gla_gain": gain(ks[6], (DEPTH, GLA_DV)),
        "rel_bias": nrm(ks[7], (REL_BUCKETS, SWA_HEADS), 0.5),
        "sinks": nrm(ks[8], (DEPTH, SWA_HEADS), 0.5),
        "w_out": nrm(ks[9], (DEPTH, D_MIX, D_MODEL), D_MIX ** -0.5),
        "norm_cross": gain(ks[10], (DEPTH, D_MODEL)),
        "norm_mem": gain(ks[11], (DEPTH, D_MODEL)),
        "w_q_c": nrm(ks[12], (DEPTH, D_MODEL, D_MODEL), D_MODEL ** -0.5),
        "w_k_c": nrm(ks[13], (DEPTH, D_MODEL, D_MODEL), D_MODEL ** -0.5),
        "w_v_c": nrm(ks[14], (DEPTH, D_MODEL, D_MODEL), D_MODEL ** -0.5),
        "w_o_c": nrm(ks[15], (DEPTH, D_MODEL, D_MODEL), D_MODEL ** -0.5),
        "norm_ffn": gain(ks[16], (DEPTH, D_MODEL)),
        "w_up": nrm(ks[17], (DEPTH, D_MODEL, 2 * D_FF_2), D_MODEL ** -0.5),
        "conv_w": nrm(ks[18], (DEPTH, CONV_WIDTH_2, 2 * D_FF_2), CONV_WIDTH_2 ** -0.5),
        "conv_b": nrm(ks[19], (DEPTH, 2 * D_FF_2), 0.01),
        "w_down": nrm(ks[20], (DEPTH, D_FF_2, D_MODEL), D_FF_2 ** -0.5),
        "norm_final": gain(ks[21], (D_MODEL,)),
    }

def second_block(x, mem, norm_mix, w_in, w_alpha, b_alpha, gla_gain, rel_bias, sinks, w_out,
              norm_cross, norm_mem, w_q_c, w_k_c, w_v_c, w_o_c, norm_ffn, w_up, conv_w, conv_b,
              w_down, norm_final):
    split_at = [int(s) for s in np.cumsum(IN_SPLITS)[:-1]]
    h = x
    for l in range(DEPTH):
        hn = rms_norm_2(h, norm_mix[l])
        proj = hn @ w_in[l]
        gq, gk, gv, gr, ga, sq, sk, sv = jnp.split(proj, split_at, axis=-1)
        o_gla = gla_mixer(gq, gk, gv, gr, ga, w_alpha[l], b_alpha[l], gla_gain[l])
        o_swa = swa_mixer(sq, sk, sv, rel_bias, sinks[l])
        h = h + jnp.concatenate([o_gla, o_swa], axis=-1) @ w_out[l]
        h = h + cross_attn(rms_norm_2(h, norm_cross[l]), rms_norm_2(mem, norm_mem[l]),
                           w_q_c[l], w_k_c[l], w_v_c[l], w_o_c[l])
        h = h + conv_ffn(rms_norm_2(h, norm_ffn[l]), w_up[l], conv_w[l], conv_b[l], w_down[l])
    return rms_norm_2(h, norm_final)


def setup_inputs(seed=0):
    out = dict(first_inputs(seed))
    for name, value in second_inputs(seed + 1).items():
        if name != "x":
            out[name + "_2"] = value
    return out


def reference(
    x, norm1_w, w_in, conv_w, conv_b, rg_wa, rg_ba, rg_wx, rg_bx, rg_lambda, q_norm_w, k_norm_w,
    idx_k_norm_w, w_o_rnn, w_o_attn, gate_b, w_out, norm2_w, w_ff_in, w_ff_out, mem_2,
    norm_mix_2, w_in_2, w_alpha_2, b_alpha_2, gla_gain_2, rel_bias_2, sinks_2, w_out_2,
    norm_cross_2, norm_mem_2, w_q_c_2, w_k_c_2, w_v_c_2, w_o_c_2, norm_ffn_2, w_up_2, conv_w_2,
    conv_b_2, w_down_2, norm_final_2,
):
    x = first_block(
        x, norm1_w, w_in, conv_w, conv_b, rg_wa, rg_ba, rg_wx, rg_bx, rg_lambda, q_norm_w,
        k_norm_w, idx_k_norm_w, w_o_rnn, w_o_attn, gate_b, w_out, norm2_w, w_ff_in, w_ff_out,
    )
    return second_block(
        x, mem_2, norm_mix_2, w_in_2, w_alpha_2, b_alpha_2, gla_gain_2, rel_bias_2, sinks_2,
        w_out_2, norm_cross_2, norm_mem_2, w_q_c_2, w_k_c_2, w_v_c_2, w_o_c_2, norm_ffn_2,
        w_up_2, conv_w_2, conv_b_2, w_down_2, norm_final_2,
    )


_drawn_inputs = setup_inputs


def setup_inputs(seed=0):
    import zlib

    import numpy as np

    out = dict(_drawn_inputs(seed))
    spreads = {}
    factors = {'norm1_w': 3.591,
     'rg_ba': 8.0,
     'rg_bx': 8.0,
     'q_norm_w': 8.0,
     'k_norm_w': 8.0,
     'idx_k_norm_w': 6.307,
     'gate_b': 8.0,
     'norm2_w': 2.814,
     'norm_mix_2': 4.761,
     'b_alpha_2': 3.636,
     'gla_gain_2': 8.0,
     'sinks_2': 45.048,
     'norm_cross_2': 8.0,
     'norm_mem_2': 8.0,
     'norm_ffn_2': 15.76,
     'conv_b_2': 32.405,
     'norm_final_2': 8.076}
    for name, (base, spread) in spreads.items():
        noise = np.random.default_rng([zlib.crc32(name.encode()), seed]).standard_normal(out[name].shape)
        drawn = base * np.exp(spread * noise) if base else spread * noise
        out[name] = __import__('jax').numpy.asarray(drawn.astype(out[name].dtype))
    for name, factor in factors.items():
        out[name] = (out[name] * factor).astype(out[name].dtype)
    return out
```

```python
from contextlib import ExitStack

import numpy as np

import concourse.bass as bass
from concourse import mybir

F32 = mybir.dt.float32
F32R = mybir.dt.float32r
BF16 = mybir.dt.bfloat16
I32 = mybir.dt.int32
ALU = mybir.AluOpType
ACT = mybir.ActivationFunctionType
AX = mybir.AxisListType.X
ds = bass.ds

P = 128
T = 512
D = 1024
KT = D // P
QT = T // P
MEM = 256
EPS = 1e-6
SLOTS = 4

J_IK = 0
J_IQ = 1
J_K = 5
J_V = 7
J_Q = 9
J_RNN = 17
J_MIX = 33
J_G1 = 49
J_OA = 57
J_OUT = 65
J_FF = 73
J_IN2 = 137
J_OUT2 = 156
J_QC = 164
J_MEM = 172
J_OC = 188
J_FF2 = 196
FF2_GROUPS = (8, 8, 6)
J_END = J_FF2 + 2 * sum(FF2_GROUPS) + 8 * len(FF2_GROUPS)
assert J_END % SLOTS == 0

VEC = {}
NVEC = 0
for _name, _n in (("norm1", 8), ("conv_w", 32), ("conv_b", 8), ("ba", 8), ("bx", 8), ("lam", 8), ("qn", 1),
                  ("kn", 1), ("ikn", 1), ("gate_b", 16), ("norm2", 8), ("mix", 8), ("b_alpha", 2), ("gla", 1),
                  ("sinks", 8), ("cross", 8), ("mem", 8), ("ffn", 8), ("conv_w2", 132), ("conv_b2", 44),
                  ("final", 8)):
    VEC[_name] = NVEC
    NVEC += _n

UNSEEN = -2.0e38
TAKEN = -3.0e38
TOP_K = 128
Y_ATT = 9
MASKED = -1.0e30
GELU_A = 0.7978845608028654
GELU_B = 0.044715


class Steps:

    def __init__(self, eng, sem):
        self.eng, self.sem, self.n, self.more = eng, sem, 0, 0

    def did(self, ins):
        ins.then_inc(self.sem, 1)
        self.n += 1

    def wait(self):
        self.eng.wait_ge(self.sem, self.more + self.n)

    def enter(self, i, per):
        self.more = self.more + i * per
        return self.n

    def leave(self, began, count, per, more):
        assert self.n - began == per, (self.n - began, per)
        self.n, self.more = began + per * count, more


def heads_of_tile(t):
    return (t, 4 + t) if t < 4 else (4 + t, 8 + t)


def build(nc, w_all, x_t, mem_t, vecs, consts, sel_c, rg_w, consts2, row_table, out):
    with ExitStack() as ctx:
        def sb(name, shape, dt=F32):
            return ctx.enter_context(nc.sbuf_tensor(name, shape, dt))

        def sem(name):
            return ctx.enter_context(nc.semaphore(name))

        raw = sb("w_raw", [P, SLOTS, KT * P])
        w_hi = sb("w_hi", [P, SLOTS, KT * P], F32R)
        w_lo = sb("w_lo", [P, SLOTS, KT * P], F32R)
        a_hi = sb("a_hi", [P, KT, T], F32R)
        a_lo = sb("a_lo", [P, KT, T], F32R)
        b_hi = sb("b_hi", [P, KT, T], F32R)
        b_lo = sb("b_lo", [P, KT, T], F32R)
        vec = sb("vec", [P, NVEC])
        cst = sb("cst", [P, 4 * P + 4])
        ident = cst[:, 0:P]
        unseen = cst[:, P:P + 64]
        masked = cst[:, P + 64:2 * P]
        halves = cst[:, 2 * P:2 * P + 2]
        ones2 = cst[:, 2 * P + 2:2 * P + 4]
        flip = cst[:, 2 * P + 4:3 * P + 4]
        in_chunk = cst[:, 3 * P + 4:4 * P + 4]
        identb = sb("identb", [P, P], BF16)
        sel = sb("sel", [P, 10, P])
        rbuf = sb("rbuf", [P, QT, P])
        small = sb("small", [P, 144])
        sq = sb("sq", [P, 2, T])
        acc = sb("acc", [P, T])
        row = acc
        rstd = sb("rstd", [P, T])
        arena = sb("arena", [P, 38, T])
        x = arena[:, 30:38, :]

        def tiles(i, n=1):
            return arena[:, i:i + n, :]

        def flat(ap):
            return ap.rearrange("p a b -> p (a b)")

        p1 = tiles(0, 17)
        score = tiles(17, 3)
        kz = tiles(20, 4)
        vz = tiles(24, 4).rearrange("p g (t c) -> p g t c", c=P)
        keep = flat(tiles(28, 2)).bitcast(BF16).rearrange("p (t c) -> p t c", c=T)
        ikz = tiles(30, 2)
        rel = tiles(32, 2)
        q_raw = tiles(9, 8)
        y_att = tiles(Y_ATT, 8)
        prob = tiles(30, 4)
        prob_t = tiles(34, 4)
        q_now = tiles(17, 2)
        mix = tiles(0, 8)
        gate = arena[:, 19, :]
        sg1 = tiles(20, 8)
        act_t = tiles(0, 2)
        act_s = tiles(2, 2)
        PAD = 8
        rx = [flat(tiles(32, 2))[:, 0:PAD + T], flat(tiles(34, 2))[:, 0:PAD + T]]
        rg = [arena[:, 0, :], arena[:, 1, :]]
        rc = [arena[:, 2, :], arena[:, 3, :]]
        rr = [arena[:, 4, :], arena[:, 5, :]]
        ri = [arena[:, 6, :], arena[:, 7, :]]
        ra = [arena[:, 36, :], arena[:, 37, :]]
        rt = [arena[:, 8, :], arena[:, 17, :]]
        rgw = tiles(30, 2)[:, :, 0:2 * P]

        in2 = tiles(0, 19)
        c2 = flat(tiles(27, 2))
        w_alpha = c2[:, 0:256]
        rel_rows = c2[:, 256:384]
        bucket = c2[:, 384:768]
        g_qd = tiles(19, 4)
        g_ki = tiles(23, 2)
        g_ke = tiles(25, 2).rearrange("p a b -> p (a b)").rearrange("p (t c) -> p t c", c=256)
        g_bc = tiles(27, 2)
        g_e = arena[:, 29, :]
        g_vt = [arena[:, i, :].rearrange("p (t c) -> p t c", c=P) for i in (27, 28, 29, 0)]
        g_st = flat(tiles(4, 4)).rearrange("p (a n c) -> p a n c", a=2, c=P)
        g_at = [arena[:, i, :] for i in (1, 2, 3, 12)]
        g_o = tiles(23, 4)
        s_kz = tiles(8, 2)
        s_vz = tiles(10, 2).rearrange("p g (t c) -> p g t c", c=P)
        s_bias = flat(tiles(4, 4)).rearrange("p (h c) -> p h c", c=256)
        s_toep = flat(tiles(19, 4)).rearrange("p (h c) -> p h c", c=256)
        s_p = [flat(tiles(i, 2)).rearrange("p (n c) -> p n c", c=256) for i in (19, 21)]
        s_pt = [flat(tiles(i, 2)).rearrange("p (n c) -> p n c", c=P) for i in (27, 0)]
        s_y = tiles(13, 4)
        row_sb = arena[:, 29, :]
        c_q = tiles(0, 8)
        c_k = flat(tiles(8, 4)).rearrange("p (k c) -> p k c", c=MEM)
        c_v = flat(tiles(12, 4)).rearrange("p (e c) -> p e c", c=D)
        c_p = [flat(tiles(i, 2)).rearrange("p (n c) -> p n c", c=MEM) for i in (16, 18)]
        c_pt = [tiles(20, 2), tiles(24, 2)]
        c_vt = flat(tiles(16, 4)).rearrange("p (k c) -> p k c", c=MEM)
        memx = flat(tiles(20, 4)).rearrange("p (k c) -> p k c", c=MEM)
        rstd_m = arena[:, 28, 0:MEM]
        f_u = [flat(tiles(i, 2))[:, 0:PAD + T] for i in (0, 2)]
        f_c = [arena[:, 4, :], arena[:, 5, :]]
        f_s = arena[:, 6, :]
        f_h = arena[:, 7, :]
        o_out = tiles(8, 8)

        job_ps = [ctx.enter_context(nc.psum_tensor(f"job{i}", [P, T], F32)) for i in range(2)]
        s_ps = [ctx.enter_context(nc.psum_tensor(f"score{i}", [P, T], F32)) for i in range(3)]
        t_ps = [ctx.enter_context(nc.psum_tensor(f"turn{i}", [P, T], F32)) for i in range(2)]
        o_ps = ctx.enter_context(nc.psum_tensor("o", [P, T], F32))
        sums = o_ps[:, 0:P].rearrange("p (t c) -> p t c", c=32)

        raw_landed = [sem(f"raw_landed{i}") for i in range(SLOTS)]
        x_landed = [sem(f"x_landed{i}") for i in range(4)]
        SEMS = {}

        def s(name):
            if name not in SEMS:
                SEMS[name] = sem(name)
            return SEMS[name]

        def vcol(name, i=0, n=1):
            if isinstance(i, int):
                return vec[:, VEC[name] + i:VEC[name] + i + n]
            return vec[:, ds(i + VEC[name], n)]

        def at(t, i):
            return t[:, i, :] if isinstance(i, int) else flat(t[:, ds(i, 1), :])

        block = ctx.enter_context(nc.Block())

        @block.sync
        def _(sp):
            for sl in range(SLOTS):
                sp.dma_start(raw[:, sl], w_all[sl]).then_inc(raw_landed[sl], 16)
            with sp.Fori(1, J_END // SLOTS) as i:
                for sl in range(SLOTS):
                    sp.wait_ge(s("lo_ready"), i * SLOTS + (sl + 1 - SLOTS))
                    sp.dma_start(raw[:, sl], w_all[ds(i * SLOTS + sl, 1)].rearrange("a p c -> p (a c)")).then_inc(
                        raw_landed[sl], 16)

        @block.gpsimd
        def _(pool):
            nc.gpsimd.memset(rbuf[:], 0.0).then_inc(s("zeroed"), 1)
            nc.gpsimd.memset(kz, 0.0).then_inc(s("zeroed"), 1)
            nc.gpsimd.memset(vz, 0.0).then_inc(s("zeroed"), 1)
            with pool.Fori(0, J_END // SLOTS) as i:
                for sl in range(SLOTS):
                    pool.wait_ge(s("hi_ready"), i * SLOTS + (sl + 1))
                    nc.gpsimd.tensor_tensor(w_lo[:, sl], raw[:, sl], w_hi[:, sl].bitcast(F32),
                                            ALU.subtract).then_inc(s("lo_ready"), 1)

        half_lam, neg_half_lam = small[:, 16:24], small[:, 24:32]
        half_ba, half_bx, half_gb = small[:, 32:40], small[:, 40:48], small[:, 48:64]
        iw = small[:, 64:96].rearrange("p (t h) -> p t h", h=8)
        top8 = small[:, 96:120]
        nmax, rsum, rinv = small[:, 120:124], small[:, 124:128], small[:, 128:132]
        g_dec = small[:, 0:16].rearrange("p (a n) -> p a n", n=8)
        g_end = small[:, 16:32].rearrange("p (a n) -> p a n", n=8)
        w_max = [small[:, 32 + 4 * i:36 + 4 * i] for i in range(2)]
        w_sum = [small[:, 40 + 4 * i:44 + 4 * i] for i in range(2)]
        w_snk = [small[:, 48 + 4 * i:52 + 4 * i] for i in range(2)]
        w_inv = [small[:, 56 + 4 * i:60 + 4 * i] for i in range(2)]

        def stat_cols(c):
            return {2: rbuf[:, :, 0:20], 5: rbuf[:, :, 0:8], 7: rbuf[:, 0:2, 0:2]}.get(c, rbuf[:, :, 0:2])

        @block.tensor
        def _(pe):
            mm, tp = nc.tensor.matmul, nc.tensor.transpose

            def block_of(k, kts, hi, lo, n=T, last=7):
                sl, ps = k % SLOTS, job_ps[k % 2]
                for kt in kts:
                    c = slice(kt * P, kt * P + P)
                    mm(ps[:, 0:n], w_hi[:, sl, c], hi[:, kt, 0:n], start=kt == 0, stop=False)
                    mm(ps[:, 0:n], w_hi[:, sl, c], lo[:, kt, 0:n], start=False, stop=False)
                    ins = mm(ps[:, 0:n], w_lo[:, sl, c], hi[:, kt, 0:n], start=False, stop=kt == last)
                return ins

            def open_job(k, m=0):
                pe.wait_ge(s("lo_ready"), 4 * m + (k + 1))
                if not (isinstance(m, int) and k + 4 * m < 2):
                    pe.wait_ge(s("job_taken"), 4 * m + (k - 1))

            def job(k, hi, lo, m=0, n=T, last=7, tiles_ready=None):
                open_job(k, m)
                if tiles_ready is None:
                    block_of(k, range(last + 1), hi, lo, n, last).then_inc(s("job_done"), 1)
                    return
                counts, base = tiles_ready
                for kt in range(last + 1):
                    pe.wait_ge(counts, base + kt + 1)
                    ins = block_of(k, [kt], hi, lo, n, last)
                ins.then_inc(s("job_done"), 1)

            def sum_stat(src, col, rhs):
                for t in range(QT):
                    ins = mm(sums[:, t, col:col + 2], src[:, t * P:t * P + P], rhs, start=True, stop=True)
                return ins

            def turn_stat(c):
                pe.wait_ge(s("st_inv"), c + 1)
                for t in range(QT):
                    ins = tp(s_ps[2][:, t * P:t * P + P], rbuf[:, t, :], ident)
                ins.then_inc(s("st_turn"), 1)

            def spread(t, ps):
                return mm(ps, sel[:, t, :], row[:], start=True, stop=True)

            def norm_stat(c, n):
                pe.wait_ge(s("acc_done"), 8 * n + 8)
                sum_stat(acc, 0, ones2).then_inc(s("st_sum"), 1)

            def norm_spread(c):
                turn_stat(c)
                pe.wait_ge(s("st_row"), c + 1)
                spread(0, t_ps[0][:]).then_inc(s("norm_spread"), 1)

            pe.wait_ge(s("const_landed"), 48)
            job(J_IK, a_hi, a_lo, tiles_ready=(s("xlo_ready"), 0))
            norm_stat(0, 0)
            job(J_IQ, a_hi, a_lo)
            norm_spread(0)
            job(J_IQ + 1, a_hi, a_lo)
            pe.wait_ge(s("qk_sq"), 1)
            sum_stat(sq[:, 0], 0, halves).then_inc(s("st_sum"), 1)
            job(J_IQ + 2, a_hi, a_lo)
            turn_stat(1)
            for t in range(QT):
                ins = tp(t_ps[1][:, t * P:t * P + P], p1[:, 0, t * P:t * P + P], ident)
            ins.then_inc(s("iw_turned"), 1)
            pe.wait_ge(s("st_row"), 2)
            pe.wait_ge(s("rstd_ready"), 1)
            spread(0, t_ps[0][:]).then_inc(s("qk_spread"), 1)
            job(J_IQ + 3, a_hi, a_lo)
            job(J_K, a_hi, a_lo)
            job(J_K + 1, a_hi, a_lo)
            pe.wait_ge(s("ik_landed"), 16)
            pe.wait_ge(s("job_taken"), 5)
            for n in range(24):
                t, h = 1 + n // 8, n % 8
                if n >= 3:
                    pe.wait_ge(s("idx_relu"), n - 2)
                mm(s_ps[n % 3][:, 0:P * (t + 1)], p1[:, J_IQ + h // 2, t * P:t * P + P],
                   ikz[:, h % 2, 0:P * (t + 1)], start=True, stop=True).then_inc(s("idx_mm"), 1)
            job(J_V, a_hi, a_lo)
            job(J_V + 1, a_hi, a_lo)
            pe.wait_ge(s("qk_sq"), 2)
            sum_stat(sq[:, 1], 0, halves).then_inc(s("qk_sum"), 1)
            with pe.Fori(0, 2) as i:
                for k in range(4):
                    job(J_Q + k, a_hi, a_lo, m=i)
                    pe.wait_ge(s("qk_sq"), 4 * i + (k + 3))
                    for t in range(QT):
                        ins = mm(o_ps[:, ds(i * 8 + (t * 32 + 2 * k + 2), 2)], sq[:, k % 2, t * P:t * P + P],
                                 halves, start=True, stop=True)
                    ins.then_inc(s("qk_sum"), 1)
            pe.wait_ge(s("qk_sq"), 11)
            sum_stat(sq[:, 0], 18, halves).then_inc(s("st_sum"), 1)
            turn_v = [t_ps[0], t_ps[1]]
            pe.wait_ge(s("iw_ready"), 1)
            for c in range(2):
                for t in range(QT):
                    ins = tp(turn_v[c][:, t * P:t * P + P], p1[:, J_V + c, t * P:t * P + P], ident)
                ins.then_inc(s("v_turned"), 1)
            job(J_RNN, a_hi, a_lo)
            job(J_RNN + 1, a_hi, a_lo)
            turn_stat(2)
            pe.wait_ge(s("st_row"), 3)
            for n in range(10):
                pe.wait_ge(s("vz_ready"), 2) if n < 2 else pe.wait_ge(s("qk_normed"), n)
                spread(n, t_ps[n % 2][:]).then_inc(s("qk_spread"), 1)

            def rnn_gates(u, i):
                pe.wait_ge(s("conv_done"), i * 2 + (u + 1))
                pe.wait_ge(s("rgw_landed"), (i + 1) * 16)
                for c in range(2):
                    ins = mm(s_ps[c][:], rgw[:, u, c * P:c * P + P], rc[u], start=True, stop=True)
                ins.then_inc(s("rnn_mm"), 1)

            def rnn_body(i, ahead):
                job(J_RNN + 2, a_hi, a_lo, m=i)
                job(J_RNN + 3, a_hi, a_lo, m=i)
                rnn_gates(0, i)
                if ahead:
                    job(J_RNN + 4, a_hi, a_lo, m=i)
                    pe.wait_ge(s("rnn_tanh"), i * 2 + 1)
                    rnn_gates(1, i)
                    job(J_RNN + 5, a_hi, a_lo, m=i)

            with pe.Fori(0, 3) as i:
                rnn_body(i, True)
            rnn_body(3, False)
            pe.wait_ge(s("rnn_tanh"), 7)
            rnn_gates(1, 3)

            def head(kvt, i, hh):
                u, half = hh // 2, hh % 2
                n, m0 = kvt * 8 + hh, i * 4
                k, m = J_MIX + n, i
                hi, lo = (a_hi, a_lo) if half == 0 else (b_hi, b_lo)

                def scores(qt, ps):
                    w = P * (qt + 1)
                    mm(ps[:, 0:w], identb[:], keep[:, qt, 0:w], start=True, stop=False)
                    mm(ps[:, 0:w], q_now[:, u, qt * P:qt * P + P], kz[:, 2 * kvt + half, 0:w],
                       start=False, stop=True).then_inc(s("att_mm"), 1)

                if half == 0:
                    pe.wait_ge(s("q_copied"), i * 2 + (kvt * 4 + u + 1))
                scores(3, s_ps[0])
                scores(1, s_ps[1])
                scores(0, s_ps[2])
                open_job(k, m)
                block_of(k, range(0, 3), hi, lo)
                pe.wait_ge(s("att_exp"), m0 * 4 + (4 * n + 3))
                scores(2, s_ps[2])
                block_of(k, range(3, 6), hi, lo)
                pe.wait_ge(s("att_prob"), m0 * 4 + (4 * n + 1))
                for kt in range(4):
                    ins = tp(t_ps[0][:, kt * P:kt * P + P], prob[:, 3, kt * P:kt * P + P], ident)
                ins.then_inc(s("att_turn"), 1)
                pe.wait_ge(s("att_prob"), m0 * 4 + (4 * n + 3))
                tp(t_ps[1][:, 0:P], prob[:, 0, 0:P], ident)
                for kt in range(2):
                    ins = tp(t_ps[1][:, P + kt * P:2 * P + kt * P], prob[:, 1, kt * P:kt * P + P], ident)
                ins.then_inc(s("att_turn"), 1)
                block_of(k, range(6, 7), hi, lo)
                pe.wait_ge(s("att_prob"), m0 * 4 + (4 * n + 4))
                pe.wait_ge(s("turn_act"), m0 * 2 + (2 * n + 1))
                for kt in range(3):
                    ins = tp(t_ps[0][:, kt * P:kt * P + P], prob[:, 2, kt * P:kt * P + P], ident)
                ins.then_inc(s("att_turn"), 1)
                block_of(k, range(7, 8), hi, lo).then_inc(s("job_done"), 1)
                pe.wait_ge(s("turn_act"), m0 * 2 + (2 * n + 2))
                pe.wait_ge(s("turn_dve"), m0 + (n + 1))
                if half == 0:
                    pe.wait_ge(s("att_out"), i * 2 + (kvt * 4 + u + 1))
                for kt in range(4):
                    ins = mm(o_ps[:, kt * P:T], vz[:, 2 * kvt + half, kt, :], prob_t[:, kt, kt * P:T],
                             start=half == 0 and kt == 0, stop=half == 1 and kt == 3, skip_group_check=True)
                ins.then_inc(s("att_pv"), 1)

            pe.sem_inc(s("att_pv"), 1)
            for kvt in range(2):
                with pe.Fori(0, 2) as i:
                    for hh in range(4):
                        head(kvt, i, hh)

            def jobs8(k, hi, lo, m=0, tiles_ready=None, n=T, last=7):
                with pe.Fori(0, 2) as i:
                    for c in range(4):
                        job(k + c, hi, lo, m=i + m, n=n, last=last, tiles_ready=tiles_ready if c == 0 else None)

            jobs8(J_G1, a_hi, a_lo)
            jobs8(J_OA, b_hi, b_lo, tiles_ready=(s("ylo_ready"), 0))
            jobs8(J_OUT, a_hi, a_lo, tiles_ready=(s("mlo_ready"), 0))

            job(J_FF, b_hi, b_lo, tiles_ready=(s("xlo_ready"), 8))
            norm_stat(3, 1)
            job(J_FF + 1, b_hi, b_lo)
            norm_spread(3)
            for c in range(2, 8):
                job(J_FF + c, b_hi, b_lo)
            jobs8(J_FF + 8, a_hi, a_lo, tiles_ready=(s("flo_ready"), 0))
            with pe.Fori(1, 4) as g:
                with pe.Fori(0, 2) as i:
                    for c in range(4):
                        job(J_FF + c, b_hi, b_lo, m=g * 4 + i)
                with pe.Fori(0, 2) as i:
                    for c in range(4):
                        job(J_FF + 8 + c, a_hi, a_lo, m=g * 4 + i,
                            tiles_ready=(s("flo_ready"), g * 8) if c == 0 else None)

            job(J_IN2, b_hi, b_lo, tiles_ready=(s("xlo_ready"), 16))
            norm_stat(4, 2)
            job(J_IN2 + 1, b_hi, b_lo)
            norm_spread(4)
            job(J_IN2 + 2, b_hi, b_lo)
            with pe.Fori(0, 4) as i:
                for c in range(4):
                    job(J_IN2 + 3 + c, b_hi, b_lo, m=i)
            pe.wait_ge(s("c2_landed"), 16)
            pe.wait_ge(s("job_taken"), J_IN2 + 13)
            mm(s_ps[2][:, 0:384], rel_rows, bucket, start=True, stop=True).then_inc(s("rel_mm"), 1)
            for c in range(2):
                ins = mm(s_ps[c][:], w_alpha[:, c * P:c * P + P], in2[:, 12, :], start=True, stop=True)
            ins.then_inc(s("gla_z"), 1)
            for h in range(4):
                if h >= 2:
                    pe.wait_ge(s("gvt_ready"), h - 1)
                for t in range(QT):
                    ins = tp(t_ps[h % 2][:, t * P:t * P + P], in2[:, 4 + h, t * P:t * P + P], ident)
                ins.then_inc(s("gv_turned"), 1)
            pe.wait_ge(s("gvt_ready"), 4)
            pe.wait_ge(s("gk_end"), 2)
            for c in range(2):
                for t in range(QT):
                    ins = tp(t_ps[c][:, t * P:t * P + P], in2[:, 2 + c, t * P:t * P + P], ident)
                ins.then_inc(s("gk_turned"), 1)
            for h in range(4):
                if h == 3:
                    pe.wait_ge(s("at_ready"), 1)
                for t in range(QT):
                    c = slice(t * P, t * P + P)
                    ins = mm((s_ps + s_ps)[h][:, c], g_ki[:, h // 2, c], g_qd[:, h, c], start=True, stop=True)
                ins.then_inc(s("gla_att"), 1)
            pe.wait_ge(s("get_ready"), 2)
            for n in range(7):
                if n >= 2:
                    pe.wait_ge(s("state_taken"), n - 1)
                r = slice(64 * (n % 2), 64 * (n % 2) + 64)
                for h in range(4):
                    ins = mm(t_ps[n % 2][:, h * P:h * P + P], g_ke[r, n // 2, h // 2 * P:h // 2 * P + P],
                             g_vt[h][r, n // 2, :], start=True, stop=True)
                ins.then_inc(s("state_mm"), 1)
            pe.wait_ge(s("state_taken"), 7)
            for h in range(4):
                ps = (o_ps, s_ps[1])[h % 2]
                pe.wait_ge(s("at_ready"), h + 1)
                if h >= 2:
                    pe.wait_ge(s("go_ready"), h - 1)
                for t in range(QT):
                    c = slice(t * P, t * P + P)
                    mm(ps[:, c], g_vt[h][:, t, :], g_at[h][:, c], start=t == 0, stop=False,
                       skip_group_check=True)
                for n in range(1, 8):
                    ins = mm(ps[:, 64 * n:64 * n + 64], g_st[:, h // 2, n, :], g_qd[:, h, 64 * n:64 * n + 64],
                             start=False, stop=n == 7, skip_group_check=True)
                ins.then_inc(s("go_mm"), 1)
            for h in range(4):
                pe.wait_ge(s("go_sq"), h + 1)
                if h == 0:
                    pe.wait_ge(s("go_ready"), 4)
                ins = sum_stat(sq[:, h % 2], 2 * h, ones2)
                ins.then_inc(s("st_sum") if h == 3 else s("go_sum"), 1)
            turn_stat(5)
            pe.wait_ge(s("st_row"), 6)
            for h in range(4):
                if h >= 2:
                    pe.wait_ge(s("go_normed"), h - 1)
                spread(h, t_ps[h % 2][:]).then_inc(s("go_spread"), 1)

            pe.wait_ge(s("toep_landed"), 16)
            pe.wait_ge(s("go_normed"), 4)
            for c in range(4):
                if c >= 2:
                    pe.wait_ge(s("bias_ready"), c - 1)
                mm(t_ps[c % 2][:], flip, s_toep[:, 2 * c:2 * c + 2, :], start=True, stop=True).then_inc(
                    s("bias_mm"), 1)
            for t in range(QT):
                ins = tp(s_ps[2][:, t * P:t * P + P], in2[:, 18, t * P:t * P + P], ident)
            ins.then_inc(s("sv_turned"), 1)
            pe.wait_ge(s("swa_ready"), 2)
            pe.wait_ge(s("bias_ready"), 4)
            pe.wait_ge(s("job_taken"), J_OUT2)
            banks = ((s_ps[0], s_ps[1]), (s_ps[2], o_ps))

            def swa_scores(n):
                t, half = n // 2, n % 2
                if n >= 2:
                    pe.wait_ge(s("swa_s"), n - 1)
                for b in range(QT):
                    k0 = max(b - 1, 0) * P
                    c0 = b % 2 * 256 + (P if b == 0 else 0)
                    ins = mm(banks[n % 2][b // 2][:, c0:b % 2 * 256 + 256], in2[:, 13 + t, b * P:b * P + P],
                             s_kz[:, half, k0:(b + 1) * P], start=True, stop=True)
                ins.then_inc(s("swa_mm"), 1)

            swa_scores(0)
            for n in range(8):
                t, half = n // 2, n % 2
                if n < 7:
                    swa_scores(n + 1)
                pe.wait_ge(s("swa_prob"), n + 1)
                if n >= 1:
                    pe.wait_ge(s("swa_pt"), 2 * n)
                for c in range(2):
                    for b in (2 * c, 2 * c + 1):
                        for e in range(2):
                            if b == 0 and e == 0:
                                continue
                            ins = tp(t_ps[c][:, (b % 2 * 2 + e) * P:(b % 2 * 2 + e + 1) * P],
                                     s_p[n % 2][:, b, e * P:e * P + P], ident)
                    ins.then_inc(s("swa_turn"), 1)
                pe.wait_ge(s("swa_pt"), 2 * n + 2)
                if half == 0 and t >= 2:
                    pe.wait_ge(s("swa_out"), t - 1)
                for b in range(QT):
                    for e in range(2):
                        if b == 0 and e == 0:
                            continue
                        ins = mm(job_ps[t % 2][:, b * P:b * P + P], s_vz[:, half, b - 1 + e, :],
                                 s_pt[n % 2][:, 2 * b + e, :], start=half == 0 and b == 0,
                                 stop=half == 1 and b == 3 and e == 1, skip_group_check=True)
                ins.then_inc(s("swa_pv"), 1)
            pe.wait_ge(s("swa_out"), 4)
            jobs8(J_OUT2, a_hi, a_lo, tiles_ready=(s("y2lo_ready"), 0))
            job(J_QC, b_hi, b_lo, tiles_ready=(s("xlo_ready"), 24))
            norm_stat(6, 3)
            job(J_QC + 1, b_hi, b_lo)
            norm_spread(6)
            for c in range(2, 8):
                job(J_QC + c, b_hi, b_lo)

            job(J_MEM, a_hi, a_lo, n=MEM, tiles_ready=(s("memlo_ready"), 0))
            pe.wait_ge(s("memacc_done"), 8)
            for e in range(2):
                ins = mm(sums[:, e, 0:2], acc[:, e * P:e * P + P], ones2, start=True, stop=True)
            ins.then_inc(s("st_sum"), 1)
            job(J_MEM + 1, a_hi, a_lo, n=MEM)
            norm_spread(7)
            job(J_MEM + 2, a_hi, a_lo, n=MEM)
            job(J_MEM + 3, a_hi, a_lo, n=MEM)
            with pe.Fori(0, 3) as i:
                for c in range(4):
                    job(J_MEM + 4 + c, a_hi, a_lo, m=i, n=MEM)
            pe.wait_ge(s("job_taken"), J_OC)
            for c in range(4):
                if c >= 2:
                    pe.wait_ge(s("cv_ready"), c - 1)
                for kk in range(2):
                    for e in range(2):
                        ins = tp(t_ps[c % 2][:, (e * 2 + kk) * P:(e * 2 + kk + 1) * P],
                                 c_vt[:, 2 * c + kk, e * P:e * P + P], ident)
                ins.then_inc(s("cv_turned"), 1)

            def cross_scores(c):
                if c >= 2:
                    pe.wait_ge(s("cr_exp"), 4 * (c - 1))
                for q in range(QT):
                    for e in range(2):
                        ins = mm(banks[c % 2][q // 2][:, q % 2 * 256:q % 2 * 256 + 256],
                                 c_q[:, 2 * c + e, q * P:q * P + P], c_k[:, 2 * c + e, :],
                                 start=e == 0, stop=e == 1)
                ins.then_inc(s("cr_mm"), 1)

            cross_scores(0)
            pe.wait_ge(s("cv_ready"), 4)
            for c in range(4):
                if c < 3:
                    cross_scores(c + 1)
                pe.wait_ge(s("cr_prob"), c + 1)
                if c >= 1:
                    pe.wait_ge(s("cr_pt"), 2 * c)
                for e in range(2):
                    for q in range(QT):
                        ins = tp(t_ps[e][:, q * P:q * P + P], c_p[c % 2][:, q, e * P:e * P + P], ident)
                    ins.then_inc(s("cr_turn"), 1)
                pe.wait_ge(s("cr_pt"), 2 * c + 2)
                for k in range(2):
                    if c >= 1:
                        pe.wait_ge(s("clo_ready"), 2 * c + k - 1)
                    for e in range(2):
                        ins = mm(job_ps[k][:], c_v[:, e, (2 * c + k) * P:(2 * c + k + 1) * P], c_pt[c % 2][:, e, :],
                                 start=e == 0, stop=e == 1)
                    ins.then_inc(s("cr_pv"), 1)
            pe.wait_ge(s("clo_ready"), 8)
            jobs8(J_OC, a_hi, a_lo)

            k, done = J_FF2, 0
            for gi, g in enumerate(FF2_GROUPS):
                if gi == 0:
                    job(k, b_hi, b_lo, tiles_ready=(s("xlo_ready"), 32))
                    norm_stat(8, 4)
                    job(k + 1, b_hi, b_lo)
                    norm_spread(8)
                    job(k + 2, b_hi, b_lo)
                    job(k + 3, b_hi, b_lo)
                with pe.Fori(1 if gi == 0 else 0, g // 2) as i:
                    for c in range(4):
                        job(k + c, b_hi, b_lo, m=i)
                k, done = k + 2 * g, done + g
                pe.wait_ge(s("hlo_ready"), done)
                jobs8(k, a_hi, a_lo, last=g - 1)
                k += 8
            norm_stat(9, 5)
            norm_spread(9)

        @block.scalar
        def _(act):
            fn = nc.scalar.activation

            def split(k, m=0):
                sl = k % SLOTS
                act.wait_ge(raw_landed[sl], 16 * m + 16 * (k // SLOTS + 1))
                if not (isinstance(m, int) and k + 4 * m < SLOTS):
                    act.wait_ge(s("job_done"), 4 * m + (k - 3))
                fn(w_hi[:, sl], raw[:, sl], ACT.Copy).then_inc(s("hi_ready"), 1)

            def root(c):
                act.wait_ge(s("st_ms"), c + 1)
                fn(stat_cols(c), stat_cols(c), ACT.Sqrt).then_inc(s("st_root"), 1)

            def rows(c):
                act.wait_ge(s("st_turn"), c + 1)
                fn(row[:], s_ps[2][:], ACT.Copy).then_inc(s("st_row"), 1)

            def take_rstd(n, dst=None, w=T):
                act.wait_ge(s("norm_spread"), n)
                fn(rstd[:] if dst is None else dst, t_ps[0][:, 0:w], ACT.Copy).then_inc(s("rstd_ready"), 1)

            def square_tile(n, f, src):
                if 8 * n + f >= 2:
                    act.wait_ge(s("acc_done"), max(8 * n + f - 1, 1))
                fn(sq[:, f % 2, :], src, ACT.Square).then_inc(s("sq_ready"), 1)

            def prep(n, f, name, hi):
                square_tile(n, f, x[:, f, :])
                fn(hi[:, f, :], x[:, f, :], ACT.Copy, scale=vcol(name, f)).then_inc(s("xhi_ready"), 1)

            def load_x():
                for c in range(4):
                    act.dma_start(x[:, 2 * c:2 * c + 2, :],
                                  x_t[2 * c:2 * c + 2].rearrange("k p t -> p k t")).then_inc(x_landed[c], 16)

            load_x()
            act.dma_start(vec[:], vecs).then_inc(s("const_landed"), 16)
            act.dma_start(cst[:], consts).then_inc(s("const_landed"), 16)
            act.dma_start(sel[:], sel_c).then_inc(s("const_landed"), 16)
            act.wait_ge(s("const_landed"), 48)
            fn(small[:, 0:8], vcol("lam", 0, 8), ACT.Abs).then_inc(s("lam_step"), 1)
            act.wait_ge(s("lam_step"), 1)
            fn(small[:, 0:8], small[:, 0:8], ACT.Exp, scale=-1.0).then_inc(s("lam_step"), 1)
            act.wait_ge(s("lam_step"), 2)
            fn(small[:, 0:8], small[:, 0:8], ACT.Ln, bias=1.0).then_inc(s("lam_step"), 1)
            for f in range(8):
                act.wait_ge(x_landed[f // 2], 16)
                prep(0, f, "norm1", a_hi)
                if f in (2, 4, 6):
                    split(f // 2 - 1)
            split(3)
            root(0)
            split(4)
            rows(0)
            take_rstd(1)
            split(5)
            act.wait_ge(s("job_taken"), 1)
            act.wait_ge(s("acc_done"), 8)
            fn(sq[:, 0, :], p1[:, 0, :], ACT.Square).then_inc(s("qk_sq"), 1)
            split(6)
            root(1)
            rows(1)
            act.wait_ge(s("iw_turned"), 1)
            fn(iw, t_ps[1][:].rearrange("p (t c) -> p t c", c=P)[:, :, 64:72], ACT.Copy,
               scale=float((64 ** -0.5) * (8 ** -0.5))).then_inc(s("iw_ready"), 1)
            split(7)
            act.wait_ge(s("ik_normed"), 1)
            act.dma_start(ikz[64:128, 1, :], ikz[0:64, 0, :]).then_inc(s("ik_landed"), 16)
            split(8)
            split(9)
            for n in range(24):
                t = 1 + n // 8
                act.wait_ge(s("idx_mm"), n + 1)
                if n >= 2:
                    act.wait_ge(s("idx_acc"), n - 1)
                fn(rel[:, n % 2, 0:P * (t + 1)], s_ps[n % 3][:, 0:P * (t + 1)], ACT.Relu).then_inc(s("idx_relu"), 1)
                if n == 12:
                    act.wait_ge(s("job_taken"), J_K + 1)
                    fn(sq[:, 1, :], p1[:, J_K, :], ACT.Square).then_inc(s("qk_sq"), 1)
            split(10)
            act.wait_ge(s("job_taken"), J_K + 2)
            fn(sq[:, 0, :], p1[:, J_K + 1, :], ACT.Square).then_inc(s("qk_sq"), 1)
            split(11)
            with act.Fori(0, 2) as i:
                for c in range(4):
                    split(J_Q + 3 + c, i)
                    act.wait_ge(s("job_taken"), i * 4 + (J_Q + c + 1))
                    act.wait_ge(s("qk_sum"), i * 4 + (c + 1))
                    fn(sq[:, (c + 1) % 2, :], at(p1, i * 4 + (J_Q + c)), ACT.Square).then_inc(s("qk_sq"), 1)
            root(2)
            act.wait_ge(s("zeroed"), 3)
            for c in range(2):
                act.wait_ge(s("v_turned"), c + 1)
                v4 = t_ps[c][:].rearrange("p (t c) -> p t c", c=P)
                fn(vz[:, 2 * c, :, 0:64], v4[:, :, 0:64], ACT.Copy)
                fn(vz[:, 2 * c + 1, :, 64:128], v4[:, :, 64:128], ACT.Copy).then_inc(s("vz_ready"), 1)
            split(J_RNN + 3)
            split(J_RNN + 4)
            rows(2)

            def conv_head(u, i):
                act.wait_ge(s("job_taken"), i * 4 + (J_RNN + 2 * u + 1))
                f = i * 2 + u
                fn(rc[u], rx[u][:, PAD:PAD + T], ACT.Identity, scale=vcol("conv_w", f + 24),
                   bias=vcol("conv_b", f)).then_inc(s("conv_head"), 1)

            def gelu_square(u, i):
                act.wait_ge(s("job_taken"), i * 4 + (J_RNN + 2 * u + 2))
                fn(sq[:, u, :], rg[u], ACT.Square).then_inc(s("gelu_sq"), 1)

            def rnn_decay(u, i):
                f, n = i * 2 + u, i * 2 + (u + 1)
                act.wait_ge(s("rnn_mm"), n)
                fn(rr[u], s_ps[0][:], ACT.Tanh, scale=0.5, bias=half_ba_at(f)).then_inc(s("act_step"), 1)
                fn(ri[u], s_ps[1][:], ACT.Tanh, scale=0.5, bias=half_bx_at(f)).then_inc(s("rnn_tanh"), 1)
                act.wait_ge(s("rnn_tanh"), n)
                fn(ra[u], rr[u], ACT.Exp, scale=half_lam_at(f), bias=half_lam_at(f)).then_inc(s("act_step"), 1)
                fn(rr[u], rr[u], ACT.Tanh, scale=neg_half_lam_at(f), bias=neg_half_lam_at(f)).then_inc(
                    s("rnn_a"), 1)

            def scol(c0, f):
                return small[:, ds(f + c0, 1)]

            def half_lam_at(f):
                return scol(16, f)

            def neg_half_lam_at(f):
                return scol(24, f)

            def half_ba_at(f):
                return scol(32, f)

            def half_bx_at(f):
                return scol(40, f)

            def rnn_pair(i, ahead):
                act.dma_start(rgw, rg_w[ds(i * 2, 2)].rearrange("f p c -> p f c")).then_inc(
                    s("rgw_landed"), 16)
                conv_head(0, i)
                gelu_square(0, i)
                split(J_RNN + 5, i)
                conv_head(1, i)
                split(J_RNN + 6, i)
                gelu_square(1, i)
                rnn_decay(0, i)
                if ahead:
                    split(J_RNN + 7, i)
                rnn_decay(1, i)
                for u in range(2):
                    act.wait_ge(s("gelu_p"), i * 2 + (u + 1))
                    fn(sq[:, u, :], sq[:, u, :], ACT.Tanh).then_inc(s("gelu_tanh"), 1)
                if ahead:
                    split(J_RNN + 8, i)
                for u in range(2):
                    act.wait_ge(s("rnn_m"), i * 2 + (u + 1))
                    fn(rt[u], rt[u], ACT.Sqrt, scale=0.25).then_inc(s("rnn_root"), 1)
                for u in range(2):
                    act.wait_ge(s("rnn_y"), i * 2 + (u + 1))
                    fn(at(b_hi, i * 2 + u), rc[u], ACT.Copy).then_inc(s("rhi_ready"), 1)

            with act.Fori(0, 3) as i:
                rnn_pair(i, True)
            rnn_pair(3, False)

            act.wait_ge(s("qk_normed"), 10)
            act.wait_ge(s("rlo_ready"), 8)
            act.sem_inc(s("att_out"), 1)
            for kvt in range(2):
                with act.Fori(0, 2) as i:
                    for u in range(2):
                        fn(q_now[:, u, :], at(q_raw, i * 2 + (kvt * 4 + u)), ACT.Copy).then_inc(s("q_copied"), 1)
                    for hh in range(4):
                        n, half, f = kvt * 8 + hh, hh % 2, i * 2 + (kvt * 4 + hh // 2)
                        split(J_MIX + n + 3, i)
                        for e, qt in enumerate((3, 1, 0, 2)):
                            w = P * (qt + 1)
                            ps = (s_ps[2], s_ps[1], s_ps[2], s_ps[0])[qt]
                            act.wait_ge(s("att_max"), i * 16 + (4 * n + e + 1))
                            fn(prob[:, qt, 0:w], ps[:, 0:w], ACT.Exp, bias=nmax[:, qt:qt + 1],
                               accum_out=rsum[:, qt:qt + 1]).then_inc(s("att_exp"), 1)
                        for e, qt in enumerate((3, 2)):
                            act.wait_ge(s("att_turn"), i * 12 + (3 * n + 2 * e + 1))
                            if e == 0:
                                act.wait_ge(s("att_pv"), i * 4 + (n + 1))
                            fn(prob_t[:, 0:qt + 1, qt * P:qt * P + P],
                               t_ps[0][:, 0:P * (qt + 1)].rearrange("p (k c) -> p k c", c=P),
                               ACT.Copy).then_inc(s("turn_act"), 1)
                        if half == 0:
                            act.wait_ge(s("job_taken"), i * 4 + (J_MIX + n + 1))
                            act.wait_ge(s("params_ready"), 1)
                            fn(gate, gate, ACT.Tanh, scale=0.5, bias=scol(48, f)).then_inc(s("gate_ready"), 1)
                        else:
                            act.wait_ge(s("att_pv"), i * 4 + (n + 2))
                            fn(at(arena, f + Y_ATT), o_ps[:], ACT.Copy).then_inc(s("att_out"), 1)

            act.wait_ge(s("att_pv"), 17)
            act.wait_ge(s("att_out"), 9)
            load_x()
            with act.Fori(0, 2) as i:
                for c in range(4):
                    split(J_G1 + 3 + c, i)
                    fn(at(b_hi, i * 4 + c), at(y_att, i * 4 + c), ACT.Copy).then_inc(s("yhi_ready"), 1)
                    act.wait_ge(s("job_taken"), i * 4 + (J_G1 + c + 1))
                    fn(at(sg1, i * 4 + c), at(sg1, i * 4 + c), ACT.Tanh, scale=0.5,
                       bias=scol(56, i * 4 + c)).then_inc(s("sg_ready"), 1)
            with act.Fori(0, 2) as i:
                for c in range(4):
                    split(J_OA + 3 + c, i)
                    act.wait_ge(s("mix_ready"), i * 4 + (c + 1))
                    fn(at(a_hi, i * 4 + c), at(mix, i * 4 + c), ACT.Copy, scale=0.5).then_inc(s("mhi_ready"), 1)
            for f in range(8):
                split(J_OUT + 3 + f)
                act.wait_ge(s("job_taken"), J_OUT + f + 1)
                prep(1, f, "norm2", b_hi)

            def ff_hidden(c, g, i):
                n = g * 8 + i * 4 + (c + 1)
                act.wait_ge(s("job_taken"), g * 16 + i * 4 + (J_FF + c + 1))
                fn(act_s[:, c % 2, :], act_t[:, c % 2, :], ACT.Square).then_inc(s("ff_sq"), 1)
                fn(at(a_hi, i * 4 + c), act_t[:, c % 2, :], ACT.Square).then_inc(s("fhi_ready"), 1)

            split(J_FF + 3)
            root(3)
            split(J_FF + 4)
            rows(3)
            take_rstd(2)
            for c in range(8):
                if c >= 2:
                    split(J_FF + 3 + c)
                ff_hidden(c % 4, 0, c // 4)
            with act.Fori(0, 2) as i:
                for c in range(4):
                    split(J_FF + 11 + c, i)
            with act.Fori(1, 3) as g:
                with act.Fori(0, 2) as i:
                    for c in range(4):
                        split(J_FF + 3 + c, g * 4 + i)
                        ff_hidden(c, g, i)
                with act.Fori(0, 2) as i:
                    for c in range(4):
                        split(J_FF + 11 + c, g * 4 + i)
            with act.Fori(0, 2) as i:
                for c in range(4):
                    split(J_FF + 3 + c, i + 12)
                    ff_hidden(c, 3, i)
            act.dma_start(c2[:, 0:768], consts2).then_inc(s("c2_landed"), 16)
            for f in range(8):
                split(J_FF + 59 + f)
                act.wait_ge(s("job_taken"), J_FF + 57 + f)
                prep(2, f, "mix", b_hi)

            split(J_IN2 + 3)
            root(4)
            split(J_IN2 + 4)
            rows(4)
            take_rstd(3)
            split(J_IN2 + 5)
            with act.Fori(0, 4) as i:
                for c in range(4):
                    split(J_IN2 + 6 + c, i)
            act.wait_ge(s("rel_mm"), 1)
            fn(row_sb[:, 0:384], s_ps[2][:, 0:384], ACT.Copy).then_inc(s("rel_row"), 1)
            act.wait_ge(s("rel_row"), 1)
            act.dma_start(row_table, row_sb[0:8, 0:384]).then_inc(s("row_stored"), 16)
            for c in range(2):
                act.wait_ge(s("z_min"), c + 1)
                fn(sq[:, c, :], s_ps[c][:], ACT.Abs, bias=vcol("b_alpha", c)).then_inc(s("gla_ln"), 1)
            act.wait_ge(s("gla_ln"), 2)
            for c in range(2):
                fn(sq[:, c, :], sq[:, c, :], ACT.Exp, scale=-1.0).then_inc(s("gla_ln"), 1)
            act.wait_ge(s("gla_ln"), 4)
            for c in range(2):
                fn(sq[:, c, :], sq[:, c, :], ACT.Ln, bias=1.0).then_inc(s("gla_ln"), 1)
            act.wait_ge(s("row_stored"), 16)
            for c in range(2):
                act.wait_ge(s("bc_ready"), 2)
                if c == 1:
                    act.wait_ge(s("gk_end"), 1)
                else:
                    act.wait_ge(s("g_end_ready"), 1)
                    fn(g_dec, g_end, ACT.Exp, scale=1 / 16).then_inc(s("gla_dec"), 1)
                fn(g_e, g_bc[:, c, :], ACT.Exp, scale=1 / 16).then_inc(s("gla_exp"), 1)
                fn(sq[:, 0, :], g_bc[:, c, :], ACT.Exp, scale=-1 / 16).then_inc(s("gla_exp"), 1)
                act.wait_ge(s("gla_left"), c + 1)
                fn(sq[:, 1, :], sq[:, 1, :], ACT.Exp, scale=1 / 16).then_inc(s("gla_exp"), 1)
            act.wait_ge(s("gk_end"), 2)
            for h in range(4):
                act.wait_ge(s("gv_turned"), h + 1)
                fn(g_vt[h], t_ps[h % 2][:].rearrange("p (t c) -> p t c", c=P), ACT.Copy).then_inc(
                    s("gvt_ready"), 1)
            for c in range(2):
                act.wait_ge(s("gk_turned"), c + 1)
                fn(g_ke[:, :, c * P:c * P + P], t_ps[c][:].rearrange("p (t c) -> p t c", c=P),
                   ACT.Copy).then_inc(s("get_ready"), 1)
            for h in range(4):
                fn(in2[:, 8 + h, :], in2[:, 8 + h, :], ACT.Silu).then_inc(s("gr_silu"), 1)
            for h in range(4):
                act.wait_ge(s("go_mm"), h + 1)
                fn(g_o[:, h, :], (o_ps, s_ps[1])[h % 2][:], ACT.Copy).then_inc(s("go_ready"), 1)
            act.dma_start(s_toep, bass.AP(row_table.tensor, 0, [[1, P], [384, 8], [1, 256]])).then_inc(
                s("toep_landed"), 16)
            for h in range(4):
                act.wait_ge(s("go_ready"), h + 1)
                if h >= 2:
                    act.wait_ge(s("go_sum"), h - 1)
                fn(sq[:, h % 2, :], g_o[:, h, :], ACT.Square).then_inc(s("go_sq"), 1)
            root(5)
            rows(5)

            for c in range(4):
                act.wait_ge(s("bias_mm"), c + 1)
                fn(s_bias[:, 2 * c:2 * c + 2, :], t_ps[c % 2][:].rearrange("p (h c) -> p h c", c=256),
                   ACT.Copy).then_inc(s("bias_ready"), 1)
            act.wait_ge(s("sv_turned"), 1)
            act.wait_ge(s("swa_zero"), 1)
            v4 = s_ps[2][:].rearrange("p (t c) -> p t c", c=P)
            fn(s_vz[:, 0, :, 0:64], v4[:, :, 0:64], ACT.Copy)
            fn(s_vz[:, 1, :, 64:128], v4[:, :, 64:128], ACT.Copy).then_inc(s("swa_ready"), 1)

            def swa_exp(n):
                t, half = n // 2, n % 2
                head = t + 4 * half
                act.wait_ge(s("swa_max"), n + 1)
                fn(w_snk[half], w_max[half], ACT.Exp, bias=vcol("sinks", head)).then_inc(s("swa_exp"), 1)
                for b in range(QT):
                    fn(s_p[half][:, b, :], s_p[half][:, b, :], ACT.Exp, bias=w_max[half][:, b:b + 1],
                       accum_out=w_sum[half][:, b:b + 1]).then_inc(s("swa_exp"), 1)

            swa_exp(0)
            for n in range(8):
                if n < 7:
                    swa_exp(n + 1)
                act.wait_ge(s("swa_turn"), 2 * n + 1)
                if n >= 2:
                    act.wait_ge(s("swa_pv"), n - 1)
                fn(s_pt[n % 2][:, 1:4, :], t_ps[0][:, P:T].rearrange("p (b c) -> p b c", c=P),
                   ACT.Copy).then_inc(s("swa_pt"), 1)
                if n % 2 == 1:
                    act.wait_ge(s("swa_pv"), n + 1)
                    fn(s_y[:, n // 2, :], job_ps[n // 2 % 2][:], ACT.Copy).then_inc(s("swa_out"), 1)
            act.wait_ge(s("swa_out"), 4)
            for f in range(8):
                fn(a_hi[:, f, :], g_o[:, f, :] if f < 4 else s_y[:, f - 4, :], ACT.Copy).then_inc(s("y2hi"), 1)
            for f in range(8):
                split(J_OUT2 + 3 + f)
                act.wait_ge(s("job_taken"), J_OUT2 + f + 1)
                prep(3, f, "cross", b_hi)
            act.wait_ge(s("y2lo_ready"), 8)
            act.dma_start(memx, mem_t.rearrange("k p t -> p k t")).then_inc(s("mem_landed"), 16)
            split(J_QC + 3)
            root(6)
            split(J_QC + 4)
            rows(6)
            take_rstd(4)
            act.wait_ge(s("mem_landed"), 16)
            act.wait_ge(s("acc_done"), 32)
            for f in range(8):
                if f < 6:
                    split(J_QC + 5 + f)
                if f >= 2:
                    act.wait_ge(s("memacc_done"), f - 1)
                fn(sq[:, f % 2, 0:MEM], memx[:, f, :], ACT.Square).then_inc(s("memsq"), 1)
                fn(a_hi[:, f, 0:MEM], memx[:, f, :], ACT.Copy, scale=vcol("mem", f)).then_inc(s("memhi"), 1)

            split(J_MEM + 3)
            root(7)
            split(J_MEM + 4)
            rows(7)
            take_rstd(5, rstd_m, MEM)
            split(J_MEM + 5)
            split(J_MEM + 6)
            with act.Fori(0, 3) as i:
                for c in range(4):
                    split(J_MEM + 7 + c, i)
            for c in range(4):
                act.wait_ge(s("cv_turned"), c + 1)
                fn(c_v[:, :, 2 * c * P:(2 * c + 2) * P], t_ps[c % 2][:].rearrange("p (e c) -> p e c", c=2 * P),
                   ACT.Copy).then_inc(s("cv_ready"), 1)
            bank2 = ((s_ps[0], s_ps[1]), (s_ps[2], o_ps))

            def cross_exp(c):
                act.wait_ge(s("cr_max"), c + 1)
                for q in range(QT):
                    fn(c_p[c % 2][:, q, :], bank2[c % 2][q // 2][:, q % 2 * 256:q % 2 * 256 + 256], ACT.Exp,
                       bias=w_max[c % 2][:, q:q + 1], scale=1 / 16,
                       accum_out=w_sum[c % 2][:, q:q + 1]).then_inc(s("cr_exp"), 1)

            cross_exp(0)
            for c in range(4):
                if c < 3:
                    cross_exp(c + 1)
                act.wait_ge(s("cr_turn"), 2 * c + 1)
                fn(c_pt[c % 2][:, 0, :], t_ps[0][:], ACT.Copy).then_inc(s("cr_pt"), 1)
                for k in range(2):
                    act.wait_ge(s("cr_pv"), 2 * c + k + 1)
                    fn(a_hi[:, 2 * c + k, :], job_ps[k][:], ACT.Copy).then_inc(s("chi_ready"), 1)
            for f in range(8):
                split(J_OC + 3 + f)
                act.wait_ge(s("job_taken"), J_OC + f + 1)
                prep(4, f, "ffn", b_hi)

            def ff2_pair(p, job0, i, f, m):
                for u in range(2):
                    act.wait_ge(s("job_taken"), i * 4 + (job0 + u + 1))
                    col = i * 2 + (22 * u + p)
                    fn(f_c[u], f_u[u][:, PAD:PAD + T], ACT.Identity, scale=vcol("conv_w2", col + 88),
                       bias=vcol("conv_b2", col)).then_inc(s("f_head"), 1)
                act.wait_ge(s("f_conv"), i * 4 + (2 * m + 1))
                fn(f_s, f_c[0], ACT.Silu).then_inc(s("f_silu"), 1)
                act.wait_ge(s("f_prod"), i * 2 + (m + 1))
                fn(at(a_hi, i * 2 + f), f_h, ACT.Copy).then_inc(s("hhi_ready"), 1)

            k, done = J_FF2, 0
            for gi, g in enumerate(FF2_GROUPS):
                if gi == 0:
                    split(k + 3)
                    root(8)
                    split(k + 4)
                    rows(8)
                    take_rstd(6)
                    ff2_pair(0, k, 0, 0, 0)
                    split(k + 5)
                    split(k + 6)
                    ff2_pair(1, k + 2, 0, 1, 1)
                with act.Fori(1 if gi == 0 else 0, g // 2) as i:
                    for pp in range(2):
                        split(k + 2 * pp + 3, i)
                        split(k + 2 * pp + 4, i)
                        ff2_pair(done + pp, k + 2 * pp, i, pp, done + pp)
                k, done = k + 2 * g, done + g
                if gi < len(FF2_GROUPS) - 1:
                    with act.Fori(0, 2) as i:
                        for c in range(4):
                            split(k + 3 + c, i)
                else:
                    for f in range(8):
                        if k + 3 + f < J_END:
                            split(k + 3 + f)
                        act.wait_ge(s("job_taken"), k + f + 1)
                        square_tile(5, f, x[:, f, :])
                k += 8
            root(9)
            rows(9)
            take_rstd(7)
            for f in range(8):
                act.wait_ge(s("out_ready"), f + 1)
                act.dma_start(out[f], o_out[:, f, :]).then_inc(s("out_stored"), 16)
            act.wait_ge(s("out_stored"), 128)

        @block.vector
        def _(dve):
            v = nc.vector
            st = Steps(dve, s("dve_step"))
            did, settle = st.did, st.wait

            def stt(out_, a, sc, b, op0=ALU.mult, op1=ALU.mult):
                return v.scalar_tensor_tensor(out=out_, in0=a, scalar=sc, in1=b, op0=op0, op1=op1)

            def tt(out_, a, b, op):
                return v.tensor_tensor(out_, a, b, op)

            def ts(out_, a, s1, s2=None, op0=ALU.mult, op1=ALU.bypass):
                if s2 is None:
                    return v.tensor_scalar(out_, a, s1, None, op0)
                return v.tensor_scalar(out_, a, s1, s2, op0, op1)

            def done(k, m=0):
                dve.wait_ge(s("job_done"), 4 * m + (k + 1))

            def take(k, dst, m=0, w=T, by=None):
                done(k, m)
                tt(dst, job_ps[k % 2][:, 0:w], rstd[:] if by is None else by, ALU.mult).then_inc(s("job_taken"), 1)

            def inverse(c, parts):
                dve.wait_ge(s("st_sum"), c + 1)
                for n, (dst, src, a, b) in enumerate(parts):
                    ins = ts(dst, src, a, b, ALU.mult, ALU.add)
                    if n < len(parts) - 1:
                        did(ins)
                ins.then_inc(s("st_ms"), 1)
                dve.wait_ge(s("st_root"), c + 1)
                v.reciprocal(stat_cols(c), stat_cols(c)).then_inc(s("st_inv"), 1)

            def norm_inverse(c):
                inverse(c, [(rbuf[:, :, 0:2], sums[:, :, 0:2], 1.0 / D, EPS)])

            def add_square(n, f):
                dve.wait_ge(s("sq_ready"), 8 * n + f + 1)
                if f == 0:
                    v.tensor_copy(acc[:], sq[:, 0, :]).then_inc(s("acc_done"), 1)
                else:
                    dve.wait_ge(s("acc_done"), 8 * n + f)
                    tt(acc[:], acc[:], sq[:, f % 2, :], ALU.add).then_inc(s("acc_done"), 1)

            def prep(n, f, name, hi, lo):
                add_square(n, f)
                dve.wait_ge(s("xhi_ready"), 8 * n + f + 1)
                stt(lo[:, f, :], x[:, f, :], vcol(name, f), hi[:, f, :].bitcast(F32), ALU.mult,
                    ALU.subtract).then_inc(s("xlo_ready"), 1)

            dve.wait_ge(s("const_landed"), 48)
            v.tensor_copy(identb[:], ident).then_inc(s("identb_ready"), 1)
            did(ts(small[:, 8:16], vcol("lam", 0, 8), -1.0, 0.0, ALU.mult, ALU.max))
            dve.wait_ge(s("lam_step"), 3)
            settle()
            did(tt(small[:, 8:16], small[:, 8:16], small[:, 0:8], ALU.add))
            settle()
            did(ts(half_lam, small[:, 8:16], -4.0))
            did(ts(neg_half_lam, small[:, 8:16], 4.0))
            did(ts(half_ba, vcol("ba", 0, 8), 0.5))
            did(ts(half_bx, vcol("bx", 0, 8), 0.5))
            ts(half_gb, vcol("gate_b", 0, 16), 0.5).then_inc(s("params_ready"), 1)
            for f in range(8):
                dve.wait_ge(x_landed[f // 2], 16)
                prep(0, f, "norm1", a_hi, a_lo)
            did(v.memset(ikz, 0.0))
            norm_inverse(0)
            dve.wait_ge(s("rstd_ready"), 1)
            take(J_IK, p1[:, 0, :])
            take(J_IQ, p1[:, 1, :])
            take(J_IQ + 1, p1[:, 2, :])
            inverse(1, [(rbuf[:, :, 0:2], sums[:, :, 0:2], 1.0 / 64, EPS)])
            take(J_IQ + 2, p1[:, 3, :])
            dve.wait_ge(s("qk_spread"), 1)
            dve.wait_ge(s("job_taken"), 1)
            settle()
            stt(ikz[0:64, 0, :], p1[0:64, 0, :], vcol("ikn")[0:64], t_ps[0][0:64, :]).then_inc(s("ik_normed"), 1)
            for k in (J_IQ + 3, J_K, J_K + 1):
                take(k, p1[:, k, :])
            dve.wait_ge(s("iw_ready"), 1)
            for n in range(24):
                t, h = 1 + n // 8, n % 8
                w = P * (t + 1)
                dve.wait_ge(s("idx_relu"), n + 1)
                if h == 0:
                    ts(score[:, t - 1, 0:w], rel[:, n % 2, 0:w], iw[:, t, h:h + 1]).then_inc(s("idx_acc"), 1)
                else:
                    dve.wait_ge(s("idx_acc"), n)
                    stt(score[:, t - 1, 0:w], rel[:, n % 2, 0:w], iw[:, t, h:h + 1], score[:, t - 1, 0:w],
                        ALU.mult, ALU.add).then_inc(s("idx_acc"), 1)
            dve.wait_ge(s("idx_acc"), 24)
            for t in (1, 2, 3):
                w = P * (t + 1)
                did(tt(score[:, t - 1, w - 64:w], score[:, t - 1, w - 64:w], unseen, ALU.add))
            for k in (J_V, J_V + 1):
                take(k, p1[:, k, :])
            for c in range(8):
                for _ in range(TOP_K // 8 // 8):
                    settle()
                    for t in range(3):
                        did(v.max(top8[:, 8 * t:8 * t + 8], score[:, t, 0:P * (t + 2)]))
                    settle()
                    for t in range(3):
                        did(v.match_replace(score[:, t, 0:P * (t + 2)], top8[:, 8 * t:8 * t + 8],
                                            score[:, t, 0:P * (t + 2)], TAKEN))
                take(J_Q + c, p1[:, J_Q + c, :])
            settle()
            did(v.memset(keep[:, 0, 0:64], 0.0))
            did(v.tensor_copy(keep[:, 0, 64:P], masked))
            for t in (1, 2, 3):
                w = P * (t + 1)
                ins = ts(keep[:, t, 0:w], score[:, t - 1, 0:w], (UNSEEN + TAKEN) / 2, MASKED, ALU.is_gt, ALU.mult)
                if t < 3:
                    did(ins)
            ins.then_inc(s("keep_ready"), 1)
            inverse(2, [(rbuf[:, :, 0:4], sums[:, :, 0:4], 1.0 / 64, EPS),
                        (rbuf[:, :, 4:20], sums[:, :, 4:20], 1.0, 64 * EPS)])
            dve.wait_ge(s("zeroed"), 3)
            for n in range(10):
                dve.wait_ge(s("qk_spread"), n + 2)
                ps = t_ps[n % 2]
                if n < 2:
                    did(stt(kz[0:64, 2 * n, :], p1[0:64, J_K + n, :], vcol("kn")[0:64], ps[0:64, :]))
                    stt(kz[64:128, 2 * n + 1, :], p1[64:128, J_K + n, :], vcol("kn")[64:128],
                        ps[64:128, :]).then_inc(s("qk_normed"), 1)
                else:
                    q = p1[:, J_Q + n - 2, :]
                    stt(q, q, vcol("qn"), ps[:]).then_inc(s("qk_normed"), 1)

            def conv_tail(u, i):
                for j in range(3):
                    dve.wait_ge(s("conv_head"), i * 2 + (u + 1)) if j == 0 else settle()
                    ins = stt(rc[u], rx[u][:, PAD - 3 + j:PAD - 3 + j + T], vcol("conv_w", i * 2 + (u + 8 * j)),
                              rc[u], ALU.mult, ALU.add)
                    if j < 2:
                        did(ins)
                ins.then_inc(s("conv_done"), 1)

            for u in range(2):
                did(v.memset(rx[u][:, 0:PAD], 0.0))
            settle()
            with dve.Fori(0, 4) as i:
                began = st.enter(i, 16)
                for u in range(2):
                    take(J_RNN + 2 * u, rx[u][:, PAD:PAD + T], m=i)
                    take(J_RNN + 2 * u + 1, rg[u], m=i)
                    dve.wait_ge(s("job_taken"), i * 4 + (J_RNN + 2 * u + 2))
                    conv_tail(u, i)
                for u in range(2):
                    n = i * 2 + (u + 1)
                    dve.wait_ge(s("gelu_sq"), n)
                    did(ts(sq[:, u, :], sq[:, u, :], GELU_A * GELU_B, GELU_A, ALU.mult, ALU.add))
                    settle()
                    tt(sq[:, u, :], sq[:, u, :], rg[u], ALU.mult).then_inc(s("gelu_p"), 1)
                for u in range(2):
                    n = i * 2 + (u + 1)
                    dve.wait_ge(s("rnn_a"), n)
                    did(tt(rt[u], ra[u], ra[u], ALU.mult))
                    settle()
                    stt(rt[u], rt[u], 1.0, rr[u], ALU.add, ALU.mult).then_inc(s("rnn_m"), 1)
                    dve.wait_ge(s("conv_done"), n)
                    did(stt(ri[u], ri[u], 1.0, rc[u], ALU.add, ALU.mult))
                    dve.wait_ge(s("gelu_tanh"), n)
                    did(stt(sq[:, u, :], sq[:, u, :], 1.0, rg[u], ALU.add, ALU.mult))
                settle()
                for u in range(2):
                    n = i * 2 + (u + 1)
                    dve.wait_ge(s("rnn_root"), n)
                    did(tt(ri[u], ri[u], rt[u], ALU.mult))
                    settle()
                    did(v.tensor_tensor_scan(rr[u], ra[u], ri[u], 0.0, ALU.mult, ALU.add))
                    settle()
                    stt(rc[u], sq[:, u, :], 0.5, rr[u]).then_inc(s("rnn_y"), 1)
                for u in range(2):
                    n = i * 2 + (u + 1)
                    dve.wait_ge(s("rhi_ready"), n)
                    dve.wait_ge(s("rnn_y"), n)
                    tt(at(b_lo, i * 2 + u), rc[u], at(b_hi, i * 2 + u).bitcast(F32), ALU.subtract).then_inc(
                        s("rlo_ready"), 1)
                st.leave(began, 4, 16, 0)

            dve.wait_ge(s("qk_normed"), 10)
            for kvt in range(2):
                with dve.Fori(0, 2) as i:
                    began = st.enter(i, 20)
                    for hh in range(4):
                        n, half, f = kvt * 8 + hh, hh % 2, i * 2 + (kvt * 4 + hh // 2)
                        order = (3, 1, 0, 2)

                        def row_max(e):
                            qt = order[e]
                            w, ps = P * (qt + 1), (s_ps[2], s_ps[1], s_ps[2], s_ps[0])[qt]
                            dve.wait_ge(s("att_mm"), i * 16 + (4 * n + e + 1))
                            v.tensor_reduce(nmax[:, qt:qt + 1], ps[:, 0:w], AX, ALU.max,
                                            negate=True).then_inc(s("att_max"), 1)

                        def probabilities(e):
                            qt = order[e]
                            w = P * (qt + 1)
                            dve.wait_ge(s("att_exp"), i * 16 + (4 * n + e + 1))
                            did(v.reciprocal(rinv[:, qt:qt + 1], rsum[:, qt:qt + 1]))
                            settle()
                            ts(prob[:, qt, 0:w], prob[:, qt, 0:w], rinv[:, qt:qt + 1]).then_inc(s("att_prob"), 1)

                        row_max(0)
                        row_max(1)
                        row_max(2)
                        probabilities(0)
                        probabilities(1)
                        probabilities(2)
                        row_max(3)
                        dve.wait_ge(s("att_turn"), i * 12 + (3 * n + 2))
                        dve.wait_ge(s("att_pv"), i * 4 + (n + 1))
                        did(v.tensor_copy(prob_t[:, 0, 0:P], t_ps[1][:, 0:P]))
                        v.tensor_copy(prob_t[:, 0:2, P:2 * P], t_ps[1][:, P:3 * P].rearrange(
                            "p (k c) -> p k c", c=P)).then_inc(s("turn_dve"), 1)
                        probabilities(3)
                        if half == 0:
                            take(J_MIX + n, gate, m=i)
                        else:
                            done(J_MIX + n, i)
                            dve.wait_ge(s("gate_ready"), i * 2 + (kvt * 4 + hh // 2 + 1))
                            stt(at(mix, f), gate, 1.0, job_ps[(J_MIX + n) % 2][:], ALU.add,
                                ALU.mult).then_inc(s("job_taken"), 1)
                    st.leave(began, 2, 20, 0)

            with dve.Fori(0, 2) as i:
                for c in range(4):
                    take(J_G1 + c, at(sg1, i * 4 + c), m=i)
                    dve.wait_ge(s("yhi_ready"), i * 4 + (c + 1))
                    tt(at(b_lo, i * 4 + c), at(y_att, i * 4 + c), at(b_hi, i * 4 + c).bitcast(F32),
                       ALU.subtract).then_inc(s("ylo_ready"), 1)
            with dve.Fori(0, 2) as i:
                began = st.enter(i, 0)
                for c in range(4):
                    n = i * 4 + (c + 1)
                    f = i * 4 + c
                    done(J_OA + c, i)
                    dve.wait_ge(s("sg_ready"), n)
                    stt(at(sg1, f), at(sg1, f), 1.0, job_ps[(J_OA + c) % 2][:], ALU.add, ALU.mult).then_inc(
                        s("job_taken"), 1)
                    dve.wait_ge(s("job_taken"), i * 4 + (J_OA + c + 1))
                    tt(at(mix, f), at(mix, f), at(sg1, f), ALU.add).then_inc(s("mix_ready"), 1)
                    dve.wait_ge(s("mhi_ready"), n)
                    stt(at(a_lo, f), at(mix, f), 0.5, at(a_hi, f).bitcast(F32), ALU.mult,
                        ALU.subtract).then_inc(s("mlo_ready"), 1)
                st.leave(began, 2, 0, 0)

            def add_to_x(k, f):
                done(k)
                tt(x[:, f, :], x[:, f, :], job_ps[k % 2][:], ALU.add).then_inc(s("job_taken"), 1)
                dve.wait_ge(s("job_taken"), k + 1)

            for f in range(8):
                dve.wait_ge(x_landed[f // 2], 32)
                add_to_x(J_OUT + f, f)
                prep(1, f, "norm2", b_hi, b_lo)

            def ff_hidden(c, g, i):
                n = g * 8 + i * 4 + (c + 1)
                k, m = J_FF + c, g * 4 + i
                done(k, m)
                if not (isinstance(g, int) and g == 0 and i == 0 and c < 2):
                    dve.wait_ge(s("fhi_ready"), g * 8 + i * 4 + (c - 1))
                stt(act_t[:, c % 2, :], job_ps[k % 2][:], 0.0, rstd[:], ALU.max, ALU.mult).then_inc(
                    s("job_taken"), 1)
                dve.wait_ge(s("fhi_ready"), n)
                tt(at(a_lo, i * 4 + c), act_s[:, c % 2, :], at(a_hi, i * 4 + c).bitcast(F32),
                   ALU.subtract).then_inc(s("flo_ready"), 1)

            def ff_down(c, g, i):
                done(J_FF + 8 + c, g * 4 + i)
                xf = at(x, i * 4 + c)
                tt(xf, xf, job_ps[(J_FF + c) % 2][:], ALU.add).then_inc(s("job_taken"), 1)

            norm_inverse(3)
            dve.wait_ge(s("rstd_ready"), 2)
            for c in range(8):
                ff_hidden(c % 4, 0, c // 4)
            with dve.Fori(0, 2) as i:
                for c in range(4):
                    ff_down(c, 0, i)
            with dve.Fori(1, 3) as g:
                with dve.Fori(0, 2) as i:
                    for c in range(4):
                        ff_hidden(c, g, i)
                with dve.Fori(0, 2) as i:
                    for c in range(4):
                        ff_down(c, g, i)
            with dve.Fori(0, 2) as i:
                for c in range(4):
                    ff_hidden(c, 3, i)
            for f in range(8):
                add_to_x(J_FF + 56 + f, f)
                prep(2, f, "mix", b_hi, b_lo)

            norm_inverse(4)
            dve.wait_ge(s("rstd_ready"), 3)
            take(J_IN2, in2[:, 0, :])
            take(J_IN2 + 1, in2[:, 1, :])
            take(J_IN2 + 2, in2[:, 2, :])
            with dve.Fori(0, 4) as i:
                for c in range(4):
                    take(J_IN2 + 3 + c, at(in2, i * 4 + (3 + c)), m=i)
            dve.wait_ge(s("gla_z"), 1)
            dve.wait_ge(s("rel_mm"), 1)
            for c in range(2):
                ts(g_bc[:, c, :], s_ps[c][:], vcol("b_alpha", c), 0.0, ALU.add, ALU.min).then_inc(
                    s("z_min"), 1)
            dve.wait_ge(s("gla_ln"), 6)
            dve.wait_ge(s("z_min"), 2)
            for c in range(2):
                did(tt(sq[:, c, :], g_bc[:, c, :], sq[:, c, :], ALU.subtract))
            settle()
            one = ones2[:, 0:1].to_broadcast([P, 64])
            for c in range(2):
                for n in range(8):
                    r = slice(64 * n, 64 * n + 64)
                    ins = v.tensor_tensor_scan(g_bc[:, c, r], one, sq[:, c, r], 0.0, ALU.mult, ALU.add)
                    if n < 7:
                        did(ins)
                ins.then_inc(s("bc_ready"), 1)
            dve.wait_ge(s("bc_ready"), 2)
            settle()
            v.tensor_copy(g_end, g_bc.rearrange("p a (n c) -> p a n c", c=64)[:, :, :, 63]).then_inc(
                s("g_end_ready"), 1)
            did(v.memset(g_qd, 0.0))
            dve.wait_ge(s("g_end_ready"), 1)
            settle()
            for c in range(2):
                dve.wait_ge(s("gla_exp"), 3 * c + 1) if c == 0 else dve.wait_ge(s("gk_end"), 1)
                bc8 = g_bc[:, c, :].rearrange("p (n c) -> p n c", c=64)
                tt(sq[:, 1, :].rearrange("p (n c) -> p n c", c=64),
                   g_end[:, c, :].unsqueeze(2).to_broadcast([P, 8, 64]), bc8, ALU.subtract).then_inc(
                    s("gla_left"), 1)
                dve.wait_ge(s("gla_exp"), 3 * c + 2)
                did(stt(g_qd[0:64, 2 * c, :], in2[0:64, c, :], 0.125, g_e[0:64, :]))
                did(stt(g_qd[64:128, 2 * c + 1, :], in2[64:128, c, :], 0.125, g_e[64:128, :]))
                tt(g_ki[:, c, :], in2[:, 2 + c, :], sq[:, 0, :], ALU.mult).then_inc(s("g_ki_ready"), 1)
                dve.wait_ge(s("gla_exp"), 3 * c + 3)
                dve.wait_ge(s("g_ki_ready"), c + 1)
                settle()
                tt(in2[:, 2 + c, :], in2[:, 2 + c, :], sq[:, 1, :], ALU.mult).then_inc(s("gk_end"), 1)
            dve.wait_ge(s("gk_turned"), 2)
            for h in range(4):
                did(v.memset(g_at[h], 0.0))
            settle()
            for h in range(4):
                dve.wait_ge(s("gla_att"), h + 1)
                v.copy_predicated(g_at[h].rearrange("p (t c) -> p t c", c=P),
                                  in_chunk.bitcast(I32).unsqueeze(1).to_broadcast([P, QT, P]),
                                  (s_ps + s_ps)[h][:].rearrange("p (t c) -> p t c", c=P)).then_inc(
                    s("at_ready"), 1)
            dve.wait_ge(s("gla_dec"), 1)
            for n in range(7):
                dve.wait_ge(s("state_mm"), n + 1)
                if n >= 1:
                    dve.wait_ge(s("state_taken"), n)
                    settle()
                for h in range(4):
                    r = slice(64 * (h % 2), 64 * (h % 2) + 64)
                    new, add = g_st[r, h // 2, n + 1, :], t_ps[n % 2][r, h * P:h * P + P]
                    if n == 0:
                        ins = v.tensor_copy(new, add)
                    else:
                        ins = stt(new, g_st[r, h // 2, n, :], g_dec[r, h // 2, n:n + 1], add, ALU.mult, ALU.add)
                    if h < 3:
                        did(ins)
                ins.then_inc(s("state_taken"), 1)
            inverse(5, [(rbuf[:, :, 0:8], sums[:, :, 0:8], 1.0 / P, EPS)])
            for h in range(4):
                dve.wait_ge(s("go_spread"), h + 1)
                did(stt(g_o[:, h, :], g_o[:, h, :], vcol("gla"), t_ps[h % 2][:]))
                dve.wait_ge(s("gr_silu"), h + 1)
                settle()
                tt(g_o[:, h, :], g_o[:, h, :], in2[:, 8 + h, :], ALU.mult).then_inc(s("go_normed"), 1)

            dve.wait_ge(s("go_normed"), 4)
            did(v.memset(s_kz, 0.0))
            v.memset(s_vz, 0.0).then_inc(s("swa_zero"), 1)
            settle()
            did(v.tensor_copy(s_kz[0:64, 0, :], in2[0:64, 17, :]))
            v.tensor_copy(s_kz[64:128, 1, :], in2[64:128, 17, :]).then_inc(s("swa_ready"), 1)
            dve.wait_ge(s("bias_ready"), 4)
            for u in range(2):
                did(v.memset(s_p[u][:, 0, 0:P], MASKED))
            banks = ((s_ps[0], s_ps[1]), (s_ps[2], o_ps))

            def swa_max(n):
                t, half = n // 2, n % 2
                head, pp, bank = t + 4 * half, s_p[half], banks[half]
                dve.wait_ge(s("swa_mm"), n + 1)
                if n >= 2:
                    dve.wait_ge(s("swa_turn"), 2 * (n - 1))
                    did(v.memset(pp[:, 0, 0:P], MASKED))
                bias = s_bias[:, head, :]
                did(stt(pp[:, 0, P:256], bank[0][:, P:256], 0.125, bias[:, P:256], ALU.mult, ALU.add))
                did(stt(pp[:, 1, :], bank[0][:, 256:512], 0.125, bias, ALU.mult, ALU.add))
                stt(pp[:, 2:4, :], bank[1][:].rearrange("p (b c) -> p b c", c=256), 0.125,
                    bias.unsqueeze(1).to_broadcast([P, 2, 256]), ALU.mult, ALU.add).then_inc(s("swa_s"), 1)
                settle()
                dve.wait_ge(s("swa_s"), n + 1)
                did(v.tensor_reduce(w_max[half], pp, AX, ALU.max))
                settle()
                ts(w_max[half], w_max[half], vcol("sinks", head), -1.0, ALU.max, ALU.mult).then_inc(
                    s("swa_max"), 1)

            swa_max(0)
            for n in range(8):
                half = n % 2
                if n < 7:
                    swa_max(n + 1)
                dve.wait_ge(s("swa_exp"), 5 * n + 5)
                did(tt(w_inv[half], w_sum[half], w_snk[half], ALU.add))
                settle()
                did(v.reciprocal(w_inv[half], w_inv[half]))
                settle()
                tt(s_p[half], s_p[half], w_inv[half].unsqueeze(2).to_broadcast([P, QT, 256]),
                   ALU.mult).then_inc(s("swa_prob"), 1)
                dve.wait_ge(s("swa_turn"), 2 * n + 2)
                if n >= 2:
                    dve.wait_ge(s("swa_pv"), n - 1)
                v.tensor_copy(s_pt[half][:, 4:8, :], t_ps[1][:].rearrange("p (b c) -> p b c", c=P)).then_inc(
                    s("swa_pt"), 1)
            for f in range(8):
                dve.wait_ge(s("y2hi"), f + 1)
                tt(a_lo[:, f, :], g_o[:, f, :] if f < 4 else s_y[:, f - 4, :], a_hi[:, f, :].bitcast(F32),
                   ALU.subtract).then_inc(s("y2lo_ready"), 1)
            for f in range(8):
                add_to_x(J_OUT2 + f, f)
                prep(3, f, "cross", b_hi, b_lo)
            norm_inverse(6)
            dve.wait_ge(s("rstd_ready"), 4)
            for f in range(8):
                take(J_QC + f, c_q[:, f, :])
                dve.wait_ge(s("memsq"), f + 1)
                if f == 0:
                    v.tensor_copy(acc[:, 0:MEM], sq[:, 0, 0:MEM]).then_inc(s("memacc_done"), 1)
                else:
                    dve.wait_ge(s("memacc_done"), f)
                    tt(acc[:, 0:MEM], acc[:, 0:MEM], sq[:, f % 2, 0:MEM], ALU.add).then_inc(s("memacc_done"), 1)
                dve.wait_ge(s("memhi"), f + 1)
                stt(a_lo[:, f, 0:MEM], memx[:, f, :], vcol("mem", f), a_hi[:, f, 0:MEM].bitcast(F32), ALU.mult,
                    ALU.subtract).then_inc(s("memlo_ready"), 1)

            inverse(7, [(rbuf[:, 0:2, 0:2], sums[:, 0:2, 0:2], 1.0 / D, EPS)])
            dve.wait_ge(s("rstd_ready"), 5)
            for f in range(8):
                take(J_MEM + f, c_k[:, f, :], w=MEM, by=rstd_m)
            for f in range(8):
                take(J_MEM + 8 + f, c_vt[:, f, :], w=MEM, by=rstd_m)

            def cross_max(c):
                dve.wait_ge(s("cr_mm"), c + 1)
                for b in range(2):
                    did(v.tensor_reduce(w_max[c % 2][:, 2 * b:2 * b + 2],
                                        banks[c % 2][b][:].rearrange("p (q c) -> p q c", c=MEM), AX, ALU.max))
                settle()
                ts(w_max[c % 2], w_max[c % 2], -1.0 / 16).then_inc(s("cr_max"), 1)

            cross_max(0)
            for c in range(4):
                if c < 3:
                    cross_max(c + 1)
                dve.wait_ge(s("cr_exp"), 4 * c + 4)
                did(v.reciprocal(w_inv[c % 2], w_sum[c % 2]))
                settle()
                tt(c_p[c % 2], c_p[c % 2], w_inv[c % 2].unsqueeze(2).to_broadcast([P, QT, MEM]),
                   ALU.mult).then_inc(s("cr_prob"), 1)
                dve.wait_ge(s("cr_turn"), 2 * c + 2)
                v.tensor_copy(c_pt[c % 2][:, 1, :], t_ps[1][:]).then_inc(s("cr_pt"), 1)
                for k in range(2):
                    dve.wait_ge(s("chi_ready"), 2 * c + k + 1)
                    tt(a_lo[:, 2 * c + k, :], job_ps[k][:], a_hi[:, 2 * c + k, :].bitcast(F32),
                       ALU.subtract).then_inc(s("clo_ready"), 1)
            for f in range(8):
                add_to_x(J_OC + f, f)
                prep(4, f, "ffn", b_hi, b_lo)

            for u in range(2):
                did(v.memset(f_u[u][:, 0:PAD], 0.0))
            norm_inverse(8)
            dve.wait_ge(s("rstd_ready"), 6)

            def ff2_pair(p, job0, i, f, m):
                for u in range(2):
                    take(job0 + u, f_u[u][:, PAD:PAD + T], m=i)
                    dve.wait_ge(s("job_taken"), i * 4 + (job0 + u + 1))
                    for j in range(2):
                        dve.wait_ge(s("f_head"), i * 4 + (2 * m + u + 1)) if j == 0 else settle()
                        ins = stt(f_c[u], f_u[u][:, PAD - 2 + j:PAD - 2 + j + T],
                                  vcol("conv_w2", i * 2 + (44 * j + 22 * u + p)), f_c[u], ALU.mult, ALU.add)
                        if j == 0:
                            did(ins)
                    ins.then_inc(s("f_conv"), 1)
                dve.wait_ge(s("f_silu"), i * 2 + (m + 1))
                dve.wait_ge(s("f_conv"), i * 4 + (2 * m + 2))
                tt(f_h, f_s, f_c[1], ALU.mult).then_inc(s("f_prod"), 1)
                dve.wait_ge(s("hhi_ready"), i * 2 + (m + 1))
                dve.wait_ge(s("f_prod"), i * 2 + (m + 1))
                tt(at(a_lo, i * 2 + f), f_h, at(a_hi, i * 2 + f).bitcast(F32), ALU.subtract).then_inc(
                    s("hlo_ready"), 1)

            k, before = J_FF2, 0
            for gi, g in enumerate(FF2_GROUPS):
                if gi == 0:
                    ff2_pair(0, k, 0, 0, 0)
                    ff2_pair(1, k + 2, 0, 1, 1)
                first = 1 if gi == 0 else 0
                with dve.Fori(first, g // 2) as i:
                    began = st.enter(i - first if first else i, 4)
                    for pp in range(2):
                        ff2_pair(before + pp, k + 2 * pp, i, pp, before + pp)
                    st.leave(began, g // 2 - first, 4, 0)
                k, before = k + 2 * g, before + g
                if gi < len(FF2_GROUPS) - 1:
                    with dve.Fori(0, 2) as i:
                        for c in range(4):
                            done(k + c, i)
                            xf = at(x, i * 4 + c)
                            tt(xf, xf, job_ps[(k + c) % 2][:], ALU.add).then_inc(s("job_taken"), 1)
                else:
                    for f in range(8):
                        add_to_x(k + f, f)
                        add_square(5, f)
                k += 8
            norm_inverse(9)
            dve.wait_ge(s("rstd_ready"), 7)
            for f in range(8):
                stt(o_out[:, f, :], x[:, f, :], vcol("final", f), rstd[:]).then_inc(s("out_ready"), 1)


def pack(w, cols=None):
    k, c = w.shape
    if c % P:
        w = np.concatenate([w, np.zeros((k, P - c % P), w.dtype)], axis=1)
    return w.reshape(k // P, P, -1, P).transpose(2, 1, 0, 3).reshape(-1, P, k)


def columns(a):
    return a.reshape(-1, P).T


def interleave(a, b):
    return np.stack([a, b], axis=1).reshape((-1,) + a.shape[1:])


def layout(i):
    f32 = np.float32
    w = i["w_in"][0]
    cuts = np.cumsum((1024, 1024, 1024, 256, 256, 512, 64, 8))
    rx, rg, q, k, v, iq, ik, iw, g = np.split(w, cuts, axis=1)
    heads = [h for t in range(8) for h in heads_of_tile(t)]
    q = q.reshape(D, 16, 64)[:, heads].reshape(D, D)
    w_oa = i["w_o_attn"][0].reshape(16, 64, D)[heads].reshape(D, D)
    ff_in = pack(i["w_ff_in"][0])
    ff_out = i["w_ff_out"][0]
    jobs = [pack(np.concatenate([ik, iw], axis=1)), pack(iq), pack(k), pack(v), pack(q),
            interleave(pack(rx), pack(rg)), interleave(pack(g[:, :D]), pack(i["w_o_rnn"][0])), pack(g[:, D:]),
            pack(w_oa), pack(i["w_out"][0])]
    for n in range(4):
        jobs += [ff_in[8 * n:8 * n + 8], pack(ff_out[D * n:D * n + D])]
    w2 = i["w_in_2"][0]
    gq, gk, gv, gr, ga, sq, sk, sv = np.split(w2, np.cumsum((256, 256, 512, 512, 16, 512, 128)), axis=1)
    swa = [t + 4 * half for t in range(4) for half in range(2)]
    sq = sq.reshape(D, 8, 64)[:, swa].reshape(D, 512)
    wo2 = i["w_out_2"][0]
    wo2 = np.concatenate([wo2[:512], wo2[512:].reshape(8, 64, D)[swa].reshape(512, D)], axis=0)
    jobs += [pack(a) for a in (gq, gk, gv, gr, ga, sq, sk, sv, wo2, i["w_q_c_2"][0], i["w_k_c_2"][0],
                               i["w_v_c_2"][0], i["w_o_c_2"][0])]
    up = pack(i["w_up_2"][0])
    down = i["w_down_2"][0]
    n = 0
    for g8 in FF2_GROUPS:
        jobs.append(interleave(up[n:n + g8], up[22 + n:22 + n + g8]))
        rows = down[P * n:P * (n + g8)]
        rows = np.concatenate([rows, np.zeros((D - rows.shape[0], D), f32)], axis=0)
        jobs.append(pack(rows))
        n += g8
    w_all = np.concatenate(jobs, axis=0)
    assert w_all.shape == (J_END, P, D), w_all.shape

    two = lambda a: np.concatenate([a, a])[:, None]
    vecs = [columns(i["norm1_w"][0]), columns(i["conv_w"][0].reshape(-1)), columns(i["conv_b"][0]),
            columns(i["rg_ba"][0]), columns(i["rg_bx"][0]), columns(i["rg_lambda"][0]), two(i["q_norm_w"][0]),
            two(i["k_norm_w"][0]), two(i["idx_k_norm_w"][0]), columns(i["gate_b"][0].reshape(-1)),
            columns(i["norm2_w"][0]), columns(i["norm_mix_2"][0]), columns(i["b_alpha_2"][0]),
            i["gla_gain_2"][0][:, None], np.broadcast_to(i["sinks_2"][0], (P, 8)), columns(i["norm_cross_2"][0]),
            columns(i["norm_mem_2"][0]), columns(i["norm_ffn_2"][0]), columns(i["conv_w_2"][0].reshape(-1)),
            columns(i["conv_b_2"][0]), columns(i["norm_final_2"])]
    vecs = np.concatenate(vecs, axis=1)
    assert vecs.shape == (P, NVEC)

    wa, wx = i["rg_wa"][0], i["rg_wx"][0]
    rg_w = np.zeros((8, P, 2 * P), f32)
    for n in range(16):
        r = slice(64 * (n % 2), 64 * (n % 2) + 64)
        rg_w[n // 2, r, r] = wa[n]
        rg_w[n // 2, r, P + 64 * (n % 2):P + 64 * (n % 2) + 64] = wx[n]

    p, c = np.arange(P)[:, None], np.arange(P)[None, :]
    first = (p < 64) + 0 * np.arange(64)
    consts = np.concatenate([(p == c), first * UNSEEN, first * MASKED, p < 64, p >= 64, np.ones((P, 2)),
                             p + c == P - 1, (p <= c) & (p // 64 == c // 64)], axis=1).astype(f32)
    sel = np.zeros((P, 10, P), f32)
    for t in range(10):
        sel[2 * t, t, 0:64] = 1
        sel[2 * t + 1, t, 64:128] = 1
    dist = 255 - np.arange(384)
    d = np.maximum(dist, 0)
    large = 16 + (np.log(np.maximum(d, 1).astype(f32) / f32(16)) / f32(np.log(8.0)) * f32(16)).astype(np.int32)
    buckets = np.where(d < 16, d, np.minimum(large, 31))
    inside = (dist >= 0) & (dist < 128)
    bucket = np.zeros((P, 384), f32)
    bucket[buckets[inside], np.arange(384)[inside]] = 1
    bucket[32, ~inside] = MASKED
    rel = np.zeros((P, P), f32)
    rel[0:32, 0:8] = i["rel_bias_2"]
    rel[32, 0:8] = 1
    w_alpha = np.zeros((P, 256), f32)
    w_alpha[0:16] = i["w_alpha_2"][0]
    return {
        "w_all": w_all, "x_t": i["x"][0].T.reshape(KT, P, T), "mem_t": i["mem_2"][0].T.reshape(KT, P, MEM),
        "vecs": vecs, "consts": consts, "sel_c": sel, "rg_w": rg_w,
        "consts2": np.concatenate([w_alpha, rel, bucket], axis=1),
    }


def kernel(**inputs):
    import concourse.bacc as bacc
    from concourse.bass_utils import run_bass_kernel_spmd

    nc = bacc.Bacc("TRN2", target_bir_lowering=False, num_devices=1)
    arrays = {k: np.ascontiguousarray(v) for k, v in layout({k: np.asarray(v) for k, v in inputs.items()}).items()}
    args = {k: nc.dram_tensor(k, v.shape, F32, kind="ExternalInput").ap() for k, v in arrays.items()}
    row_table = nc.dram_tensor("row_table", (8, 384), F32, kind="Internal").ap()
    out = nc.dram_tensor("out_t", (KT, P, T), F32, kind="ExternalOutput").ap()
    build(nc, row_table=row_table, out=out, **args)
    r = run_bass_kernel_spmd(nc, [arrays], core_ids=[0])
    y = np.asarray(r.results[0]["out_t"])
    return np.ascontiguousarray(y.reshape(D, T).T)[None]
```

```python
from contextlib import ExitStack

import numpy as np

import concourse.bass as bass
from concourse import mybir

F32 = mybir.dt.float32
F32R = mybir.dt.float32r
BF16 = mybir.dt.bfloat16
I32 = mybir.dt.int32
ALU = mybir.AluOpType
ACT = mybir.ActivationFunctionType
AX = mybir.AxisListType.X
ds = bass.ds

P = 128
T = 512
D = 1024
KT = D // P
QT = T // P
MEM = 256
EPS = 1e-6
SLOTS = 4

J_IK = 0
J_IQ = 1
J_K = 5
J_V = 7
J_Q = 9
J_RNN = 17
J_MIX = 33
J_G1 = 49
J_OA = 57
J_OUT = 65
J_FF = 73
J_IN2 = 137
J_OUT2 = 156
J_QC = 164
J_MEM = 172
J_OC = 188
J_FF2 = 196
FF2_GROUPS = (8, 8, 6)
J_END = J_FF2 + 2 * sum(FF2_GROUPS) + 8 * len(FF2_GROUPS)
assert J_END % SLOTS == 0

VEC = {}
NVEC = 0
for _name, _n in (("norm1", 8), ("conv_w", 32), ("conv_b", 8), ("ba", 8), ("bx", 8), ("lam", 8), ("qn", 1),
                  ("kn", 1), ("ikn", 1), ("gate_b", 16), ("norm2", 8), ("mix", 8), ("b_alpha", 2), ("gla", 1),
                  ("sinks", 8), ("cross", 8), ("mem", 8), ("ffn", 8), ("conv_w2", 132), ("conv_b2", 44),
                  ("final", 8)):
    VEC[_name] = NVEC
    NVEC += _n

UNSEEN = -2.0e38
TAKEN = -3.0e38
TOP_K = 128
SEL_ROWS = 32
Y_ATT = 9
MASKED = -1.0e30
GELU_A = 0.7978845608028654
GELU_B = 0.044715


class Steps:

    def __init__(self, eng, sem):
        self.eng, self.sem, self.n, self.more = eng, sem, 0, 0

    def did(self, ins):
        ins.then_inc(self.sem, 1)
        self.n += 1

    def wait(self):
        self.eng.wait_ge(self.sem, self.more + self.n)

    def enter(self, i, per):
        self.more = self.more + i * per
        return self.n

    def leave(self, began, count, per, more):
        assert self.n - began == per, (self.n - began, per)
        self.n, self.more = began + per * count, more


def heads_of_tile(t):
    return (t, 4 + t) if t < 4 else (4 + t, 8 + t)


def build(nc, w_all, x_t, mem_t, vecs, consts, sel_c, rg_w, consts2, row_table, out):
    with ExitStack() as ctx:
        def sb(name, shape, dt=F32):
            return ctx.enter_context(nc.sbuf_tensor(name, shape, dt))

        def sem(name):
            return ctx.enter_context(nc.semaphore(name))

        raw = sb("w_raw", [P, SLOTS, KT * P])
        w_hi = sb("w_hi", [P, SLOTS, KT * P], F32R)
        w_lo = sb("w_lo", [P, SLOTS, KT * P], F32R)
        a_hi = sb("a_hi", [P, KT, T], F32R)
        a_lo = sb("a_lo", [P, KT, T], F32R)
        b_hi = sb("b_hi", [P, KT, T], F32R)
        b_lo = sb("b_lo", [P, KT, T], F32R)
        vec = sb("vec", [P, NVEC])
        cst = sb("cst", [P, 4 * P + 4])
        ident = cst[:, 0:P]
        unseen = cst[:, P:P + 64]
        masked = cst[:, P + 64:2 * P]
        halves = cst[:, 2 * P:2 * P + 2]
        ones2 = cst[:, 2 * P + 2:2 * P + 4]
        flip = cst[:, 2 * P + 4:3 * P + 4]
        in_chunk = cst[:, 3 * P + 4:4 * P + 4]
        identb = sb("identb", [P, P], BF16)
        sel = sb("sel", [SEL_ROWS, 10, P])
        rbuf = sb("rbuf", [P, QT, P])
        small = sb("small", [P, 144])
        sq = sb("sq", [P, 2, T])
        acc = sb("acc", [P, T])
        row = acc
        rstd = sb("rstd", [P, T])
        arena = sb("arena", [P, 38, T])
        x = arena[:, 30:38, :]

        def tiles(i, n=1):
            return arena[:, i:i + n, :]

        def flat(ap):
            return ap.rearrange("p a b -> p (a b)")

        p1 = tiles(0, 17)
        score = tiles(17, 3)
        kz = tiles(20, 4)
        vz = tiles(24, 4).rearrange("p g (t c) -> p g t c", c=P)
        keep = flat(tiles(28, 2)).bitcast(BF16).rearrange("p (t c) -> p t c", c=T)
        ikz = tiles(30, 2)
        rel = tiles(32, 2)
        q_raw = tiles(9, 8)
        y_att = tiles(Y_ATT, 8)
        prob = tiles(30, 4)
        prob_t = tiles(34, 4)
        q_now = tiles(17, 2)
        mix = tiles(0, 8)
        gate = arena[:, 19, :]
        sg1 = tiles(20, 8)
        act_t = tiles(0, 2)
        act_s = tiles(2, 2)
        PAD = 8
        rx = [flat(tiles(32, 2))[:, 0:PAD + T], flat(tiles(34, 2))[:, 0:PAD + T]]
        rg = [arena[:, 0, :], arena[:, 1, :]]
        rc = [arena[:, 2, :], arena[:, 3, :]]
        rr = [arena[:, 4, :], arena[:, 5, :]]
        ri = [arena[:, 6, :], arena[:, 7, :]]
        ra = [arena[:, 36, :], arena[:, 37, :]]
        rt = [arena[:, 8, :], arena[:, 19, :]]
        rgw = tiles(30, 2)[:, :, 0:2 * P]

        in2 = tiles(0, 19)
        in2_tile = [12] + list(range(12)) + list(range(13, 19))
        c2 = flat(tiles(27, 2))
        w_alpha = c2[:, 0:256]
        rel_rows = c2[:, 256:384]
        bucket = c2[:, 384:768]
        g_qd = tiles(19, 4)
        g_ki = tiles(23, 2)
        g_ke = tiles(25, 2).rearrange("p a b -> p (a b)").rearrange("p (t c) -> p t c", c=256)
        g_bc = tiles(27, 2)
        g_e = arena[:, 29, :]
        g_vt = [arena[:, i, :].rearrange("p (t c) -> p t c", c=P) for i in (27, 28, 29, 0)]
        g_st = flat(tiles(4, 4)).rearrange("p (a n c) -> p a n c", a=2, c=P)
        g_at = [arena[:, i, :] for i in (1, 2, 3, 12)]
        g_o = tiles(23, 4)
        s_kz = tiles(2, 2)
        s_vz = tiles(17, 2).rearrange("p g (t c) -> p g t c", c=P)
        s_bias = flat(tiles(4, 4)).rearrange("p (h c) -> p h c", c=256)
        s_toep = flat(tiles(19, 4)).rearrange("p (h c) -> p h c", c=256)
        s_p = [flat(tiles(i, 2)).rearrange("p (n c) -> p n c", c=256) for i in (19, 21)]
        s_pt = [flat(tiles(i, 2)).rearrange("p (n c) -> p n c", c=P) for i in (27, 0)]
        s_y = tiles(13, 4)
        row_sb = arena[:, 29, :]
        c_q = tiles(0, 8)
        c_k = flat(tiles(8, 4)).rearrange("p (k c) -> p k c", c=MEM)
        c_v = flat(tiles(12, 4)).rearrange("p (e c) -> p e c", c=D)
        c_p = [flat(tiles(i, 2)).rearrange("p (n c) -> p n c", c=MEM) for i in (22, 24)]
        c_pt = [tiles(20, 2), tiles(26, 2)]
        c_vt = flat(tiles(16, 4)).rearrange("p (k c) -> p k c", c=MEM)
        memx = flat(tiles(20, 4)).rearrange("p (k c) -> p k c", c=MEM)
        rstd_m = arena[:, 28, 0:MEM]
        f_u = [flat(tiles(i, 2))[:, 0:PAD + T] for i in (0, 2)]
        f_c = [arena[:, 4, :], arena[:, 5, :]]
        f_s = arena[:, 6, :]
        f_h = arena[:, 7, :]
        o_out = tiles(8, 8)

        job_ps = [ctx.enter_context(nc.psum_tensor(f"job{i}", [P, T], F32)) for i in range(2)]
        s_ps = [ctx.enter_context(nc.psum_tensor(f"score{i}", [P, T], F32)) for i in range(3)]
        t_ps = [ctx.enter_context(nc.psum_tensor(f"turn{i}", [P, T], F32)) for i in range(2)]
        o_ps = ctx.enter_context(nc.psum_tensor("o", [P, T], F32))
        rnn_ps = ((s_ps[0], s_ps[1]), (s_ps[2], o_ps))
        sums = o_ps[:, 0:P].rearrange("p (t c) -> p t c", c=32)

        raw_landed = [sem(f"raw_landed{i}") for i in range(SLOTS)]
        x_landed = [sem(f"x_landed{i}") for i in range(4)]
        SEMS = {}

        def s(name):
            if name not in SEMS:
                SEMS[name] = sem(name)
            return SEMS[name]

        def vcol(name, i=0, n=1):
            if isinstance(i, int):
                return vec[:, VEC[name] + i:VEC[name] + i + n]
            return vec[:, ds(i + VEC[name], n)]

        def at(t, i):
            return t[:, i, :] if isinstance(i, int) else flat(t[:, ds(i, 1), :])

        block = ctx.enter_context(nc.Block())

        @block.sync
        def _(sp):
            for sl in range(SLOTS):
                if sl >= 1:
                    sp.wait_ge(x_landed[sl], 16)
                sp.dma_start(raw[:, sl], w_all[sl]).then_inc(raw_landed[sl], 16)
            with sp.Fori(1, J_END // SLOTS) as i:
                for sl in range(SLOTS):
                    sp.wait_ge(s("lo_ready"), i * SLOTS + (sl + 1 - SLOTS))
                    sp.dma_start(raw[:, sl], w_all[ds(i * SLOTS + sl, 1)].rearrange("a p c -> p (a c)")).then_inc(
                        raw_landed[sl], 16)

        @block.gpsimd
        def _(pool):
            nc.gpsimd.memset(rbuf[:], 0.0).then_inc(s("zeroed"), 1)
            with pool.Fori(0, J_END // SLOTS) as i:
                for sl in range(SLOTS):
                    pool.wait_ge(s("hi_ready"), i * SLOTS + (sl + 1))
                    nc.gpsimd.tensor_tensor(w_lo[:, sl], raw[:, sl], w_hi[:, sl].bitcast(F32),
                                            ALU.subtract).then_inc(s("lo_ready"), 1)

        half_lam, neg_half_lam = small[:, 16:24], small[:, 24:32]
        half_ba, half_bx, half_gb = small[:, 32:40], small[:, 40:48], small[:, 48:64]
        iw = small[:, 64:96].rearrange("p (t h) -> p t h", h=8)
        top8 = small[:, 96:120]
        nmax, rsum, rinv = small[:, 120:124], small[:, 124:128], small[:, 128:132]
        g_dec = small[:, 0:16].rearrange("p (a n) -> p a n", n=8)
        g_end = small[:, 16:32].rearrange("p (a n) -> p a n", n=8)
        w_max = [small[:, 32 + 4 * i:36 + 4 * i] for i in range(2)]
        w_sum = [small[:, 40 + 4 * i:44 + 4 * i] for i in range(2)]
        w_snk = [small[:, 48 + 4 * i:52 + 4 * i] for i in range(2)]
        w_inv = [small[:, 56 + 4 * i:60 + 4 * i] for i in range(2)]

        def stat_cols(c):
            return {2: rbuf[:, :, 0:20], 5: rbuf[:, :, 0:8], 7: rbuf[:, 0:2, 0:2]}.get(c, rbuf[:, :, 0:2])

        @block.tensor
        def _(pe):
            mm, tp = nc.tensor.matmul, nc.tensor.transpose

            def block_of(k, kts, hi, lo, n=T, last=7):
                sl, ps = k % SLOTS, job_ps[k % 2]
                for kt in kts:
                    c = slice(kt * P, kt * P + P)
                    mm(ps[:, 0:n], w_hi[:, sl, c], hi[:, kt, 0:n], start=kt == 0, stop=False)
                    mm(ps[:, 0:n], w_hi[:, sl, c], lo[:, kt, 0:n], start=False, stop=False)
                    ins = mm(ps[:, 0:n], w_lo[:, sl, c], hi[:, kt, 0:n], start=False, stop=kt == last)
                return ins

            def open_job(k, m=0):
                pe.wait_ge(s("lo_ready"), 4 * m + (k + 1))
                if not (isinstance(m, int) and k + 4 * m < 2):
                    pe.wait_ge(s("job_taken"), 4 * m + (k - 1))

            def job(k, hi, lo, m=0, n=T, last=7, tiles_ready=None):
                open_job(k, m)
                if tiles_ready is None:
                    block_of(k, range(last + 1), hi, lo, n, last).then_inc(s("job_done"), 1)
                    return
                counts, base = tiles_ready
                for kt in range(last + 1):
                    pe.wait_ge(counts, base + kt + 1)
                    ins = block_of(k, [kt], hi, lo, n, last)
                ins.then_inc(s("job_done"), 1)

            def sum_stat(src, col, rhs):
                for t in range(QT):
                    ins = mm(sums[:, t, col:col + 2], src[:, t * P:t * P + P], rhs, start=True, stop=True)
                return ins

            def turn_stat(c):
                pe.wait_ge(s("st_inv"), c + 1)
                for t in range(QT):
                    ins = tp(s_ps[2][:, t * P:t * P + P], rbuf[:, t, :], ident)
                ins.then_inc(s("st_turn"), 1)

            def spread(t, ps):
                return mm(ps, sel[:, t, :], row[0:SEL_ROWS, :], start=True, stop=True)

            def norm_stat(c, n):
                pe.wait_ge(s("acc_done"), 8 * n + 8)
                sum_stat(acc, 0, ones2).then_inc(s("st_sum"), 1)

            def norm_spread(c, k=None, hi=None, lo=None, n=T):
                if k is not None:
                    open_job(k)
                    block_of(k, range(0, 4), hi, lo, n)
                turn_stat(c)
                if k is not None:
                    block_of(k, range(4, 6), hi, lo, n)
                pe.wait_ge(s("st_row"), c + 1)
                spread(0, t_ps[0][:]).then_inc(s("norm_spread"), 1)
                if k is not None:
                    block_of(k, range(6, 8), hi, lo, n).then_inc(s("job_done"), 1)

            job(J_IK, a_hi, a_lo, tiles_ready=(s("xlo_ready"), 0))
            pe.wait_ge(s("const_landed"), 32)
            norm_stat(0, 0)
            norm_spread(0, J_IQ, a_hi, a_lo)
            job(J_IQ + 1, a_hi, a_lo)
            pe.wait_ge(s("qk_sq"), 1)
            sum_stat(sq[:, 0], 0, halves).then_inc(s("st_sum"), 1)
            job(J_IQ + 2, a_hi, a_lo)
            turn_stat(1)
            for t in range(QT):
                ins = tp(t_ps[1][:, t * P:t * P + P], p1[:, 0, t * P:t * P + P], ident)
            ins.then_inc(s("iw_turned"), 1)
            pe.wait_ge(s("st_row"), 2)
            pe.wait_ge(s("rstd_ready"), 1)
            spread(0, t_ps[0][:]).then_inc(s("qk_spread"), 1)
            job(J_IQ + 3, a_hi, a_lo)
            job(J_K, a_hi, a_lo)
            job(J_K + 1, a_hi, a_lo)
            pe.wait_ge(s("ik_landed"), 16)
            pe.wait_ge(s("job_taken"), 5)
            for n in range(24):
                t, h = 1 + n // 8, n % 8
                if n >= 3:
                    pe.wait_ge(s("idx_relu"), n - 2)
                mm(s_ps[n % 3][:, 0:P * (t + 1)], p1[:, J_IQ + h // 2, t * P:t * P + P],
                   ikz[:, h % 2, 0:P * (t + 1)], start=True, stop=True).then_inc(s("idx_mm"), 1)
            job(J_V, a_hi, a_lo)
            job(J_V + 1, a_hi, a_lo)
            pe.wait_ge(s("qk_sq"), 2)
            sum_stat(sq[:, 1], 0, halves).then_inc(s("qk_sum"), 1)
            with pe.Fori(0, 2) as i:
                for k in range(4):
                    job(J_Q + k, a_hi, a_lo, m=i)
                    pe.wait_ge(s("qk_sq"), 4 * i + (k + 3))
                    for t in range(QT):
                        ins = mm(o_ps[:, ds(i * 8 + (t * 32 + 2 * k + 2), 2)], sq[:, k % 2, t * P:t * P + P],
                                 halves, start=True, stop=True)
                    ins.then_inc(s("qk_sum"), 1)
            turn_v = [t_ps[0], t_ps[1]]
            pe.wait_ge(s("iw_ready"), 1)
            for c in range(2):
                for t in range(QT):
                    ins = tp(turn_v[c][:, t * P:t * P + P], p1[:, J_V + c, t * P:t * P + P], ident)
                ins.then_inc(s("v_turned"), 1)
            job(J_RNN, a_hi, a_lo)
            pe.wait_ge(s("qk_sq"), 11)
            sum_stat(sq[:, 0], 18, halves).then_inc(s("st_sum"), 1)
            job(J_RNN + 1, a_hi, a_lo)
            turn_stat(2)
            pe.wait_ge(s("st_row"), 3)
            pe.wait_ge(s("vz_ready"), 2)
            for n in range(10):
                if n >= 4:
                    pe.wait_ge(s("qk_normed"), n - 3)
                spread(n, (t_ps + s_ps)[n % 4][:]).then_inc(s("qk_spread"), 1)

            def rnn_gates(u, i):
                pe.wait_ge(s("conv_done"), i * 2 + (u + 1))
                pe.wait_ge(s("rgw_landed"), (i + 1) * 16)
                for c in range(2):
                    ins = mm(rnn_ps[u][c][:], rgw[:, u, c * P:c * P + P], rc[u], start=True, stop=True)
                ins.then_inc(s("rnn_mm"), 1)

            def rnn_body(i, ahead):
                job(J_RNN + 2, a_hi, a_lo, m=i)
                job(J_RNN + 3, a_hi, a_lo, m=i)
                rnn_gates(0, i)
                if ahead:
                    job(J_RNN + 4, a_hi, a_lo, m=i)
                    rnn_gates(1, i)
                    job(J_RNN + 5, a_hi, a_lo, m=i)

            with pe.Fori(0, 3) as i:
                rnn_body(i, True)
            rnn_body(3, False)
            rnn_gates(1, 3)

            def head(kvt, i, hh):
                u, half = hh // 2, hh % 2
                n, m0 = kvt * 8 + hh, i * 4
                k, m = J_MIX + n, i
                hi, lo = (a_hi, a_lo) if half == 0 else (b_hi, b_lo)

                def scores(qt, ps):
                    w = P * (qt + 1)
                    mm(ps[:, 0:w], identb[:], keep[:, qt, 0:w], start=True, stop=False)
                    mm(ps[:, 0:w], q_now[:, u, qt * P:qt * P + P], kz[:, 2 * kvt + half, 0:w],
                       start=False, stop=True).then_inc(s("att_mm"), 1)

                if half == 0:
                    pe.wait_ge(s("q_copied"), i * 2 + (kvt * 4 + u + 1))
                scores(3, s_ps[0])
                scores(1, s_ps[1])
                scores(0, s_ps[2])
                if hh == 1:
                    pe.wait_ge(s("rlo_ready"), 8)
                open_job(k, m)
                block_of(k, range(0, 3), hi, lo)
                pe.wait_ge(s("att_exp"), m0 * 4 + (4 * n + 3))
                scores(2, s_ps[2])
                block_of(k, range(3, 6), hi, lo)
                pe.wait_ge(s("att_prob"), m0 * 4 + (4 * n + 1))
                for kt in range(4):
                    ins = tp(t_ps[0][:, kt * P:kt * P + P], prob[:, 3, kt * P:kt * P + P], ident)
                ins.then_inc(s("att_turn"), 1)
                pe.wait_ge(s("att_prob"), m0 * 4 + (4 * n + 3))
                tp(t_ps[1][:, 0:P], prob[:, 0, 0:P], ident)
                for kt in range(2):
                    ins = tp(t_ps[1][:, P + kt * P:2 * P + kt * P], prob[:, 1, kt * P:kt * P + P], ident)
                ins.then_inc(s("att_turn"), 1)
                block_of(k, range(6, 7), hi, lo)
                pe.wait_ge(s("att_prob"), m0 * 4 + (4 * n + 4))
                pe.wait_ge(s("turn_act"), m0 * 2 + (2 * n + 1))
                for kt in range(3):
                    ins = tp(t_ps[0][:, kt * P:kt * P + P], prob[:, 2, kt * P:kt * P + P], ident)
                ins.then_inc(s("att_turn"), 1)
                block_of(k, range(7, 8), hi, lo).then_inc(s("job_done"), 1)
                pe.wait_ge(s("turn_act"), m0 * 2 + (2 * n + 2))
                pe.wait_ge(s("turn_dve"), m0 + (n + 1))
                if half == 0:
                    pe.wait_ge(s("att_out"), i * 2 + (kvt * 4 + u + 1))
                for kt in range(4):
                    ins = mm(o_ps[:, kt * P:T], vz[:, 2 * kvt + half, kt, :], prob_t[:, kt, kt * P:T],
                             start=half == 0 and kt == 0, stop=half == 1 and kt == 3, skip_group_check=True)
                ins.then_inc(s("att_pv"), 1)

            pe.sem_inc(s("att_pv"), 1)
            pe.wait_ge(s("rnn_tanh"), 8)
            pe.wait_ge(s("identb_ready"), 1)
            pe.wait_ge(s("keep_ready"), 1)
            for kvt in range(2):
                with pe.Fori(0, 2) as i:
                    for hh in range(4):
                        head(kvt, i, hh)

            def jobs8(k, hi, lo, m=0, tiles_ready=None, n=T, last=7):
                with pe.Fori(0, 2) as i:
                    for c in range(4):
                        job(k + c, hi, lo, m=i + m, n=n, last=last, tiles_ready=tiles_ready if c == 0 else None)

            jobs8(J_G1, a_hi, a_lo)
            jobs8(J_OA, b_hi, b_lo, tiles_ready=(s("ylo_ready"), 0))
            jobs8(J_OUT, a_hi, a_lo, tiles_ready=(s("mlo_ready"), 0))

            job(J_FF, b_hi, b_lo, tiles_ready=(s("xlo_ready"), 8))
            norm_stat(3, 1)
            norm_spread(3, J_FF + 1, b_hi, b_lo)
            for c in range(2, 8):
                job(J_FF + c, b_hi, b_lo)
            jobs8(J_FF + 8, a_hi, a_lo, tiles_ready=(s("flo_ready"), 0))
            with pe.Fori(1, 4) as g:
                with pe.Fori(0, 2) as i:
                    for c in range(4):
                        job(J_FF + c, b_hi, b_lo, m=g * 4 + i)
                with pe.Fori(0, 2) as i:
                    for c in range(4):
                        job(J_FF + 8 + c, a_hi, a_lo, m=g * 4 + i,
                            tiles_ready=(s("flo_ready"), g * 8) if c == 0 else None)

            def in2_jobs(first, n):
                for k in range(J_IN2 + first, J_IN2 + first + n):
                    job(k, b_hi, b_lo)

            job(J_IN2, b_hi, b_lo, tiles_ready=(s("xlo_ready"), 16))
            norm_stat(4, 2)
            norm_spread(4, J_IN2 + 1, b_hi, b_lo)
            in2_jobs(2, 1)
            pe.wait_ge(s("c2_landed"), 16)
            pe.wait_ge(s("job_taken"), J_IN2 + 1)
            mm(s_ps[2][:, 0:384], rel_rows, bucket, start=True, stop=True).then_inc(s("rel_mm"), 1)
            for c in range(2):
                ins = mm(s_ps[c][:], w_alpha[:, c * P:c * P + P], in2[:, 12, :], start=True, stop=True)
            ins.then_inc(s("gla_z"), 1)
            in2_jobs(3, 7)
            pe.wait_ge(s("job_taken"), J_IN2 + 9)
            for h in range(4):
                if h == 2:
                    in2_jobs(10, 1)
                if h >= 2:
                    pe.wait_ge(s("gvt_ready"), h - 1)
                for t in range(QT):
                    ins = tp(t_ps[h % 2][:, t * P:t * P + P], in2[:, 4 + h, t * P:t * P + P], ident)
                ins.then_inc(s("gv_turned"), 1)
            in2_jobs(11, 1)
            pe.wait_ge(s("gvt_ready"), 4)
            pe.wait_ge(s("gk_end"), 2)
            for c in range(2):
                for t in range(QT):
                    ins = tp(t_ps[c][:, t * P:t * P + P], in2[:, 2 + c, t * P:t * P + P], ident)
                ins.then_inc(s("gk_turned"), 1)

            def gla_products(h):
                for t in range(QT):
                    c = slice(t * P, t * P + P)
                    ins = mm((s_ps + s_ps)[h][:, c], g_ki[:, h // 2, c], g_qd[:, h, c], start=True, stop=True)
                ins.then_inc(s("gla_att"), 1)

            for h in range(3):
                gla_products(h)
            in2_jobs(12, 1)
            pe.wait_ge(s("at_ready"), 1)
            gla_products(3)
            pe.wait_ge(s("get_ready"), 2)
            for n in range(7):
                if n in (2, 4, 6):
                    in2_jobs(12 + n // 2, 1)
                if n >= 2:
                    pe.wait_ge(s("state_taken"), n - 1)
                r = slice(64 * (n % 2), 64 * (n % 2) + 64)
                for h in range(4):
                    ins = mm(t_ps[n % 2][:, h * P:h * P + P], g_ke[r, n // 2, h // 2 * P:h // 2 * P + P],
                             g_vt[h][r, n // 2, :], start=True, stop=True)
                ins.then_inc(s("state_mm"), 1)
            in2_jobs(16, 1)
            pe.wait_ge(s("state_taken"), 7)
            for h in range(4):
                ps = (o_ps, s_ps[1])[h % 2]
                pe.wait_ge(s("at_ready"), h + 1)
                if h == 2:
                    in2_jobs(17, 1)
                if h >= 2:
                    pe.wait_ge(s("go_ready"), h - 1)
                for t in range(QT):
                    c = slice(t * P, t * P + P)
                    mm(ps[:, c], g_vt[h][:, t, :], g_at[h][:, c], start=t == 0, stop=False,
                       skip_group_check=True)
                for n in range(1, 8):
                    ins = mm(ps[:, 64 * n:64 * n + 64], g_st[:, h // 2, n, :], g_qd[:, h, 64 * n:64 * n + 64],
                             start=False, stop=n == 7, skip_group_check=True)
                ins.then_inc(s("go_mm"), 1)
            in2_jobs(18, 1)
            for h in range(4):
                pe.wait_ge(s("go_sq"), h + 1)
                if h == 0:
                    pe.wait_ge(s("go_ready"), 4)
                ins = sum_stat(sq[:, h % 2], 2 * h, ones2)
                ins.then_inc(s("st_sum") if h == 3 else s("go_sum"), 1)
            pe.wait_ge(s("job_taken"), J_OUT2)
            for t in range(QT):
                ins = tp(t_ps[0][:, t * P:t * P + P], in2[:, 18, t * P:t * P + P], ident)
            ins.then_inc(s("sv_turned"), 1)

            def bias_band(c):
                mm(t_ps[(c + 1) % 2][:], flip, s_toep[:, 2 * c:2 * c + 2, :], start=True, stop=True).then_inc(
                    s("bias_mm"), 1)

            def go_spread(h):
                spread(h, job_ps[h % 2][:]).then_inc(s("go_spread"), 1)

            pe.wait_ge(s("toep_landed"), 16)
            bias_band(0)
            turn_stat(5)
            pe.wait_ge(s("swa_values"), 1)
            bias_band(1)
            for c in (2, 3):
                pe.wait_ge(s("bias_ready"), c - 1)
                bias_band(c)
            banks = ((s_ps[0], s_ps[1]), (s_ps[2], o_ps))

            def swa_scores(n):
                t, half = n // 2, n % 2
                if n >= 2:
                    pe.wait_ge(s("swa_s"), n - 1)
                for b in range(QT):
                    k0 = max(b - 1, 0) * P
                    c0 = b % 2 * 256 + (P if b == 0 else 0)
                    ins = mm(banks[n % 2][b // 2][:, c0:b % 2 * 256 + 256], in2[:, 13 + t, b * P:b * P + P],
                             s_kz[:, half, k0:(b + 1) * P], start=True, stop=True)
                ins.then_inc(s("swa_mm"), 1)

            pe.wait_ge(s("swa_keys"), 1)
            swa_scores(0)
            pe.wait_ge(s("st_row"), 6)
            go_spread(0)
            go_spread(1)
            swa_scores(1)
            for h in (2, 3):
                pe.wait_ge(s("go_normed"), h - 1)
                go_spread(h)
            for n in range(8):
                t, half = n // 2, n % 2
                pe.wait_ge(s("swa_prob"), n + 1)
                if n >= 1:
                    pe.wait_ge(s("swa_pt"), 2 * n)
                for c in range(2):
                    for b in (2 * c, 2 * c + 1):
                        for e in range(2):
                            if b == 0 and e == 0:
                                continue
                            ins = tp(t_ps[c][:, (b % 2 * 2 + e) * P:(b % 2 * 2 + e + 1) * P],
                                     s_p[n % 2][:, b, e * P:e * P + P], ident)
                    ins.then_inc(s("swa_turn"), 1)
                if n < 6:
                    swa_scores(n + 2)
                pe.wait_ge(s("swa_pt"), 2 * n + 2)
                if n == 0:
                    pe.wait_ge(s("go_normed"), 4)
                if half == 0 and t >= 2:
                    pe.wait_ge(s("swa_out"), t - 1)
                for b in range(QT):
                    for e in range(2):
                        if b == 0 and e == 0:
                            continue
                        ins = mm(job_ps[t % 2][:, b * P:b * P + P], s_vz[:, half, b - 1 + e, :],
                                 s_pt[n % 2][:, 2 * b + e, :], start=half == 0 and b == 0,
                                 stop=half == 1 and b == 3 and e == 1, skip_group_check=True)
                ins.then_inc(s("swa_pv"), 1)
            pe.wait_ge(s("swa_out"), 4)
            jobs8(J_OUT2, a_hi, a_lo, tiles_ready=(s("y2lo_ready"), 0))
            job(J_QC, b_hi, b_lo, tiles_ready=(s("xlo_ready"), 24))
            norm_stat(6, 3)
            norm_spread(6, J_QC + 1, b_hi, b_lo)
            for c in range(2, 8):
                job(J_QC + c, b_hi, b_lo)

            job(J_MEM, a_hi, a_lo, n=MEM, tiles_ready=(s("memlo_ready"), 0))
            pe.wait_ge(s("memacc_done"), 8)
            for e in range(2):
                ins = mm(sums[:, e, 0:2], acc[:, e * P:e * P + P], ones2, start=True, stop=True)
            ins.then_inc(s("st_sum"), 1)
            norm_spread(7, J_MEM + 1, a_hi, a_lo, MEM)
            job(J_MEM + 2, a_hi, a_lo, n=MEM)
            job(J_MEM + 3, a_hi, a_lo, n=MEM)
            with pe.Fori(0, 3) as i:
                for c in range(4):
                    job(J_MEM + 4 + c, a_hi, a_lo, m=i, n=MEM)
            pe.wait_ge(s("job_taken"), J_OC)
            def cross_scores(c):
                if c >= 2:
                    pe.wait_ge(s("cr_exp"), 4 * (c - 1))
                for q in range(QT):
                    for e in range(2):
                        ins = mm(banks[c % 2][q // 2][:, q % 2 * 256:q % 2 * 256 + 256],
                                 c_q[:, 2 * c + e, q * P:q * P + P], c_k[:, 2 * c + e, :],
                                 start=e == 0, stop=e == 1)
                ins.then_inc(s("cr_mm"), 1)

            cross_scores(0)
            cross_scores(1)
            for c in range(4):
                if c >= 2:
                    pe.wait_ge(s("cv_ready"), c - 1)
                for kk in range(2):
                    for e in range(2):
                        ins = tp(t_ps[c % 2][:, (e * 2 + kk) * P:(e * 2 + kk + 1) * P],
                                 c_vt[:, 2 * c + kk, e * P:e * P + P], ident)
                ins.then_inc(s("cv_turned"), 1)
            pe.wait_ge(s("cv_ready"), 4)
            for c in range(4):
                pe.wait_ge(s("cr_prob"), c + 1)
                if c >= 1:
                    pe.wait_ge(s("cr_pt"), 2 * c)
                for e in range(2):
                    for q in range(QT):
                        ins = tp(t_ps[e][:, q * P:q * P + P], c_p[c % 2][:, q, e * P:e * P + P], ident)
                    ins.then_inc(s("cr_turn"), 1)
                if c < 2:
                    cross_scores(c + 2)
                pe.wait_ge(s("cr_pt"), 2 * c + 2)
                for k in range(2):
                    if c >= 1:
                        pe.wait_ge(s("clo_ready"), 2 * c + k - 1)
                    for e in range(2):
                        ins = mm(job_ps[k][:], c_v[:, e, (2 * c + k) * P:(2 * c + k + 1) * P], c_pt[c % 2][:, e, :],
                                 start=e == 0, stop=e == 1)
                    ins.then_inc(s("cr_pv"), 1)
            pe.wait_ge(s("clo_ready"), 8)
            jobs8(J_OC, a_hi, a_lo)

            k, done = J_FF2, 0
            for gi, g in enumerate(FF2_GROUPS):
                if gi == 0:
                    job(k, b_hi, b_lo, tiles_ready=(s("xlo_ready"), 32))
                    norm_stat(8, 4)
                    norm_spread(8, k + 1, b_hi, b_lo)
                    job(k + 2, b_hi, b_lo)
                    job(k + 3, b_hi, b_lo)
                with pe.Fori(1 if gi == 0 else 0, g // 2) as i:
                    for c in range(4):
                        job(k + c, b_hi, b_lo, m=i)
                k, done = k + 2 * g, done + g
                open_job(k)
                for kt in range(g - 2):
                    pe.wait_ge(s("hlo_ready"), done - g + kt + 1)
                    block_of(k, [kt], a_hi, a_lo, last=g - 1)
                open_job(k + 1)
                block_of(k + 1, range(g - 2), a_hi, a_lo, last=g - 1)
                for kt in (g - 2, g - 1):
                    pe.wait_ge(s("hlo_ready"), done - g + kt + 1)
                    ins = block_of(k, [kt], a_hi, a_lo, last=g - 1)
                ins.then_inc(s("job_done"), 1)
                block_of(k + 1, range(g - 2, g), a_hi, a_lo, last=g - 1).then_inc(s("job_done"), 1)
                for c in range(2, 8):
                    job(k + c, a_hi, a_lo, last=g - 1)
                k += 8
            norm_stat(9, 5)
            norm_spread(9)

        @block.scalar
        def _(act):
            fn = nc.scalar.activation

            def split(k, m=0):
                sl = k % SLOTS
                act.wait_ge(raw_landed[sl], 16 * m + 16 * (k // SLOTS + 1))
                if not (isinstance(m, int) and k + 4 * m < SLOTS):
                    act.wait_ge(s("job_done"), 4 * m + (k - 3))
                fn(w_hi[:, sl], raw[:, sl], ACT.Copy).then_inc(s("hi_ready"), 1)

            def root(c):
                act.wait_ge(s("st_ms"), c + 1)
                fn(stat_cols(c), stat_cols(c), ACT.Sqrt).then_inc(s("st_root"), 1)

            def rows(c):
                act.wait_ge(s("st_turn"), c + 1)
                fn(row[:], s_ps[2][:], ACT.Copy).then_inc(s("st_row"), 1)

            def take_rstd(n, dst=None, w=T):
                act.wait_ge(s("norm_spread"), n)
                fn(rstd[:] if dst is None else dst, t_ps[0][:, 0:w], ACT.Copy).then_inc(s("rstd_ready"), 1)

            def square_tile(n, f, src):
                if 8 * n + f >= 2:
                    act.wait_ge(s("acc_done"), max(8 * n + f - 1, 1))
                fn(sq[:, f % 2, :], src, ACT.Square).then_inc(s("sq_ready"), 1)

            def prep(n, f, name, hi):
                square_tile(n, f, x[:, f, :])
                fn(hi[:, f, :], x[:, f, :], ACT.Copy, scale=vcol(name, f)).then_inc(s("xhi_ready"), 1)

            def load_x():
                for c in range(4):
                    act.dma_start(x[:, 2 * c:2 * c + 2, :],
                                  x_t[2 * c:2 * c + 2].rearrange("k p t -> p k t")).then_inc(x_landed[c], 16)

            act.dma_start(vec[:], vecs).then_inc(s("vec_landed"), 16)
            load_x()
            act.dma_start(cst[:], consts).then_inc(s("const_landed"), 16)
            act.dma_start(sel[:], sel_c).then_inc(s("const_landed"), 16)
            act.wait_ge(s("vec_landed"), 16)
            fn(small[:, 0:8], vcol("lam", 0, 8), ACT.Abs).then_inc(s("lam_step"), 1)
            act.wait_ge(s("lam_step"), 1)
            fn(small[:, 0:8], small[:, 0:8], ACT.Exp, scale=-1.0).then_inc(s("lam_step"), 1)
            act.wait_ge(s("lam_step"), 2)
            fn(small[:, 0:8], small[:, 0:8], ACT.Ln, bias=1.0).then_inc(s("lam_step"), 1)
            for f in range(8):
                act.wait_ge(x_landed[f // 2], 16)
                fn(a_hi[:, f, :], x[:, f, :], ACT.Copy, scale=vcol("norm1", f)).then_inc(s("xhi_ready"), 1)
                if f == 0:
                    split(0)
            for f in range(8):
                if f in (0, 3, 6):
                    split(1 + f // 3)
                square_tile(0, f, x[:, f, :])
            root(0)
            split(4)
            rows(0)
            take_rstd(1)
            split(5)
            act.wait_ge(s("job_taken"), 1)
            act.wait_ge(s("acc_done"), 8)
            fn(sq[:, 0, :], p1[:, 0, :], ACT.Square).then_inc(s("qk_sq"), 1)
            split(6)
            root(1)
            rows(1)
            act.wait_ge(s("iw_turned"), 1)
            fn(iw, t_ps[1][:].rearrange("p (t c) -> p t c", c=P)[:, :, 64:72], ACT.Copy,
               scale=float((64 ** -0.5) * (8 ** -0.5))).then_inc(s("iw_ready"), 1)
            split(7)
            act.wait_ge(s("ik_normed"), 1)
            act.dma_start(ikz[64:128, 1, :], ikz[0:64, 0, :]).then_inc(s("ik_landed"), 16)
            split(8)
            split(9)
            for n in range(24):
                t = 1 + n // 8
                act.wait_ge(s("idx_mm"), n + 1)
                if n >= 2:
                    act.wait_ge(s("idx_acc"), n - 1)
                fn(rel[:, n % 2, 0:P * (t + 1)], s_ps[n % 3][:, 0:P * (t + 1)], ACT.Relu).then_inc(s("idx_relu"), 1)
                if n == 12:
                    act.wait_ge(s("job_taken"), J_K + 1)
                    fn(sq[:, 1, :], p1[:, J_K, :], ACT.Square).then_inc(s("qk_sq"), 1)
            split(10)
            act.wait_ge(s("job_taken"), J_K + 2)
            fn(sq[:, 0, :], p1[:, J_K + 1, :], ACT.Square).then_inc(s("qk_sq"), 1)
            split(11)
            with act.Fori(0, 2) as i:
                for c in range(4):
                    split(J_Q + 3 + c, i)
                    act.wait_ge(s("job_taken"), i * 4 + (J_Q + c + 1))
                    act.wait_ge(s("qk_sum"), i * 4 + (c + 1))
                    fn(sq[:, (c + 1) % 2, :], at(p1, i * 4 + (J_Q + c)), ACT.Square).then_inc(s("qk_sq"), 1)
            act.wait_ge(s("kv_zeroed"), 2)
            for c in range(2):
                act.wait_ge(s("v_turned"), c + 1)
                v4 = t_ps[c][:].rearrange("p (t c) -> p t c", c=P)
                fn(vz[:, 2 * c, :, 0:64], v4[:, :, 0:64], ACT.Copy)
                fn(vz[:, 2 * c + 1, :, 64:128], v4[:, :, 64:128], ACT.Copy).then_inc(s("vz_ready"), 1)
            split(J_RNN + 3)
            root(2)
            split(J_RNN + 4)
            rows(2)

            def conv_head(u, i):
                act.wait_ge(s("job_taken"), i * 4 + (J_RNN + 2 * u + 1))
                f = i * 2 + u
                fn(rc[u], rx[u][:, PAD:PAD + T], ACT.Identity, scale=vcol("conv_w", f + 24),
                   bias=vcol("conv_b", f)).then_inc(s("conv_head"), 1)

            def gelu_square(u, i):
                act.wait_ge(s("job_taken"), i * 4 + (J_RNN + 2 * u + 2))
                fn(sq[:, u, :], rg[u], ACT.Square).then_inc(s("gelu_sq"), 1)

            def rnn_decay(u, i):
                f, n = i * 2 + u, i * 2 + (u + 1)
                act.wait_ge(s("rnn_mm"), n)
                fn(rr[u], rnn_ps[u][0][:], ACT.Tanh, scale=0.5, bias=half_ba_at(f)).then_inc(s("act_step"), 1)
                fn(ri[u], rnn_ps[u][1][:], ACT.Tanh, scale=0.5, bias=half_bx_at(f)).then_inc(s("rnn_tanh"), 1)
                act.wait_ge(s("rnn_tanh"), n)
                fn(ra[u], rr[u], ACT.Exp, scale=half_lam_at(f), bias=half_lam_at(f)).then_inc(s("act_step"), 1)
                fn(rr[u], rr[u], ACT.Tanh, scale=neg_half_lam_at(f), bias=neg_half_lam_at(f)).then_inc(
                    s("rnn_a"), 1)

            def scol(c0, f):
                return small[:, ds(f + c0, 1)]

            def half_lam_at(f):
                return scol(16, f)

            def neg_half_lam_at(f):
                return scol(24, f)

            def half_ba_at(f):
                return scol(32, f)

            def half_bx_at(f):
                return scol(40, f)

            def rnn_pair(i, ahead):
                act.dma_start(rgw, rg_w[ds(i * 2, 2)].rearrange("f p c -> p f c")).then_inc(
                    s("rgw_landed"), 16)
                conv_head(0, i)
                gelu_square(0, i)
                split(J_RNN + 5, i)
                conv_head(1, i)
                split(J_RNN + 6, i)
                gelu_square(1, i)
                rnn_decay(0, i)
                if ahead:
                    split(J_RNN + 7, i)
                rnn_decay(1, i)
                for u in range(2):
                    act.wait_ge(s("gelu_p"), i * 2 + (u + 1))
                    fn(sq[:, u, :], sq[:, u, :], ACT.Tanh).then_inc(s("gelu_tanh"), 1)
                if ahead:
                    split(J_RNN + 8, i)
                for u in range(2):
                    act.wait_ge(s("rnn_m"), i * 2 + (u + 1))
                    fn(rt[u], rt[u], ACT.Sqrt, scale=0.25).then_inc(s("rnn_root"), 1)
                for u in range(2):
                    act.wait_ge(s("rnn_y"), i * 2 + (u + 1))
                    fn(at(b_hi, i * 2 + u), rt[u], ACT.Copy).then_inc(s("rhi_ready"), 1)

            def q_copy(tile):
                for u in range(2):
                    fn(q_now[:, u, :], at(q_raw, tile + u), ACT.Copy).then_inc(s("q_copied"), 1)

            with act.Fori(0, 3) as i:
                rnn_pair(i, True)
            act.wait_ge(s("qk_normed"), 10)
            q_copy(0)
            rnn_pair(3, False)

            act.sem_inc(s("att_out"), 1)

            def two_pairs(kvt, i):
                for hh in range(4):
                    n, half, f = kvt * 8 + hh, hh % 2, i * 2 + (kvt * 4 + hh // 2)
                    split(J_MIX + n + 3, i)
                    for e, qt in enumerate((3, 1, 0, 2)):
                        w = P * (qt + 1)
                        ps = (s_ps[2], s_ps[1], s_ps[2], s_ps[0])[qt]
                        act.wait_ge(s("att_max"), i * 16 + (4 * n + e + 1))
                        fn(prob[:, qt, 0:w], ps[:, 0:w], ACT.Exp, bias=nmax[:, qt:qt + 1],
                           accum_out=rsum[:, qt:qt + 1]).then_inc(s("att_exp"), 1)
                    for e, qt in enumerate((3, 2)):
                        act.wait_ge(s("att_turn"), i * 12 + (3 * n + 2 * e + 1))
                        if e == 0:
                            act.wait_ge(s("att_pv"), i * 4 + (n + 1))
                        fn(prob_t[:, 0:qt + 1, qt * P:qt * P + P],
                           t_ps[0][:, 0:P * (qt + 1)].rearrange("p (k c) -> p k c", c=P),
                           ACT.Copy).then_inc(s("turn_act"), 1)
                    if half == 0:
                        act.wait_ge(s("job_taken"), i * 4 + (J_MIX + n + 1))
                        act.wait_ge(s("params_ready"), 1)
                        fn(gate, gate, ACT.Tanh, scale=0.5, bias=scol(48, f)).then_inc(s("gate_ready"), 1)
                    else:
                        act.wait_ge(s("att_pv"), i * 4 + (n + 2))
                        fn(at(arena, f + Y_ATT), o_ps[:], ACT.Copy).then_inc(s("att_out"), 1)

            with act.Fori(0, 2) as i:
                two_pairs(0, i)
                q_copy(i * 2 + 2)
            two_pairs(1, 0)
            q_copy(6)
            two_pairs(1, 1)

            act.wait_ge(s("att_pv"), 17)
            act.wait_ge(s("att_out"), 9)
            load_x()
            with act.Fori(0, 2) as i:
                for c in range(4):
                    split(J_G1 + 3 + c, i)
                    fn(at(b_hi, i * 4 + c), at(y_att, i * 4 + c), ACT.Copy).then_inc(s("yhi_ready"), 1)
                    act.wait_ge(s("job_taken"), i * 4 + (J_G1 + c + 1))
                    fn(at(sg1, i * 4 + c), at(sg1, i * 4 + c), ACT.Tanh, scale=0.5,
                       bias=scol(56, i * 4 + c)).then_inc(s("sg_ready"), 1)
            with act.Fori(0, 2) as i:
                for c in range(4):
                    split(J_OA + 3 + c, i)
                    act.wait_ge(s("mix_ready"), i * 4 + (c + 1))
                    fn(at(a_hi, i * 4 + c), at(mix, i * 4 + c), ACT.Copy, scale=0.5).then_inc(s("mhi_ready"), 1)
            for f in range(8):
                split(J_OUT + 3 + f)
                act.wait_ge(s("job_taken"), J_OUT + f + 1)
                prep(1, f, "norm2", b_hi)

            def ff_hidden(c, g, i):
                n = g * 8 + i * 4 + (c + 1)
                act.wait_ge(s("job_taken"), g * 16 + i * 4 + (J_FF + c + 1))
                fn(act_s[:, c % 2, :], act_t[:, c % 2, :], ACT.Square).then_inc(s("ff_sq"), 1)
                fn(at(a_hi, i * 4 + c), act_t[:, c % 2, :], ACT.Square).then_inc(s("fhi_ready"), 1)

            split(J_FF + 3)
            root(3)
            split(J_FF + 4)
            rows(3)
            take_rstd(2)
            for c in range(8):
                if c >= 2:
                    split(J_FF + 3 + c)
                ff_hidden(c % 4, 0, c // 4)
            with act.Fori(0, 2) as i:
                for c in range(4):
                    split(J_FF + 11 + c, i)
            with act.Fori(1, 3) as g:
                with act.Fori(0, 2) as i:
                    for c in range(4):
                        split(J_FF + 3 + c, g * 4 + i)
                        ff_hidden(c, g, i)
                with act.Fori(0, 2) as i:
                    for c in range(4):
                        split(J_FF + 11 + c, g * 4 + i)
            with act.Fori(0, 2) as i:
                for c in range(4):
                    split(J_FF + 3 + c, i + 12)
                    ff_hidden(c, 3, i)
            act.dma_start(c2[:, 0:768], consts2).then_inc(s("c2_landed"), 16)
            for f in range(8):
                split(J_FF + 59 + f)
                act.wait_ge(s("job_taken"), J_FF + 57 + f)
                prep(2, f, "mix", b_hi)

            split(J_IN2 + 3)
            root(4)
            split(J_IN2 + 4)
            rows(4)
            take_rstd(3)
            split(J_IN2 + 5)
            split(J_IN2 + 6)
            act.wait_ge(s("rel_mm"), 1)
            fn(row_sb[:, 0:384], s_ps[2][:, 0:384], ACT.Copy).then_inc(s("rel_row"), 1)
            act.wait_ge(s("rel_row"), 1)
            act.dma_start(row_table, row_sb[0:8, 0:384]).then_inc(s("row_stored"), 16)
            split(J_IN2 + 7)
            for c in range(2):
                act.wait_ge(s("z_min"), c + 1)
                fn(sq[:, c, :], s_ps[c][:], ACT.Abs, bias=vcol("b_alpha", c)).then_inc(s("gla_ln"), 1)
            act.wait_ge(s("gla_ln"), 2)
            for c in range(2):
                fn(sq[:, c, :], sq[:, c, :], ACT.Exp, scale=-1.0).then_inc(s("gla_ln"), 1)
            act.wait_ge(s("gla_ln"), 4)
            for c in range(2):
                fn(sq[:, c, :], sq[:, c, :], ACT.Ln, bias=1.0).then_inc(s("gla_ln"), 1)
            split(J_IN2 + 8)
            act.wait_ge(s("row_stored"), 16)
            for c in range(2):
                act.wait_ge(s("bc_ready"), 2)
                if c == 1:
                    act.wait_ge(s("gk_end"), 1)
                else:
                    act.wait_ge(s("g_end_ready"), 1)
                    fn(g_dec, g_end, ACT.Exp, scale=1 / 16).then_inc(s("gla_dec"), 1)
                fn(g_e, g_bc[:, c, :], ACT.Exp, scale=1 / 16).then_inc(s("gla_exp"), 1)
                fn(sq[:, 0, :], g_bc[:, c, :], ACT.Exp, scale=-1 / 16).then_inc(s("gla_exp"), 1)
                act.wait_ge(s("gla_left"), c + 1)
                fn(sq[:, 1, :], sq[:, 1, :], ACT.Exp, scale=1 / 16).then_inc(s("gla_exp"), 1)
                split(J_IN2 + 9 + 2 * c)
                split(J_IN2 + 10 + 2 * c)
            split(J_IN2 + 13)
            act.wait_ge(s("gk_end"), 2)
            for h in range(4):
                if h == 2:
                    split(J_IN2 + 14)
                act.wait_ge(s("gv_turned"), h + 1)
                fn(g_vt[h], t_ps[h % 2][:].rearrange("p (t c) -> p t c", c=P), ACT.Copy).then_inc(
                    s("gvt_ready"), 1)
            split(J_IN2 + 15)
            for c in range(2):
                act.wait_ge(s("gk_turned"), c + 1)
                fn(g_ke[:, :, c * P:c * P + P], t_ps[c][:].rearrange("p (t c) -> p t c", c=P),
                   ACT.Copy).then_inc(s("get_ready"), 1)
            for k in range(16, 20):
                split(J_IN2 + k)
                if k == 17:
                    act.wait_ge(s("job_taken"), J_IN2 + 13)
                    for h in range(4):
                        fn(in2[:, 8 + h, :], in2[:, 8 + h, :], ACT.Silu).then_inc(s("gr_silu"), 1)
            for h in range(4):
                if h == 2:
                    split(J_IN2 + 20)
                act.wait_ge(s("go_mm"), h + 1)
                fn(g_o[:, h, :], (o_ps, s_ps[1])[h % 2][:], ACT.Copy).then_inc(s("go_ready"), 1)
            act.dma_start(s_toep, bass.AP(row_table.tensor, 0, [[1, P], [384, 8], [1, 256]])).then_inc(
                s("toep_landed"), 16)
            for h in range(4):
                act.wait_ge(s("go_ready"), h + 1)
                if h >= 2:
                    act.wait_ge(s("go_sum"), h - 1)
                fn(sq[:, h % 2, :], g_o[:, h, :], ACT.Square).then_inc(s("go_sq"), 1)
                if h == 0:
                    split(J_IN2 + 21)
            root(5)

            def bias_copy(c):
                act.wait_ge(s("bias_mm"), c + 1)
                fn(s_bias[:, 2 * c:2 * c + 2, :], t_ps[(c + 1) % 2][:].rearrange("p (h c) -> p h c", c=256),
                   ACT.Copy).then_inc(s("bias_ready"), 1)

            bias_copy(0)
            act.wait_ge(s("sv_turned"), 1)
            act.wait_ge(s("swa_zero"), 1)
            v4 = t_ps[0][:].rearrange("p (t c) -> p t c", c=P)
            fn(s_vz[:, 0, :, 0:64], v4[:, :, 0:64], ACT.Copy)
            fn(s_vz[:, 1, :, 64:128], v4[:, :, 64:128], ACT.Copy).then_inc(s("swa_values"), 1)
            rows(5)
            for c in range(1, 4):
                bias_copy(c)

            def swa_exp(n):
                t, half = n // 2, n % 2
                head = t + 4 * half
                act.wait_ge(s("swa_max"), n + 1)
                fn(w_snk[half], w_max[half], ACT.Exp, bias=vcol("sinks", head)).then_inc(s("swa_exp"), 1)
                for b in range(QT):
                    fn(s_p[half][:, b, :], s_p[half][:, b, :], ACT.Exp, bias=w_max[half][:, b:b + 1],
                       accum_out=w_sum[half][:, b:b + 1]).then_inc(s("swa_exp"), 1)

            def swa_probabilities(n):
                half = n % 2
                act.wait_ge(s("swa_inv"), n + 1)
                for b in range(QT):
                    ins = fn(s_p[half][:, b, :], s_p[half][:, b, :], ACT.Copy, scale=w_inv[half][:, b:b + 1])
                ins.then_inc(s("swa_prob"), 1)

            swa_exp(0)
            swa_probabilities(0)
            swa_exp(1)
            for n in range(8):
                act.wait_ge(s("swa_turn"), 2 * n + 1)
                if n >= 2:
                    act.wait_ge(s("swa_pv"), n - 1)
                fn(s_pt[n % 2][:, 1:4, :], t_ps[0][:, P:T].rearrange("p (b c) -> p b c", c=P),
                   ACT.Copy).then_inc(s("swa_pt"), 1)
                act.wait_ge(s("swa_turn"), 2 * n + 2)
                fn(s_pt[n % 2][:, 4:8, :], t_ps[1][:].rearrange("p (b c) -> p b c", c=P),
                   ACT.Copy).then_inc(s("swa_pt"), 1)
                if n < 7:
                    swa_probabilities(n + 1)
                if n < 6:
                    swa_exp(n + 2)
                if n % 2 == 1:
                    act.wait_ge(s("swa_pv"), n + 1)
                    fn(s_y[:, n // 2, :], job_ps[n // 2 % 2][:], ACT.Copy).then_inc(s("swa_out"), 1)
            act.wait_ge(s("swa_out"), 4)
            for f in range(8):
                fn(a_hi[:, f, :], g_o[:, f, :] if f < 4 else s_y[:, f - 4, :], ACT.Copy).then_inc(s("y2hi"), 1)
            for f in range(8):
                split(J_OUT2 + 3 + f)
                act.wait_ge(s("job_taken"), J_OUT2 + f + 1)
                prep(3, f, "cross", b_hi)
            act.wait_ge(s("y2lo_ready"), 8)
            act.dma_start(memx, mem_t.rearrange("k p t -> p k t")).then_inc(s("mem_landed"), 16)
            split(J_QC + 3)
            root(6)
            split(J_QC + 4)
            rows(6)
            take_rstd(4)
            act.wait_ge(s("mem_landed"), 16)
            act.wait_ge(s("acc_done"), 32)
            for f in range(8):
                if f < 6:
                    split(J_QC + 5 + f)
                if f >= 2:
                    act.wait_ge(s("memacc_done"), f - 1)
                fn(sq[:, f % 2, 0:MEM], memx[:, f, :], ACT.Square).then_inc(s("memsq"), 1)
                fn(a_hi[:, f, 0:MEM], memx[:, f, :], ACT.Copy, scale=vcol("mem", f)).then_inc(s("memhi"), 1)

            split(J_MEM + 3)
            root(7)
            split(J_MEM + 4)
            rows(7)
            take_rstd(5, rstd_m, MEM)
            split(J_MEM + 5)
            split(J_MEM + 6)
            with act.Fori(0, 3) as i:
                for c in range(4):
                    split(J_MEM + 7 + c, i)
            bank2 = ((s_ps[0], s_ps[1]), (s_ps[2], o_ps))

            def cross_exp(c):
                act.wait_ge(s("cr_max"), c + 1)
                for q in range(QT):
                    fn(c_p[c % 2][:, q, :], bank2[c % 2][q // 2][:, q % 2 * 256:q % 2 * 256 + 256], ACT.Exp,
                       bias=w_max[c % 2][:, q:q + 1], scale=1 / 16,
                       accum_out=w_sum[c % 2][:, q:q + 1]).then_inc(s("cr_exp"), 1)

            def cross_probabilities(c):
                act.wait_ge(s("cr_inv"), c + 1)
                for q in range(QT):
                    ins = fn(c_p[c % 2][:, q, :], c_p[c % 2][:, q, :], ACT.Copy, scale=w_inv[c % 2][:, q:q + 1])
                ins.then_inc(s("cr_prob"), 1)

            cross_exp(0)
            for c in range(4):
                act.wait_ge(s("cv_turned"), c + 1)
                fn(c_v[:, :, 2 * c * P:(2 * c + 2) * P], t_ps[c % 2][:].rearrange("p (e c) -> p e c", c=2 * P),
                   ACT.Copy).then_inc(s("cv_ready"), 1)
            cross_probabilities(0)
            cross_exp(1)
            for c in range(4):
                for e in range(2):
                    act.wait_ge(s("cr_turn"), 2 * c + e + 1)
                    fn(c_pt[c % 2][:, e, :], t_ps[e][:], ACT.Copy).then_inc(s("cr_pt"), 1)
                if c < 3:
                    cross_probabilities(c + 1)
                if c < 2:
                    cross_exp(c + 2)
                for k in range(2):
                    act.wait_ge(s("cr_pv"), 2 * c + k + 1)
                    fn(a_hi[:, 2 * c + k, :], job_ps[k][:], ACT.Copy).then_inc(s("chi_ready"), 1)
            for f in range(8):
                split(J_OC + 3 + f)
                act.wait_ge(s("job_taken"), J_OC + f + 1)
                prep(4, f, "ffn", b_hi)

            def ff2_pair(p, job0, i, f, m):
                for u in range(2):
                    act.wait_ge(s("job_taken"), i * 4 + (job0 + u + 1))
                    col = i * 2 + (22 * u + p)
                    fn(f_c[u], f_u[u][:, PAD:PAD + T], ACT.Identity, scale=vcol("conv_w2", col + 88),
                       bias=vcol("conv_b2", col)).then_inc(s("f_head"), 1)
                act.wait_ge(s("f_conv"), i * 4 + (2 * m + 1))
                fn(f_s, f_c[0], ACT.Silu).then_inc(s("f_silu"), 1)
                act.wait_ge(s("f_prod"), i * 2 + (m + 1))
                fn(at(a_hi, i * 2 + f), f_h, ACT.Copy).then_inc(s("hhi_ready"), 1)

            k, done = J_FF2, 0
            for gi, g in enumerate(FF2_GROUPS):
                if gi == 0:
                    split(k + 3)
                    root(8)
                    split(k + 4)
                    rows(8)
                    take_rstd(6)
                    ff2_pair(0, k, 0, 0, 0)
                    split(k + 5)
                    split(k + 6)
                    ff2_pair(1, k + 2, 0, 1, 1)
                with act.Fori(1 if gi == 0 else 0, g // 2) as i:
                    for pp in range(2):
                        split(k + 2 * pp + 3, i)
                        split(k + 2 * pp + 4, i)
                        ff2_pair(done + pp, k + 2 * pp, i, pp, done + pp)
                k, done = k + 2 * g, done + g
                if gi < len(FF2_GROUPS) - 1:
                    with act.Fori(0, 2) as i:
                        for c in range(4):
                            split(k + 3 + c, i)
                else:
                    for f in range(8):
                        if k + 3 + f < J_END:
                            split(k + 3 + f)
                        act.wait_ge(s("job_taken"), k + f + 1)
                        square_tile(5, f, x[:, f, :])
                k += 8
            root(9)
            rows(9)
            take_rstd(7)
            for f in range(8):
                act.wait_ge(s("out_ready"), f + 1)
                act.dma_start(out[f], o_out[:, f, :]).then_inc(s("out_stored"), 16)
            act.wait_ge(s("out_stored"), 128)

        @block.vector
        def _(dve):
            v = nc.vector
            st = Steps(dve, s("dve_step"))
            did, settle = st.did, st.wait

            def stt(out_, a, sc, b, op0=ALU.mult, op1=ALU.mult):
                return v.scalar_tensor_tensor(out=out_, in0=a, scalar=sc, in1=b, op0=op0, op1=op1)

            def tt(out_, a, b, op):
                return v.tensor_tensor(out_, a, b, op)

            def ts(out_, a, s1, s2=None, op0=ALU.mult, op1=ALU.bypass):
                if s2 is None:
                    return v.tensor_scalar(out_, a, s1, None, op0)
                return v.tensor_scalar(out_, a, s1, s2, op0, op1)

            def done(k, m=0):
                dve.wait_ge(s("job_done"), 4 * m + (k + 1))

            def take(k, dst, m=0, w=T, by=None):
                done(k, m)
                tt(dst, job_ps[k % 2][:, 0:w], rstd[:] if by is None else by, ALU.mult).then_inc(s("job_taken"), 1)

            def inverse(c, parts):
                dve.wait_ge(s("st_sum"), c + 1)
                for n, (dst, src, a, b) in enumerate(parts):
                    ins = ts(dst, src, a, b, ALU.mult, ALU.add)
                    if n < len(parts) - 1:
                        did(ins)
                ins.then_inc(s("st_ms"), 1)
                dve.wait_ge(s("st_root"), c + 1)
                v.reciprocal(stat_cols(c), stat_cols(c)).then_inc(s("st_inv"), 1)

            def norm_inverse(c):
                inverse(c, [(rbuf[:, :, 0:2], sums[:, :, 0:2], 1.0 / D, EPS)])

            def add_square(n, f):
                dve.wait_ge(s("sq_ready"), 8 * n + f + 1)
                if f == 0:
                    v.tensor_copy(acc[:], sq[:, 0, :]).then_inc(s("acc_done"), 1)
                else:
                    dve.wait_ge(s("acc_done"), 8 * n + f)
                    tt(acc[:], acc[:], sq[:, f % 2, :], ALU.add).then_inc(s("acc_done"), 1)

            def prep(n, f, name, hi, lo):
                add_square(n, f)
                lo_part(n, f, name, hi, lo)

            def lo_part(n, f, name, hi, lo):
                dve.wait_ge(s("xhi_ready"), 8 * n + f + 1)
                stt(lo[:, f, :], x[:, f, :], vcol(name, f), hi[:, f, :].bitcast(F32), ALU.mult,
                    ALU.subtract).then_inc(s("xlo_ready"), 1)

            dve.wait_ge(s("vec_landed"), 16)
            for f in range(8):
                dve.wait_ge(x_landed[f // 2], 16)
                lo_part(0, f, "norm1", a_hi, a_lo)
            for f in range(8):
                add_square(0, f)
            dve.wait_ge(s("const_landed"), 32)
            v.tensor_copy(identb[:], ident).then_inc(s("identb_ready"), 1)
            did(ts(small[:, 8:16], vcol("lam", 0, 8), -1.0, 0.0, ALU.mult, ALU.max))
            dve.wait_ge(s("lam_step"), 3)
            settle()
            did(tt(small[:, 8:16], small[:, 8:16], small[:, 0:8], ALU.add))
            settle()
            did(ts(half_lam, small[:, 8:16], -4.0))
            did(ts(neg_half_lam, small[:, 8:16], 4.0))
            did(ts(half_ba, vcol("ba", 0, 8), 0.5))
            did(ts(half_bx, vcol("bx", 0, 8), 0.5))
            ts(half_gb, vcol("gate_b", 0, 16), 0.5).then_inc(s("params_ready"), 1)
            v.memset(kz, 0.0).then_inc(s("kv_zeroed"), 1)
            v.memset(vz, 0.0).then_inc(s("kv_zeroed"), 1)
            did(v.memset(ikz, 0.0))
            dve.wait_ge(s("zeroed"), 1)
            norm_inverse(0)
            dve.wait_ge(s("rstd_ready"), 1)
            take(J_IK, p1[:, 0, :])
            take(J_IQ, p1[:, 1, :])
            take(J_IQ + 1, p1[:, 2, :])
            inverse(1, [(rbuf[:, :, 0:2], sums[:, :, 0:2], 1.0 / 64, EPS)])
            take(J_IQ + 2, p1[:, 3, :])
            dve.wait_ge(s("qk_spread"), 1)
            dve.wait_ge(s("job_taken"), 1)
            settle()
            stt(ikz[0:64, 0, :], p1[0:64, 0, :], vcol("ikn")[0:64], t_ps[0][0:64, :]).then_inc(s("ik_normed"), 1)
            for k in (J_IQ + 3, J_K, J_K + 1):
                take(k, p1[:, k, :])
            dve.wait_ge(s("iw_ready"), 1)
            for n in range(24):
                t, h = 1 + n // 8, n % 8
                w = P * (t + 1)
                dve.wait_ge(s("idx_relu"), n + 1)
                if h == 0:
                    ts(score[:, t - 1, 0:w], rel[:, n % 2, 0:w], iw[:, t, h:h + 1]).then_inc(s("idx_acc"), 1)
                else:
                    dve.wait_ge(s("idx_acc"), n)
                    stt(score[:, t - 1, 0:w], rel[:, n % 2, 0:w], iw[:, t, h:h + 1], score[:, t - 1, 0:w],
                        ALU.mult, ALU.add).then_inc(s("idx_acc"), 1)
            dve.wait_ge(s("idx_acc"), 24)
            for t in (1, 2, 3):
                w = P * (t + 1)
                did(tt(score[:, t - 1, w - 64:w], score[:, t - 1, w - 64:w], unseen, ALU.add))
            for k in (J_V, J_V + 1):
                take(k, p1[:, k, :])
            for c in range(8):
                for _ in range(TOP_K // 8 // 8):
                    settle()
                    for t in range(3):
                        did(v.max(top8[:, 8 * t:8 * t + 8], score[:, t, 0:P * (t + 2)]))
                    settle()
                    for t in range(3):
                        did(v.match_replace(score[:, t, 0:P * (t + 2)], top8[:, 8 * t:8 * t + 8],
                                            score[:, t, 0:P * (t + 2)], TAKEN))
                take(J_Q + c, p1[:, J_Q + c, :])
            settle()
            did(v.memset(keep[:, 0, 0:64], 0.0))
            did(v.tensor_copy(keep[:, 0, 64:P], masked))
            for t in (1, 2, 3):
                w = P * (t + 1)
                ins = ts(keep[:, t, 0:w], score[:, t - 1, 0:w], (UNSEEN + TAKEN) / 2, MASKED, ALU.is_gt, ALU.mult)
                if t < 3:
                    did(ins)
            ins.then_inc(s("keep_ready"), 1)
            inverse(2, [(rbuf[:, :, 0:4], sums[:, :, 0:4], 1.0 / 64, EPS),
                        (rbuf[:, :, 4:20], sums[:, :, 4:20], 1.0, 64 * EPS)])
            dve.wait_ge(s("kv_zeroed"), 2)
            for n in range(10):
                dve.wait_ge(s("qk_spread"), n + 2)
                ps = (t_ps + s_ps)[n % 4]
                if n < 2:
                    did(stt(kz[0:64, 2 * n, :], p1[0:64, J_K + n, :], vcol("kn")[0:64], ps[0:64, :]))
                    stt(kz[64:128, 2 * n + 1, :], p1[64:128, J_K + n, :], vcol("kn")[64:128],
                        ps[64:128, :]).then_inc(s("qk_normed"), 1)
                else:
                    q = p1[:, J_Q + n - 2, :]
                    stt(q, q, vcol("qn"), ps[:]).then_inc(s("qk_normed"), 1)

            def conv_tail(u, i):
                for j in range(3):
                    dve.wait_ge(s("conv_head"), i * 2 + (u + 1)) if j == 0 else settle()
                    ins = stt(rc[u], rx[u][:, PAD - 3 + j:PAD - 3 + j + T], vcol("conv_w", i * 2 + (u + 8 * j)),
                              rc[u], ALU.mult, ALU.add)
                    if j < 2:
                        did(ins)
                ins.then_inc(s("conv_done"), 1)

            def rnn_pair(i, ahead):
                dve.wait_ge(s("job_taken"), i * 4 + (J_RNN + 1))
                conv_tail(0, i)
                take(J_RNN + 2, rx[1][:, PAD:PAD + T], m=i)
                take(J_RNN + 3, rg[1], m=i)
                dve.wait_ge(s("job_taken"), i * 4 + (J_RNN + 4))
                conv_tail(1, i)
                for u in range(2):
                    n = i * 2 + (u + 1)
                    dve.wait_ge(s("gelu_sq"), n)
                    did(ts(sq[:, u, :], sq[:, u, :], GELU_A * GELU_B, GELU_A, ALU.mult, ALU.add))
                    settle()
                    tt(sq[:, u, :], sq[:, u, :], rg[u], ALU.mult).then_inc(s("gelu_p"), 1)
                if ahead:
                    take(J_RNN + 4, rx[0][:, PAD:PAD + T], m=i)
                for u in range(2):
                    n = i * 2 + (u + 1)
                    dve.wait_ge(s("rnn_a"), n)
                    did(tt(rt[u], ra[u], ra[u], ALU.mult))
                    settle()
                    stt(rt[u], rt[u], 1.0, rr[u], ALU.add, ALU.mult).then_inc(s("rnn_m"), 1)
                    dve.wait_ge(s("conv_done"), n)
                    did(stt(ri[u], ri[u], 1.0, rc[u], ALU.add, ALU.mult))
                    dve.wait_ge(s("gelu_tanh"), n)
                    did(stt(sq[:, u, :], sq[:, u, :], 1.0, rg[u], ALU.add, ALU.mult))
                if ahead:
                    take(J_RNN + 5, rg[0], m=i)
                settle()
                for u in range(2):
                    n = i * 2 + (u + 1)
                    dve.wait_ge(s("rnn_root"), n)
                    did(tt(ri[u], ri[u], rt[u], ALU.mult))
                    settle()
                    did(v.tensor_tensor_scan(rr[u], ra[u], ri[u], 0.0, ALU.mult, ALU.add))
                    settle()
                    stt(rt[u], sq[:, u, :], 0.5, rr[u]).then_inc(s("rnn_y"), 1)
                for u in range(2):
                    n = i * 2 + (u + 1)
                    dve.wait_ge(s("rhi_ready"), n)
                    dve.wait_ge(s("rnn_y"), n)
                    tt(at(b_lo, i * 2 + u), rt[u], at(b_hi, i * 2 + u).bitcast(F32), ALU.subtract).then_inc(
                        s("rlo_ready"), 1)

            for u in range(2):
                did(v.memset(rx[u][:, 0:PAD], 0.0))
            settle()
            take(J_RNN, rx[0][:, PAD:PAD + T])
            take(J_RNN + 1, rg[0])
            with dve.Fori(0, 3) as i:
                began = st.enter(i, 16)
                rnn_pair(i, True)
                st.leave(began, 3, 16, 0)
            rnn_pair(3, False)

            dve.wait_ge(s("qk_normed"), 10)
            for kvt in range(2):
                with dve.Fori(0, 2) as i:
                    began = st.enter(i, 20)
                    for hh in range(4):
                        n, half, f = kvt * 8 + hh, hh % 2, i * 2 + (kvt * 4 + hh // 2)
                        order = (3, 1, 0, 2)

                        def row_max(e):
                            qt = order[e]
                            w, ps = P * (qt + 1), (s_ps[2], s_ps[1], s_ps[2], s_ps[0])[qt]
                            dve.wait_ge(s("att_mm"), i * 16 + (4 * n + e + 1))
                            v.tensor_reduce(nmax[:, qt:qt + 1], ps[:, 0:w], AX, ALU.max,
                                            negate=True).then_inc(s("att_max"), 1)

                        def probabilities(e):
                            qt = order[e]
                            w = P * (qt + 1)
                            dve.wait_ge(s("att_exp"), i * 16 + (4 * n + e + 1))
                            did(v.reciprocal(rinv[:, qt:qt + 1], rsum[:, qt:qt + 1]))
                            settle()
                            ts(prob[:, qt, 0:w], prob[:, qt, 0:w], rinv[:, qt:qt + 1]).then_inc(s("att_prob"), 1)

                        row_max(0)
                        row_max(1)
                        row_max(2)
                        probabilities(0)
                        probabilities(1)
                        probabilities(2)
                        row_max(3)
                        probabilities(3)
                        dve.wait_ge(s("att_turn"), i * 12 + (3 * n + 2))
                        dve.wait_ge(s("att_pv"), i * 4 + (n + 1))
                        did(v.tensor_copy(prob_t[:, 0, 0:P], t_ps[1][:, 0:P]))
                        v.tensor_copy(prob_t[:, 0:2, P:2 * P], t_ps[1][:, P:3 * P].rearrange(
                            "p (k c) -> p k c", c=P)).then_inc(s("turn_dve"), 1)
                        if half == 0:
                            take(J_MIX + n, gate, m=i)
                        else:
                            done(J_MIX + n, i)
                            dve.wait_ge(s("gate_ready"), i * 2 + (kvt * 4 + hh // 2 + 1))
                            stt(at(mix, f), gate, 1.0, job_ps[(J_MIX + n) % 2][:], ALU.add,
                                ALU.mult).then_inc(s("job_taken"), 1)
                    st.leave(began, 2, 20, 0)

            with dve.Fori(0, 2) as i:
                for c in range(4):
                    take(J_G1 + c, at(sg1, i * 4 + c), m=i)
                    dve.wait_ge(s("yhi_ready"), i * 4 + (c + 1))
                    tt(at(b_lo, i * 4 + c), at(y_att, i * 4 + c), at(b_hi, i * 4 + c).bitcast(F32),
                       ALU.subtract).then_inc(s("ylo_ready"), 1)
            with dve.Fori(0, 2) as i:
                began = st.enter(i, 0)
                for c in range(4):
                    n = i * 4 + (c + 1)
                    f = i * 4 + c
                    done(J_OA + c, i)
                    dve.wait_ge(s("sg_ready"), n)
                    stt(at(sg1, f), at(sg1, f), 1.0, job_ps[(J_OA + c) % 2][:], ALU.add, ALU.mult).then_inc(
                        s("job_taken"), 1)
                    dve.wait_ge(s("job_taken"), i * 4 + (J_OA + c + 1))
                    tt(at(mix, f), at(mix, f), at(sg1, f), ALU.add).then_inc(s("mix_ready"), 1)
                    dve.wait_ge(s("mhi_ready"), n)
                    stt(at(a_lo, f), at(mix, f), 0.5, at(a_hi, f).bitcast(F32), ALU.mult,
                        ALU.subtract).then_inc(s("mlo_ready"), 1)
                st.leave(began, 2, 0, 0)

            def add_to_x(k, f):
                done(k)
                tt(x[:, f, :], x[:, f, :], job_ps[k % 2][:], ALU.add).then_inc(s("job_taken"), 1)
                dve.wait_ge(s("job_taken"), k + 1)

            for f in range(8):
                dve.wait_ge(x_landed[f // 2], 32)
                add_to_x(J_OUT + f, f)
                prep(1, f, "norm2", b_hi, b_lo)

            def ff_hidden(c, g, i):
                n = g * 8 + i * 4 + (c + 1)
                k, m = J_FF + c, g * 4 + i
                done(k, m)
                if not (isinstance(g, int) and g == 0 and i == 0 and c < 2):
                    dve.wait_ge(s("fhi_ready"), g * 8 + i * 4 + (c - 1))
                stt(act_t[:, c % 2, :], job_ps[k % 2][:], 0.0, rstd[:], ALU.max, ALU.mult).then_inc(
                    s("job_taken"), 1)
                dve.wait_ge(s("fhi_ready"), n)
                tt(at(a_lo, i * 4 + c), act_s[:, c % 2, :], at(a_hi, i * 4 + c).bitcast(F32),
                   ALU.subtract).then_inc(s("flo_ready"), 1)

            def ff_down(c, g, i):
                done(J_FF + 8 + c, g * 4 + i)
                xf = at(x, i * 4 + c)
                tt(xf, xf, job_ps[(J_FF + c) % 2][:], ALU.add).then_inc(s("job_taken"), 1)

            norm_inverse(3)
            dve.wait_ge(s("rstd_ready"), 2)
            for c in range(8):
                ff_hidden(c % 4, 0, c // 4)
            with dve.Fori(0, 2) as i:
                for c in range(4):
                    ff_down(c, 0, i)
            with dve.Fori(1, 3) as g:
                with dve.Fori(0, 2) as i:
                    for c in range(4):
                        ff_hidden(c, g, i)
                with dve.Fori(0, 2) as i:
                    for c in range(4):
                        ff_down(c, g, i)
            with dve.Fori(0, 2) as i:
                for c in range(4):
                    ff_hidden(c, 3, i)
            for f in range(8):
                add_to_x(J_FF + 56 + f, f)
                prep(2, f, "mix", b_hi, b_lo)

            norm_inverse(4)
            dve.wait_ge(s("rstd_ready"), 3)

            def take_in2(first, n=1):
                for k in range(first, first + n):
                    take(J_IN2 + k, in2[:, in2_tile[k], :])

            take_in2(0, 3)
            dve.wait_ge(s("gla_z"), 1)
            dve.wait_ge(s("rel_mm"), 1)
            for c in range(2):
                ts(g_bc[:, c, :], s_ps[c][:], vcol("b_alpha", c), 0.0, ALU.add, ALU.min).then_inc(
                    s("z_min"), 1)
            take_in2(3)
            dve.wait_ge(s("gla_ln"), 6)
            dve.wait_ge(s("z_min"), 2)
            for c in range(2):
                did(tt(sq[:, c, :], g_bc[:, c, :], sq[:, c, :], ALU.subtract))
            settle()
            one = ones2[:, 0:1].to_broadcast([P, 64])
            for c in range(2):
                take_in2(4 + c)
                for n in range(8):
                    r = slice(64 * n, 64 * n + 64)
                    ins = v.tensor_tensor_scan(g_bc[:, c, r], one, sq[:, c, r], 0.0, ALU.mult, ALU.add)
                    if n < 7:
                        did(ins)
                ins.then_inc(s("bc_ready"), 1)
            dve.wait_ge(s("bc_ready"), 2)
            settle()
            v.tensor_copy(g_end, g_bc.rearrange("p a (n c) -> p a n c", c=64)[:, :, :, 63]).then_inc(
                s("g_end_ready"), 1)
            did(v.memset(g_qd, 0.0))
            dve.wait_ge(s("g_end_ready"), 1)
            settle()
            for c in range(2):
                take_in2(6 + c)
                dve.wait_ge(s("gla_exp"), 3 * c + 1) if c == 0 else dve.wait_ge(s("gk_end"), 1)
                bc8 = g_bc[:, c, :].rearrange("p (n c) -> p n c", c=64)
                tt(sq[:, 1, :].rearrange("p (n c) -> p n c", c=64),
                   g_end[:, c, :].unsqueeze(2).to_broadcast([P, 8, 64]), bc8, ALU.subtract).then_inc(
                    s("gla_left"), 1)
                dve.wait_ge(s("gla_exp"), 3 * c + 2)
                did(stt(g_qd[0:64, 2 * c, :], in2[0:64, c, :], 0.125, g_e[0:64, :]))
                did(stt(g_qd[64:128, 2 * c + 1, :], in2[64:128, c, :], 0.125, g_e[64:128, :]))
                tt(g_ki[:, c, :], in2[:, 2 + c, :], sq[:, 0, :], ALU.mult).then_inc(s("g_ki_ready"), 1)
                dve.wait_ge(s("gla_exp"), 3 * c + 3)
                dve.wait_ge(s("g_ki_ready"), c + 1)
                settle()
                tt(in2[:, 2 + c, :], in2[:, 2 + c, :], sq[:, 1, :], ALU.mult).then_inc(s("gk_end"), 1)
            take_in2(8, 4)
            dve.wait_ge(s("gk_turned"), 2)
            for h in range(4):
                did(v.memset(g_at[h], 0.0))
            settle()
            for h in range(4):
                if h == 3:
                    take_in2(12)
                dve.wait_ge(s("gla_att"), h + 1)
                v.copy_predicated(g_at[h].rearrange("p (t c) -> p t c", c=P),
                                  in_chunk.bitcast(I32).unsqueeze(1).to_broadcast([P, QT, P]),
                                  (s_ps + s_ps)[h][:].rearrange("p (t c) -> p t c", c=P)).then_inc(
                    s("at_ready"), 1)
            dve.wait_ge(s("gla_dec"), 1)
            for n in range(7):
                dve.wait_ge(s("state_mm"), n + 1)
                if n >= 1:
                    dve.wait_ge(s("state_taken"), n)
                    settle()
                if n in (2, 4, 6):
                    take_in2(12 + n // 2)
                for h in range(4):
                    r = slice(64 * (h % 2), 64 * (h % 2) + 64)
                    new, add = g_st[r, h // 2, n + 1, :], t_ps[n % 2][r, h * P:h * P + P]
                    if n == 0:
                        ins = v.tensor_copy(new, add)
                    else:
                        ins = stt(new, g_st[r, h // 2, n, :], g_dec[r, h // 2, n:n + 1], add, ALU.mult, ALU.add)
                    if h < 3:
                        did(ins)
                ins.then_inc(s("state_taken"), 1)
            take_in2(16, 3)
            dve.wait_ge(s("go_ready"), 4)
            did(v.memset(s_kz, 0.0))
            settle()
            did(v.tensor_copy(s_kz[0:64, 0, :], in2[0:64, 17, :]))
            v.tensor_copy(s_kz[64:128, 1, :], in2[64:128, 17, :]).then_inc(s("swa_keys"), 1)
            inverse(5, [(rbuf[:, :, 0:8], sums[:, :, 0:8], 1.0 / P, EPS)])
            dve.wait_ge(s("sv_turned"), 1)
            dve.wait_ge(s("swa_keys"), 1)
            v.memset(s_vz, 0.0).then_inc(s("swa_zero"), 1)

            def go_norm(h):
                dve.wait_ge(s("go_spread"), h + 1)
                did(stt(g_o[:, h, :], g_o[:, h, :], vcol("gla"), job_ps[h % 2][:]))
                dve.wait_ge(s("gr_silu"), h + 1)
                settle()
                tt(g_o[:, h, :], g_o[:, h, :], in2[:, 8 + h, :], ALU.mult).then_inc(s("go_normed"), 1)

            dve.wait_ge(s("bias_ready"), 4)
            for u in range(2):
                did(v.memset(s_p[u][:, 0, 0:P], MASKED))
            banks = ((s_ps[0], s_ps[1]), (s_ps[2], o_ps))

            def swa_max(n):
                t, half = n // 2, n % 2
                head, pp, bank = t + 4 * half, s_p[half], banks[half]
                dve.wait_ge(s("swa_mm"), n + 1)
                if n >= 2:
                    dve.wait_ge(s("swa_turn"), 2 * (n - 1))
                    did(v.memset(pp[:, 0, 0:P], MASKED))
                bias = s_bias[:, head, :]
                did(stt(pp[:, 0, P:256], bank[0][:, P:256], 0.125, bias[:, P:256], ALU.mult, ALU.add))
                did(stt(pp[:, 1, :], bank[0][:, 256:512], 0.125, bias, ALU.mult, ALU.add))
                stt(pp[:, 2:4, :], bank[1][:].rearrange("p (b c) -> p b c", c=256), 0.125,
                    bias.unsqueeze(1).to_broadcast([P, 2, 256]), ALU.mult, ALU.add).then_inc(s("swa_s"), 1)
                settle()
                dve.wait_ge(s("swa_s"), n + 1)
                did(v.tensor_reduce(w_max[half], pp, AX, ALU.max))
                settle()
                ts(w_max[half], w_max[half], vcol("sinks", head), -1.0, ALU.max, ALU.mult).then_inc(
                    s("swa_max"), 1)

            def swa_inverse(n):
                half = n % 2
                dve.wait_ge(s("swa_exp"), 5 * n + 5)
                did(tt(w_inv[half], w_sum[half], w_snk[half], ALU.add))
                settle()
                v.reciprocal(w_inv[half], w_inv[half]).then_inc(s("swa_inv"), 1)

            swa_max(0)
            go_norm(0)
            go_norm(1)
            swa_inverse(0)
            swa_max(1)
            go_norm(2)
            go_norm(3)
            for n in range(1, 8):
                swa_inverse(n)
                if n < 7:
                    swa_max(n + 1)
            for f in range(8):
                dve.wait_ge(s("y2hi"), f + 1)
                tt(a_lo[:, f, :], g_o[:, f, :] if f < 4 else s_y[:, f - 4, :], a_hi[:, f, :].bitcast(F32),
                   ALU.subtract).then_inc(s("y2lo_ready"), 1)
            for f in range(8):
                add_to_x(J_OUT2 + f, f)
                prep(3, f, "cross", b_hi, b_lo)
            norm_inverse(6)
            dve.wait_ge(s("rstd_ready"), 4)
            for f in range(8):
                take(J_QC + f, c_q[:, f, :])
                dve.wait_ge(s("memsq"), f + 1)
                if f == 0:
                    v.tensor_copy(acc[:, 0:MEM], sq[:, 0, 0:MEM]).then_inc(s("memacc_done"), 1)
                else:
                    dve.wait_ge(s("memacc_done"), f)
                    tt(acc[:, 0:MEM], acc[:, 0:MEM], sq[:, f % 2, 0:MEM], ALU.add).then_inc(s("memacc_done"), 1)
                dve.wait_ge(s("memhi"), f + 1)
                stt(a_lo[:, f, 0:MEM], memx[:, f, :], vcol("mem", f), a_hi[:, f, 0:MEM].bitcast(F32), ALU.mult,
                    ALU.subtract).then_inc(s("memlo_ready"), 1)

            inverse(7, [(rbuf[:, 0:2, 0:2], sums[:, 0:2, 0:2], 1.0 / D, EPS)])
            dve.wait_ge(s("rstd_ready"), 5)
            for f in range(8):
                take(J_MEM + f, c_k[:, f, :], w=MEM, by=rstd_m)
            for f in range(8):
                take(J_MEM + 8 + f, c_vt[:, f, :], w=MEM, by=rstd_m)

            def cross_max(c):
                dve.wait_ge(s("cr_mm"), c + 1)
                for b in range(2):
                    did(v.tensor_reduce(w_max[c % 2][:, 2 * b:2 * b + 2],
                                        banks[c % 2][b][:].rearrange("p (q c) -> p q c", c=MEM), AX, ALU.max))
                settle()
                ts(w_max[c % 2], w_max[c % 2], -1.0 / 16).then_inc(s("cr_max"), 1)

            def cross_inverse(c):
                dve.wait_ge(s("cr_exp"), 4 * c + 4)
                v.reciprocal(w_inv[c % 2], w_sum[c % 2]).then_inc(s("cr_inv"), 1)

            cross_max(0)
            cross_inverse(0)
            cross_max(1)
            for c in range(4):
                if c < 3:
                    cross_inverse(c + 1)
                if c < 2:
                    cross_max(c + 2)
                for k in range(2):
                    dve.wait_ge(s("chi_ready"), 2 * c + k + 1)
                    tt(a_lo[:, 2 * c + k, :], job_ps[k][:], a_hi[:, 2 * c + k, :].bitcast(F32),
                       ALU.subtract).then_inc(s("clo_ready"), 1)
            for f in range(8):
                add_to_x(J_OC + f, f)
                prep(4, f, "ffn", b_hi, b_lo)

            for u in range(2):
                did(v.memset(f_u[u][:, 0:PAD], 0.0))
            norm_inverse(8)
            dve.wait_ge(s("rstd_ready"), 6)

            def ff2_pair(p, job0, i, f, m):
                for u in range(2):
                    take(job0 + u, f_u[u][:, PAD:PAD + T], m=i)
                    dve.wait_ge(s("job_taken"), i * 4 + (job0 + u + 1))
                    for j in range(2):
                        dve.wait_ge(s("f_head"), i * 4 + (2 * m + u + 1)) if j == 0 else settle()
                        ins = stt(f_c[u], f_u[u][:, PAD - 2 + j:PAD - 2 + j + T],
                                  vcol("conv_w2", i * 2 + (44 * j + 22 * u + p)), f_c[u], ALU.mult, ALU.add)
                        if j == 0:
                            did(ins)
                    ins.then_inc(s("f_conv"), 1)
                dve.wait_ge(s("f_silu"), i * 2 + (m + 1))
                dve.wait_ge(s("f_conv"), i * 4 + (2 * m + 2))
                tt(f_h, f_s, f_c[1], ALU.mult).then_inc(s("f_prod"), 1)
                dve.wait_ge(s("hhi_ready"), i * 2 + (m + 1))
                dve.wait_ge(s("f_prod"), i * 2 + (m + 1))
                tt(at(a_lo, i * 2 + f), f_h, at(a_hi, i * 2 + f).bitcast(F32), ALU.subtract).then_inc(
                    s("hlo_ready"), 1)

            k, before = J_FF2, 0
            for gi, g in enumerate(FF2_GROUPS):
                if gi == 0:
                    ff2_pair(0, k, 0, 0, 0)
                    ff2_pair(1, k + 2, 0, 1, 1)
                first = 1 if gi == 0 else 0
                with dve.Fori(first, g // 2) as i:
                    began = st.enter(i - first if first else i, 4)
                    for pp in range(2):
                        ff2_pair(before + pp, k + 2 * pp, i, pp, before + pp)
                    st.leave(began, g // 2 - first, 4, 0)
                k, before = k + 2 * g, before + g
                if gi < len(FF2_GROUPS) - 1:
                    with dve.Fori(0, 2) as i:
                        for c in range(4):
                            done(k + c, i)
                            xf = at(x, i * 4 + c)
                            tt(xf, xf, job_ps[(k + c) % 2][:], ALU.add).then_inc(s("job_taken"), 1)
                else:
                    for f in range(8):
                        add_to_x(k + f, f)
                        add_square(5, f)
                k += 8
            norm_inverse(9)
            dve.wait_ge(s("rstd_ready"), 7)
            for f in range(8):
                stt(o_out[:, f, :], x[:, f, :], vcol("final", f), rstd[:]).then_inc(s("out_ready"), 1)


def pack(w, cols=None):
    k, c = w.shape
    if c % P:
        w = np.concatenate([w, np.zeros((k, P - c % P), w.dtype)], axis=1)
    return w.reshape(k // P, P, -1, P).transpose(2, 1, 0, 3).reshape(-1, P, k)


def columns(a):
    return a.reshape(-1, P).T


def interleave(a, b):
    return np.stack([a, b], axis=1).reshape((-1,) + a.shape[1:])


def layout(i):
    f32 = np.float32
    w = i["w_in"][0]
    cuts = np.cumsum((1024, 1024, 1024, 256, 256, 512, 64, 8))
    rx, rg, q, k, v, iq, ik, iw, g = np.split(w, cuts, axis=1)
    heads = [h for t in range(8) for h in heads_of_tile(t)]
    q = q.reshape(D, 16, 64)[:, heads].reshape(D, D)
    w_oa = i["w_o_attn"][0].reshape(16, 64, D)[heads].reshape(D, D)
    ff_in = pack(i["w_ff_in"][0])
    ff_out = i["w_ff_out"][0]
    jobs = [pack(np.concatenate([ik, iw], axis=1)), pack(iq), pack(k), pack(v), pack(q),
            interleave(pack(rx), pack(rg)), interleave(pack(g[:, :D]), pack(i["w_o_rnn"][0])), pack(g[:, D:]),
            pack(w_oa), pack(i["w_out"][0])]
    for n in range(4):
        jobs += [ff_in[8 * n:8 * n + 8], pack(ff_out[D * n:D * n + D])]
    w2 = i["w_in_2"][0]
    gq, gk, gv, gr, ga, sq, sk, sv = np.split(w2, np.cumsum((256, 256, 512, 512, 16, 512, 128)), axis=1)
    swa = [t + 4 * half for t in range(4) for half in range(2)]
    sq = sq.reshape(D, 8, 64)[:, swa].reshape(D, 512)
    wo2 = i["w_out_2"][0]
    wo2 = np.concatenate([wo2[:512], wo2[512:].reshape(8, 64, D)[swa].reshape(512, D)], axis=0)
    jobs += [pack(a) for a in (ga, gq, gk, gv, gr, sq, sk, sv, wo2, i["w_q_c_2"][0], i["w_k_c_2"][0],
                               i["w_v_c_2"][0], i["w_o_c_2"][0])]
    up = pack(i["w_up_2"][0])
    down = i["w_down_2"][0]
    n = 0
    for g8 in FF2_GROUPS:
        jobs.append(interleave(up[n:n + g8], up[22 + n:22 + n + g8]))
        rows = down[P * n:P * (n + g8)]
        rows = np.concatenate([rows, np.zeros((D - rows.shape[0], D), f32)], axis=0)
        jobs.append(pack(rows))
        n += g8
    w_all = np.concatenate(jobs, axis=0)
    assert w_all.shape == (J_END, P, D), w_all.shape

    two = lambda a: np.concatenate([a, a])[:, None]
    vecs = [columns(i["norm1_w"][0]), columns(i["conv_w"][0].reshape(-1)), columns(i["conv_b"][0]),
            columns(i["rg_ba"][0]), columns(i["rg_bx"][0]), columns(i["rg_lambda"][0]), two(i["q_norm_w"][0]),
            two(i["k_norm_w"][0]), two(i["idx_k_norm_w"][0]), columns(i["gate_b"][0].reshape(-1)),
            columns(i["norm2_w"][0]), columns(i["norm_mix_2"][0]), columns(i["b_alpha_2"][0]),
            i["gla_gain_2"][0][:, None], np.broadcast_to(i["sinks_2"][0], (P, 8)), columns(i["norm_cross_2"][0]),
            columns(i["norm_mem_2"][0]), columns(i["norm_ffn_2"][0]), columns(i["conv_w_2"][0].reshape(-1)),
            columns(i["conv_b_2"][0]), columns(i["norm_final_2"])]
    vecs = np.concatenate(vecs, axis=1)
    assert vecs.shape == (P, NVEC)

    wa, wx = i["rg_wa"][0], i["rg_wx"][0]
    rg_w = np.zeros((8, P, 2 * P), f32)
    for n in range(16):
        r = slice(64 * (n % 2), 64 * (n % 2) + 64)
        rg_w[n // 2, r, r] = wa[n]
        rg_w[n // 2, r, P + 64 * (n % 2):P + 64 * (n % 2) + 64] = wx[n]

    p, c = np.arange(P)[:, None], np.arange(P)[None, :]
    first = (p < 64) + 0 * np.arange(64)
    consts = np.concatenate([(p == c), first * UNSEEN, first * MASKED, p < 64, p >= 64, np.ones((P, 2)),
                             p + c == P - 1, (p <= c) & (p // 64 == c // 64)], axis=1).astype(f32)
    sel = np.zeros((SEL_ROWS, 10, P), f32)
    for t in range(10):
        sel[2 * t, t, 0:64] = 1
        sel[2 * t + 1, t, 64:128] = 1
    dist = 255 - np.arange(384)
    d = np.maximum(dist, 0)
    large = 16 + (np.log(np.maximum(d, 1).astype(f32) / f32(16)) / f32(np.log(8.0)) * f32(16)).astype(np.int32)
    buckets = np.where(d < 16, d, np.minimum(large, 31))
    inside = (dist >= 0) & (dist < 128)
    bucket = np.zeros((P, 384), f32)
    bucket[buckets[inside], np.arange(384)[inside]] = 1
    bucket[32, ~inside] = MASKED
    rel = np.zeros((P, P), f32)
    rel[0:32, 0:8] = i["rel_bias_2"]
    rel[32, 0:8] = 1
    w_alpha = np.zeros((P, 256), f32)
    w_alpha[0:16] = i["w_alpha_2"][0]
    return {
        "w_all": w_all, "x_t": i["x"][0].T.reshape(KT, P, T), "mem_t": i["mem_2"][0].T.reshape(KT, P, MEM),
        "vecs": vecs, "consts": consts, "sel_c": sel, "rg_w": rg_w,
        "consts2": np.concatenate([w_alpha, rel, bucket], axis=1),
    }


def kernel(**inputs):
    import concourse.bacc as bacc
    from concourse.bass_utils import run_bass_kernel_spmd

    nc = bacc.Bacc("TRN2", target_bir_lowering=False, num_devices=1)
    arrays = {k: np.ascontiguousarray(v) for k, v in layout({k: np.asarray(v) for k, v in inputs.items()}).items()}
    args = {k: nc.dram_tensor(k, v.shape, F32, kind="ExternalInput").ap() for k, v in arrays.items()}
    row_table = nc.dram_tensor("row_table", (8, 384), F32, kind="Internal").ap()
    out = nc.dram_tensor("out_t", (KT, P, T), F32, kind="ExternalOutput").ap()
    build(nc, row_table=row_table, out=out, **args)
    r = run_bass_kernel_spmd(nc, [arrays], core_ids=[0])
    y = np.asarray(r.results[0]["out_t"])
    return np.ascontiguousarray(y.reshape(D, T).T)[None]
```
